# Optimizing a Trainium2 kernel written in Bass

```python
import jax, jax.numpy as jnp
from jax import lax
import numpy as np
import math

D_MODEL = 1024
BATCH = 1
SEQ = 256
DEPTH = 1

GRID_W = 64
CTX_LEN = 256
N_HEADS = 6
QK_NOPE_DIM = 128
QK_ROPE_DIM = 64
V_HEAD_DIM = 128
Q_LORA_RANK = 384
KV_LORA_RANK = 256
MLA_WIDTH = N_HEADS * V_HEAD_DIM
FOURIER_GROUPS = 4
FOURIER_GROUP_DIM = 64
FOURIER_WIDTH = FOURIER_GROUPS * FOURIER_GROUP_DIM
MIX_WIDTH = MLA_WIDTH + FOURIER_WIDTH
IN_PROJ_WIDTH = FOURIER_WIDTH + Q_LORA_RANK + KV_LORA_RANK + QK_ROPE_DIM
ROPE_BASE = 10000.0
Q_BLOCK = 128
N_EXPERTS = 32
TOP_K = 4
D_FF = 1024
SWIGLU_LIMIT = 7.0
SWIGLU_ALPHA = 1.702
EXPERT_BLOCK = 128
RMS_EPS = 1e-6
N_MOD = 6


def rms_norm(x, g):
    xf = x.astype(jnp.float32)
    y = xf * lax.rsqrt(jnp.mean(xf * xf, axis=-1, keepdims=True) + RMS_EPS)
    return (y * g.astype(jnp.float32)).astype(x.dtype)

def modulate(x, g, shift, scale):
    return rms_norm(x, g) * (1 + scale) + shift

def axial_rope_tables(n_tokens):
    rows = n_tokens // GRID_W
    row = jnp.repeat(jnp.arange(rows, dtype=jnp.float32), GRID_W)
    col = jnp.tile(jnp.arange(GRID_W, dtype=jnp.float32), rows)
    half = QK_ROPE_DIM // 2
    inv = 1.0 / (ROPE_BASE ** (jnp.arange(0, half, 2, dtype=jnp.float32) / half))
    ang = jnp.concatenate([row[:, None] * inv, col[:, None] * inv], axis=-1)
    return jnp.cos(ang), jnp.sin(ang)

def rotate(x, cos, sin):
    xf = x.astype(jnp.float32)
    xe, xo = xf[..., 0::2], xf[..., 1::2]
    out = jnp.stack([xe * cos - xo * sin, xe * sin + xo * cos], axis=-1)
    return out.reshape(x.shape).astype(x.dtype)

def mla_project(p, norm_q, norm_kv, w_q_up, w_kv_up, rope):
    B, N, _ = p.shape
    q_lat, kv_lat, k_rope = jnp.split(p, [Q_LORA_RANK, Q_LORA_RANK + KV_LORA_RANK], axis=-1)
    q = (rms_norm(q_lat, norm_q) @ w_q_up).reshape(B, N, N_HEADS, QK_NOPE_DIM + QK_ROPE_DIM)
    kv = (rms_norm(kv_lat, norm_kv) @ w_kv_up).reshape(B, N, N_HEADS, QK_NOPE_DIM + V_HEAD_DIM)
    q_nope, q_rope = jnp.split(q, [QK_NOPE_DIM], axis=-1)
    k_nope, v = jnp.split(kv, [QK_NOPE_DIM], axis=-1)
    if rope is not None:
        cos, sin = rope
        q_rope = rotate(q_rope, cos[:, None, :], sin[:, None, :])
        k_rope = rotate(k_rope, cos, sin)
    k_rope = jnp.broadcast_to(k_rope[:, :, None, :], (B, N, N_HEADS, QK_ROPE_DIM))
    q = jnp.concatenate([q_nope, q_rope], axis=-1)
    k = jnp.concatenate([k_nope, k_rope], axis=-1)
    return q, k, v

def attend(q, k, v):
    B, N, H, Dq = q.shape
    nb = N // Q_BLOCK
    scale = Dq ** -0.5
    qb = jnp.moveaxis(q.reshape(B, nb, Q_BLOCK, H, Dq), 1, 0)

    def one_block(q_blk):
        s = jnp.einsum('bqhd,bkhd->bhqk', q_blk, k, preferred_element_type=jnp.float32) * scale
        pr = jax.nn.softmax(s, axis=-1).astype(v.dtype)
        return jnp.einsum('bhqk,bkhd->bqhd', pr, v)

    o = lax.map(one_block, qb)
    return jnp.moveaxis(o, 0, 1).reshape(B, N, H * V_HEAD_DIM)

def fourier_mix(u, w):
    B, N, _ = u.shape
    ug = u.reshape(B, N, FOURIER_GROUPS, FOURIER_GROUP_DIM).astype(jnp.float32)
    f = jnp.fft.fft2(ug, axes=(1, 3), norm='ortho').real.astype(u.dtype)
    return jnp.einsum('bngc,gcd->bngd', f, w).reshape(B, N, FOURIER_WIDTH)

def moe(h, w_router, b_router, w_gate, b_gate, w_up, b_up, w_down, b_down):
    T, D = h.shape
    logits = jnp.dot(h, w_router, preferred_element_type=jnp.float32) + b_router.astype(jnp.float32)
    top_logit, top_idx = lax.top_k(logits, TOP_K)
    gates = jax.nn.softmax(top_logit, axis=-1)
    n_pairs = T * TOP_K
    flat_e = top_idx.reshape(n_pairs)
    order = jnp.argsort(flat_e)
    sorted_e = flat_e[order]
    pair_tok = order // TOP_K
    pair_gate = gates.reshape(n_pairs)[order].astype(h.dtype)
    counts = jnp.bincount(flat_e, length=N_EXPERTS)
    padded = (counts + EXPERT_BLOCK - 1) // EXPERT_BLOCK * EXPERT_BLOCK
    pad_end = jnp.cumsum(padded)
    pad_start = pad_end - padded
    start = jnp.cumsum(counts) - counts
    dest = pad_start[sorted_e] + jnp.arange(n_pairs) - start[sorted_e]
    n_blocks = -(-n_pairs // EXPERT_BLOCK) + N_EXPERTS
    slot_tok = jnp.zeros((n_blocks * EXPERT_BLOCK,), jnp.int32).at[dest].set(pair_tok.astype(jnp.int32))
    block_e = jnp.minimum(
        jnp.searchsorted(pad_end, jnp.arange(n_blocks) * EXPERT_BLOCK, side='right'), N_EXPERTS - 1)
    xs = h[slot_tok].reshape(n_blocks, EXPERT_BLOCK, D)

    def expert_block(args):
        xb, e = args
        g = jnp.minimum(xb @ w_gate[e] + b_gate[e], SWIGLU_LIMIT)
        u = jnp.clip(xb @ w_up[e] + b_up[e], -SWIGLU_LIMIT, SWIGLU_LIMIT)
        act = g * jax.nn.sigmoid(SWIGLU_ALPHA * g) * (u + 1)
        return act @ w_down[e] + b_down[e]

    ys = lax.map(expert_block, (xs, block_e)).reshape(n_blocks * EXPERT_BLOCK, D)
    y_pairs = ys[dest] * pair_gate[:, None]
    return jnp.zeros_like(h).at[pair_tok].add(y_pairs)

def first_inputs(seed: int = 0) -> dict:
    key = jax.random.key(seed)
    ks = jax.random.split(key, 32)
    f32 = jnp.float32
    L, D = DEPTH, D_MODEL

    def nrm(k, shape, scale):
        return jax.random.normal(k, shape, f32) * scale

    def gain(k, shape):
        return 1.0 + 0.05 * jax.random.normal(k, shape, f32)

    return {
        'x': nrm(ks[0], (BATCH, SEQ, D), 1.0),
        'c': nrm(ks[1], (BATCH, D), 1.0),
        'ctx': nrm(ks[2], (BATCH, CTX_LEN, D), 1.0),
        'c_ctx': nrm(ks[3], (D,), 1.0),
        'w_mod': nrm(ks[4], (L, D, N_MOD * D), 0.5 * D ** -0.5),
        'b_mod': nrm(ks[5], (L, N_MOD * D), 0.01),
        'norm_attn_pre': gain(ks[6], (L, D)),
        'norm_attn_post': gain(ks[7], (L, D)),
        'norm_ffn_pre': gain(ks[8], (L, D)),
        'norm_ffn_post': gain(ks[9], (L, D)),
        'w_in': nrm(ks[10], (L, D, IN_PROJ_WIDTH), D ** -0.5),
        'norm_q_lat': gain(ks[11], (L, Q_LORA_RANK)),
        'norm_kv_lat': gain(ks[12], (L, KV_LORA_RANK)),
        'w_q_up': nrm(ks[13], (L, Q_LORA_RANK, N_HEADS * (QK_NOPE_DIM + QK_ROPE_DIM)), Q_LORA_RANK ** -0.5),
        'w_kv_up': nrm(ks[14], (L, KV_LORA_RANK, N_HEADS * (QK_NOPE_DIM + V_HEAD_DIM)), KV_LORA_RANK ** -0.5),
        'w_fourier': nrm(ks[15], (L, FOURIER_GROUPS, FOURIER_GROUP_DIM, FOURIER_GROUP_DIM), FOURIER_GROUP_DIM ** -0.5),
        'w_out': nrm(ks[16], (L, MIX_WIDTH, D), MIX_WIDTH ** -0.5),
        'w_router': nrm(ks[17], (L, D, N_EXPERTS), D ** -0.5),
        'b_router': nrm(ks[18], (L, N_EXPERTS), 0.01),
        'w_gate': nrm(ks[19], (L, N_EXPERTS, D, D_FF), D ** -0.5),
        'b_gate': nrm(ks[20], (L, N_EXPERTS, D_FF), 0.01),
        'w_up': nrm(ks[21], (L, N_EXPERTS, D, D_FF), D ** -0.5),
        'b_up': nrm(ks[22], (L, N_EXPERTS, D_FF), 0.01),
        'w_down': nrm(ks[23], (L, N_EXPERTS, D_FF, D), D_FF ** -0.5),
        'b_down': nrm(ks[24], (L, N_EXPERTS, D), 0.01),
    }

def first_block(x, c, ctx, c_ctx, w_mod, b_mod, norm_attn_pre, norm_attn_post, norm_ffn_pre,
              norm_ffn_post, w_in, norm_q_lat, norm_kv_lat, w_q_up, w_kv_up, w_fourier, w_out,
              w_router, b_router, w_gate, b_gate, w_up, b_up, w_down, b_down):
    B, N, D = x.shape
    rope = axial_rope_tables(N)
    for l in range(DEPTH):
        last = l == DEPTH - 1
        m = jax.nn.silu(c) @ w_mod[l] + b_mod[l]
        sh1, sc1, g1, sh2, sc2, g2 = jnp.split(m[:, None, :], N_MOD, axis=-1)
        mc = jax.nn.silu(c_ctx) @ w_mod[l] + b_mod[l]
        csh1, csc1, cg1, csh2, csc2, cg2 = jnp.split(mc, N_MOD, axis=-1)

        hx = modulate(x, norm_attn_pre[l], sh1, sc1)
        hc = modulate(ctx, norm_attn_pre[l], csh1, csc1)
        px = hx @ w_in[l]
        pc = hc @ w_in[l]
        qx, kx, vx = mla_project(px[..., FOURIER_WIDTH:], norm_q_lat[l], norm_kv_lat[l],
                                 w_q_up[l], w_kv_up[l], rope)
        qc, kc, vc = mla_project(pc[..., FOURIER_WIDTH:], norm_q_lat[l], norm_kv_lat[l],
                                 w_q_up[l], w_kv_up[l], None)
        k_all = jnp.concatenate([kx, kc], axis=1)
        v_all = jnp.concatenate([vx, vc], axis=1)
        att_x = attend(qx, k_all, v_all)
        four_x = fourier_mix(px[..., :FOURIER_WIDTH], w_fourier[l])
        mix_x = jnp.concatenate([att_x, four_x], axis=-1) @ w_out[l]
        x = x + g1 * rms_norm(mix_x, norm_attn_post[l])
        if not last:
            att_c = attend(qc, kc, vc)
            four_c = fourier_mix(pc[..., :FOURIER_WIDTH], w_fourier[l])
            mix_c = jnp.concatenate([att_c, four_c], axis=-1) @ w_out[l]
            ctx = ctx + cg1 * rms_norm(mix_c, norm_attn_post[l])

        hx2 = modulate(x, norm_ffn_pre[l], sh2, sc2)
        yx = moe(hx2.reshape(B * N, D), w_router[l], b_router[l], w_gate[l], b_gate[l],
                 w_up[l], b_up[l], w_down[l], b_down[l]).reshape(B, N, D)
        x = x + g2 * rms_norm(yx, norm_ffn_post[l])
        if not last:
            hc2 = modulate(ctx, norm_ffn_pre[l], csh2, csc2)
            yc = moe(hc2.reshape(-1, D), w_router[l], b_router[l], w_gate[l], b_gate[l],
                     w_up[l], b_up[l], w_down[l], b_down[l]).reshape(ctx.shape)
            ctx = ctx + cg2 * rms_norm(yc, norm_ffn_post[l])
    return x


DEPTH_2 = 2

HEAD_DIM = 64
MOBA_HEADS = D_MODEL // (2 * HEAD_DIM)
MOBA_BLOCK = 256
MOBA_TOPK = 3
NSA_HEADS = D_MODEL // (2 * HEAD_DIM)
NSA_KV_GROUPS = 2
NSA_HEADS_PER_GROUP = NSA_HEADS // NSA_KV_GROUPS
NSA_CMP_BLOCK = 32
NSA_CMP_STRIDE = 16
NSA_CMP_HIDDEN = 256
NSA_SLC_BLOCK = 64
NSA_TOPN = 16
NSA_WINDOW = 512
NSA_FORCE_SCORE = 1e6
FOX_HEADS = D_MODEL // HEAD_DIM
D_FF_2 = 4 * D_MODEL
REL_BUCKETS = 32
REL_MAX_DISTANCE = 1024
QUERY_BLOCK = 128
SEQ_ALIGN = MOBA_BLOCK
RMS_EPS_2 = 1e-5
NEG_INF = -1e30

MOBA_W = MOBA_HEADS * HEAD_DIM
NSA_W = NSA_HEADS * HEAD_DIM
NSA_KV_W = NSA_KV_GROUPS * HEAD_DIM
EVEN_SPLITS = (MOBA_W, MOBA_W, MOBA_W, NSA_W) + (NSA_KV_W,) * 6 + (3 * NSA_HEADS,)
EVEN_IN = sum(EVEN_SPLITS)
FOX_W = FOX_HEADS * HEAD_DIM
ODD_SPLITS = (FOX_W, FOX_W, FOX_W, FOX_HEADS)
ODD_IN = sum(ODD_SPLITS)
N_BIAS_HEADS = MOBA_HEADS + NSA_HEADS


def _split(t, sizes):
    offs = [int(o) for o in np.cumsum(sizes)[:-1]]
    return jnp.split(t, offs, axis=-1)

def rmsnorm(x, g):
    xf = x.astype(jnp.float32)
    y = xf * lax.rsqrt(jnp.mean(xf * xf, axis=-1, keepdims=True) + RMS_EPS_2)
    return (y * g.astype(jnp.float32)).astype(x.dtype)

def masked_softmax(logits, mask):
    logits = jnp.where(mask, logits.astype(jnp.float32), NEG_INF)
    p = jax.nn.softmax(logits, axis=-1)
    return p * jnp.any(mask, axis=-1, keepdims=True)

def rel_bucket(dist):
    n = jnp.maximum(dist, 0)
    max_exact = REL_BUCKETS // 2
    nf = jnp.maximum(n, 1).astype(jnp.float32)
    large = max_exact + (jnp.log(nf / max_exact) / math.log(REL_MAX_DISTANCE / max_exact)
                         * (REL_BUCKETS - max_exact)).astype(jnp.int32)
    large = jnp.minimum(large, REL_BUCKETS - 1)
    return jnp.where(n < max_exact, n, large)

def moba_nsa_mixer(h, w_in, w_out, rel_bias, cmp_pos_k, cmp_pos_v,
                   cmp_k_w1, cmp_k_w2, cmp_v_w1, cmp_v_w2):
    B, S, _ = h.shape
    S_pad = -(-S // SEQ_ALIGN) * SEQ_ALIGN
    hp = jnp.pad(h, ((0, 0), (0, S_pad - S), (0, 0)))
    mq, mk, mv, nq, kc, vc, ksl, vsl, kwn, vwn, gz = _split(hp @ w_in, EVEN_SPLITS)
    scale = HEAD_DIM ** -0.5
    Q = QUERY_BLOCK
    G, J = NSA_KV_GROUPS, NSA_HEADS_PER_GROUP
    n_qc = S_pad // Q
    f32 = jnp.float32

    n_mb = S_pad // MOBA_BLOCK
    k_moba = min(MOBA_TOPK, n_mb)
    mq = mq.reshape(B, S_pad, MOBA_HEADS, HEAD_DIM).transpose(0, 2, 1, 3)
    mk = mk.reshape(B, n_mb, MOBA_BLOCK, MOBA_HEADS, HEAD_DIM).transpose(0, 3, 1, 2, 4)
    mv = mv.reshape(B, n_mb, MOBA_BLOCK, MOBA_HEADS, HEAD_DIM).transpose(0, 3, 1, 2, 4)
    k_mean = jnp.mean(mk, axis=3)

    nq = nq.reshape(B, S_pad, NSA_HEADS, HEAD_DIM).transpose(0, 2, 1, 3)
    n_cmp = (S_pad - NSA_CMP_BLOCK) // NSA_CMP_STRIDE + 1
    cmp_idx = np.arange(n_cmp)[:, None] * NSA_CMP_STRIDE + np.arange(NSA_CMP_BLOCK)[None, :]
    cmp_end = jnp.asarray(cmp_idx[:, -1])

    def compress(raw, pos, w1, w2):
        blocks = raw.reshape(B, S_pad, G, HEAD_DIM)[:, cmp_idx] + pos[:, None, :]
        blocks = blocks.transpose(0, 3, 1, 2, 4).reshape(B, G, n_cmp, NSA_CMP_BLOCK * HEAD_DIM)
        return jax.nn.silu(blocks @ w1) @ w2

    k_cmp = compress(kc, cmp_pos_k, cmp_k_w1, cmp_k_w2)
    v_cmp = compress(vc, cmp_pos_v, cmp_v_w1, cmp_v_w2)
    n_sb = S_pad // NSA_SLC_BLOCK
    n_sel = min(NSA_TOPN, n_sb)
    k_slc = ksl.reshape(B, n_sb, NSA_SLC_BLOCK, G, HEAD_DIM).transpose(0, 3, 1, 2, 4)
    v_slc = vsl.reshape(B, n_sb, NSA_SLC_BLOCK, G, HEAD_DIM).transpose(0, 3, 1, 2, 4)
    pad_w = ((0, 0), (0, 0), (NSA_WINDOW, 0), (0, 0))
    k_win = jnp.pad(kwn.reshape(B, S_pad, G, HEAD_DIM).transpose(0, 2, 1, 3), pad_w)
    v_win = jnp.pad(vwn.reshape(B, S_pad, G, HEAD_DIM).transpose(0, 2, 1, 3), pad_w)
    gates = jax.nn.sigmoid(gz.reshape(B, S_pad, NSA_HEADS, 3).transpose(0, 2, 1, 3))
    ci = np.arange(n_cmp)[:, None] * NSA_CMP_STRIDE
    sj = np.arange(n_sb)[None, :] * NSA_SLC_BLOCK
    overlap = jnp.asarray(((ci < sj + NSA_SLC_BLOCK) & (ci + NSA_CMP_BLOCK > sj)).astype(np.float32))

    table = rel_bias.T
    tb_moba = table[:MOBA_HEADS]
    tb_nsa = table[MOBA_HEADS:].reshape(G, J, REL_BUCKETS)
    h_m = jnp.arange(MOBA_HEADS)[:, None, None]
    g_i = jnp.arange(G)[:, None, None]
    g5 = jnp.arange(G)[:, None, None, None, None]
    j5 = jnp.arange(J)[None, :, None, None, None]

    def query_block(bc):
        b, c = bc
        q0 = c * Q
        t = q0 + jnp.arange(Q)
        qm = lax.dynamic_slice_in_dim(mq[b], q0, Q, axis=1)
        mk_b, mv_b = mk[b], mv[b]
        blk = q0 // MOBA_BLOCK
        route = jnp.einsum('hqd,hnd->hqn', qm, k_mean[b]).astype(f32)
        route = jnp.where(jnp.arange(n_mb) < blk, route, NEG_INF)
        _, sel = lax.top_k(route, k_moba)
        sel_ok = sel < blk
        k_sel = mk_b[h_m, sel]
        v_sel = mv_b[h_m, sel]
        k_own = lax.dynamic_index_in_dim(mk_b, blk, axis=1, keepdims=False)
        v_own = lax.dynamic_index_in_dim(mv_b, blk, axis=1, keepdims=False)
        d_sel = t[:, None, None] - (sel[..., None] * MOBA_BLOCK + jnp.arange(MOBA_BLOCK))
        d_own = t[:, None] - (blk * MOBA_BLOCK + jnp.arange(MOBA_BLOCK))[None, :]
        s_sel = (jnp.einsum('hqd,hqnkd->hqnk', qm, k_sel).astype(f32) * scale
                 + tb_moba[h_m[..., None], rel_bucket(d_sel)])
        s_own = (jnp.einsum('hqd,hkd->hqk', qm, k_own).astype(f32) * scale
                 + tb_moba[:, rel_bucket(d_own)])
        n_k = k_moba * MOBA_BLOCK
        m_sel = jnp.broadcast_to(sel_ok[..., None], d_sel.shape).reshape(MOBA_HEADS, Q, n_k)
        m_own = jnp.broadcast_to((d_own >= 0)[None], s_own.shape)
        p = masked_softmax(jnp.concatenate([s_sel.reshape(MOBA_HEADS, Q, n_k), s_own], axis=-1),
                           jnp.concatenate([m_sel, m_own], axis=-1))
        o_a = (jnp.einsum('hqnk,hqnkd->hqd', p[..., :n_k].reshape(MOBA_HEADS, Q, k_moba, MOBA_BLOCK), v_sel)
               + jnp.einsum('hqk,hkd->hqd', p[..., n_k:], v_own))
        qn = lax.dynamic_slice_in_dim(nq[b], q0, Q, axis=1).reshape(G, J, Q, HEAD_DIM)
        d_cmp = t[:, None] - cmp_end[None, :]
        s_cmp = (jnp.einsum('gjqd,gnd->gjqn', qn, k_cmp[b]).astype(f32) * scale
                 + tb_nsa[:, :, rel_bucket(d_cmp)])
        p_cmp = masked_softmax(s_cmp, (d_cmp >= 0)[None, None])
        o_cmp = jnp.einsum('gjqn,gnd->gjqd', p_cmp, v_cmp[b])
        imp = jnp.einsum('gjqn,nm->gqm', p_cmp, overlap)
        s_blk = t // NSA_SLC_BLOCK
        jb = jnp.arange(n_sb)[None, :]
        forced = (jb == 0) | (jb == s_blk[:, None]) | (jb == s_blk[:, None] - 1)
        imp = jnp.where(forced, imp + NSA_FORCE_SCORE, jnp.where(jb <= s_blk[:, None], imp, NEG_INF))
        _, sidx = lax.top_k(imp, n_sel)
        k_s = k_slc[b][g_i, sidx]
        v_s = v_slc[b][g_i, sidx]
        d_s = t[:, None, None] - (sidx[..., None] * NSA_SLC_BLOCK + jnp.arange(NSA_SLC_BLOCK))
        m_s = (d_s >= 0) & (sidx <= s_blk[:, None])[..., None]
        s_s = (jnp.einsum('gjqd,gqnkd->gjqnk', qn, k_s).astype(f32) * scale
               + tb_nsa[g5, j5, rel_bucket(d_s)[:, None]])
        n_ks = n_sel * NSA_SLC_BLOCK
        p_s = masked_softmax(s_s.reshape(G, J, Q, n_ks), m_s.reshape(G, 1, Q, n_ks))
        o_slc = jnp.einsum('gjqnk,gqnkd->gjqd', p_s.reshape(G, J, Q, n_sel, NSA_SLC_BLOCK), v_s)
        k_w = lax.dynamic_slice_in_dim(k_win[b], q0, Q + NSA_WINDOW, axis=1)
        v_w = lax.dynamic_slice_in_dim(v_win[b], q0, Q + NSA_WINDOW, axis=1)
        pos_w = q0 - NSA_WINDOW + jnp.arange(Q + NSA_WINDOW)
        d_w = t[:, None] - pos_w[None, :]
        m_w = (d_w >= 0) & (d_w < NSA_WINDOW) & (pos_w >= 0)[None, :]
        s_w = (jnp.einsum('gjqd,gkd->gjqk', qn, k_w).astype(f32) * scale
               + tb_nsa[:, :, rel_bucket(d_w)])
        p_w = masked_softmax(s_w, m_w[None, None])
        o_win = jnp.einsum('gjqk,gkd->gjqd', p_w, v_w)
        g = lax.dynamic_slice_in_dim(gates[b], q0, Q, axis=1).astype(f32)
        o_b = (g[..., 0:1] * o_cmp.reshape(NSA_HEADS, Q, HEAD_DIM)
               + g[..., 1:2] * o_slc.reshape(NSA_HEADS, Q, HEAD_DIM)
               + g[..., 2:3] * o_win.reshape(NSA_HEADS, Q, HEAD_DIM))
        return jnp.concatenate([o_a.astype(f32), o_b.astype(f32)], axis=0)

    b_idx = jnp.repeat(jnp.arange(B), n_qc)
    c_idx = jnp.tile(jnp.arange(n_qc), B)
    o = lax.map(query_block, (b_idx, c_idx))
    o = o.reshape(B, n_qc, MOBA_HEADS + NSA_HEADS, Q, HEAD_DIM).transpose(0, 1, 3, 2, 4)
    o = o.reshape(B, S_pad, MOBA_W + NSA_W)[:, :S]
    return o.astype(h.dtype) @ w_out

def fox_mixer(h, w_in, b_forget, w_out):
    B, S, _ = h.shape
    Q = QUERY_BLOCK
    scale = HEAD_DIM ** -0.5
    q, k, v, fz = _split(h @ w_in, ODD_SPLITS)
    q = q.reshape(B, S, FOX_HEADS, HEAD_DIM).transpose(0, 2, 1, 3)
    k = k.reshape(B, S, FOX_HEADS, HEAD_DIM).transpose(0, 2, 1, 3)
    v = v.reshape(B, S, FOX_HEADS, HEAD_DIM).transpose(0, 2, 1, 3)
    log_f = jax.nn.log_sigmoid((fz + b_forget).astype(jnp.float32))
    cum = jnp.cumsum(log_f, axis=1).transpose(0, 2, 1)
    key_pos = jnp.arange(S)

    def block(c):
        q0 = c * Q
        qc = lax.dynamic_slice_in_dim(q, q0, Q, axis=2)
        cq = lax.dynamic_slice_in_dim(cum, q0, Q, axis=2)
        t = q0 + jnp.arange(Q)
        s = (jnp.einsum('bhqd,bhkd->bhqk', qc, k).astype(jnp.float32) * scale
             + cq[..., None] - cum[:, :, None, :])
        p = masked_softmax(s, key_pos[None, :] <= t[:, None])
        return jnp.einsum('bhqk,bhkd->bhqd', p, v).astype(jnp.float32)

    o = lax.map(block, jnp.arange(S // Q))
    o = o.transpose(1, 0, 3, 2, 4).reshape(B, S, FOX_W)
    return o.astype(h.dtype) @ w_out

def sqrelu_mlp(h, w1, w2):
    a = jax.nn.relu(h @ w1)
    return (a * a) @ w2

def second_inputs(seed: int = 0) -> dict:
    key = jax.random.key(seed)
    ks = jax.random.split(key, 20)
    f32 = jnp.float32

    def nrm(k, shape, scale):
        return jax.random.normal(k, shape, f32) * scale

    n_even = (DEPTH_2 + 1) // 2
    n_odd = DEPTH_2 // 2
    cmp_in = NSA_CMP_BLOCK * HEAD_DIM
    return {
        'x': nrm(ks[0], (BATCH, SEQ, D_MODEL), 1.0),
        'rel_bias': nrm(ks[1], (REL_BUCKETS, N_BIAS_HEADS), 0.5),
        'mix_norm': 1.0 + nrm(ks[2], (DEPTH_2, D_MODEL), 0.02),
        'mlp_norm': 1.0 + nrm(ks[3], (DEPTH_2, D_MODEL), 0.02),
        'even_w_in': nrm(ks[4], (n_even, D_MODEL, EVEN_IN), D_MODEL ** -0.5),
        'even_w_out': nrm(ks[5], (n_even, MOBA_W + NSA_W, D_MODEL), (MOBA_W + NSA_W) ** -0.5),
        'cmp_pos_k': nrm(ks[6], (n_even, NSA_CMP_BLOCK, HEAD_DIM), 0.2),
        'cmp_pos_v': nrm(ks[7], (n_even, NSA_CMP_BLOCK, HEAD_DIM), 0.2),
        'cmp_k_w1': nrm(ks[8], (n_even, cmp_in, NSA_CMP_HIDDEN), cmp_in ** -0.5),
        'cmp_k_w2': nrm(ks[9], (n_even, NSA_CMP_HIDDEN, HEAD_DIM), NSA_CMP_HIDDEN ** -0.5),
        'cmp_v_w1': nrm(ks[10], (n_even, cmp_in, NSA_CMP_HIDDEN), cmp_in ** -0.5),
        'cmp_v_w2': nrm(ks[11], (n_even, NSA_CMP_HIDDEN, HEAD_DIM), NSA_CMP_HIDDEN ** -0.5),
        'odd_w_in': nrm(ks[12], (n_odd, D_MODEL, ODD_IN), D_MODEL ** -0.5),
        'odd_b_forget': 3.0 + nrm(ks[13], (n_odd, FOX_HEADS), 0.5),
        'odd_w_out': nrm(ks[14], (n_odd, FOX_W, D_MODEL), FOX_W ** -0.5),
        'mlp_w1': nrm(ks[15], (DEPTH_2, D_MODEL, D_FF_2), D_MODEL ** -0.5),
        'mlp_w2': nrm(ks[16], (DEPTH_2, D_FF_2, D_MODEL), D_FF_2 ** -0.5),
        'final_norm': 1.0 + nrm(ks[17], (D_MODEL,), 0.02),
    }

def second_block(x, rel_bias, mix_norm, mlp_norm, even_w_in, even_w_out, cmp_pos_k, cmp_pos_v,
              cmp_k_w1, cmp_k_w2, cmp_v_w1, cmp_v_w2, odd_w_in, odd_b_forget, odd_w_out,
              mlp_w1, mlp_w2, final_norm):
    h = x
    for layer in range(DEPTH_2):
        hn = rmsnorm(h, mix_norm[layer])
        i = layer // 2
        if layer % 2 == 0:
            h = h + moba_nsa_mixer(hn, even_w_in[i], even_w_out[i], rel_bias,
                                   cmp_pos_k[i], cmp_pos_v[i], cmp_k_w1[i], cmp_k_w2[i],
                                   cmp_v_w1[i], cmp_v_w2[i])
        else:
            h = h + fox_mixer(hn, odd_w_in[i], odd_b_forget[i], odd_w_out[i])
        h = h + sqrelu_mlp(rmsnorm(h, mlp_norm[layer]), mlp_w1[layer], mlp_w2[layer])
    return rmsnorm(h, final_norm)


def setup_inputs(seed=0):
    out = dict(first_inputs(seed))
    for name, value in second_inputs(seed + 1).items():
        if name != "x":
            out[name + "_2"] = value
    return out


def reference(
    x, c, ctx, c_ctx, w_mod, b_mod, norm_attn_pre, norm_attn_post, norm_ffn_pre, norm_ffn_post,
    w_in, norm_q_lat, norm_kv_lat, w_q_up, w_kv_up, w_fourier, w_out, w_router, b_router,
    w_gate, b_gate, w_up, b_up, w_down, b_down, rel_bias_2, mix_norm_2, mlp_norm_2, even_w_in_2,
    even_w_out_2, cmp_pos_k_2, cmp_pos_v_2, cmp_k_w1_2, cmp_k_w2_2, cmp_v_w1_2, cmp_v_w2_2,
    odd_w_in_2, odd_b_forget_2, odd_w_out_2, mlp_w1_2, mlp_w2_2, final_norm_2,
):
    x = first_block(
        x, c, ctx, c_ctx, w_mod, b_mod, norm_attn_pre, norm_attn_post, norm_ffn_pre,
        norm_ffn_post, w_in, norm_q_lat, norm_kv_lat, w_q_up, w_kv_up, w_fourier, w_out,
        w_router, b_router, w_gate, b_gate, w_up, b_up, w_down, b_down,
    )
    return second_block(
        x, rel_bias_2, mix_norm_2, mlp_norm_2, even_w_in_2, even_w_out_2, cmp_pos_k_2,
        cmp_pos_v_2, cmp_k_w1_2, cmp_k_w2_2, cmp_v_w1_2, cmp_v_w2_2, odd_w_in_2, odd_b_forget_2,
        odd_w_out_2, mlp_w1_2, mlp_w2_2, final_norm_2,
    )


_drawn_inputs = setup_inputs


def setup_inputs(seed=0):
    import zlib

    import numpy as np

    out = dict(_drawn_inputs(seed))
    spreads = {}
    factors = {'norm_ffn_post': 3.228,
     'norm_q_lat': 7.241,
     'norm_kv_lat': 2.799,
     'b_router': 2.773,
     'b_gate': 8.0,
     'b_up': 8.0,
     'b_down': 8.0,
     'mix_norm_2': 5.627,
     'cmp_pos_k_2': 8.0,
     'final_norm_2': 2.869}
    for name, (base, spread) in spreads.items():
        noise = np.random.default_rng([zlib.crc32(name.encode()), seed]).standard_normal(out[name].shape)
        drawn = base * np.exp(spread * noise) if base else spread * noise
        out[name] = __import__('jax').numpy.asarray(drawn.astype(out[name].dtype))
    for name, factor in factors.items():
        out[name] = (out[name] * factor).astype(out[name].dtype)
    return out
```

```python
import math
from contextlib import ExitStack

import numpy as np

import concourse.bass as bass
import concourse.mybir as mybir

F32 = mybir.dt.float32
I32 = mybir.dt.int32
U32 = mybir.dt.uint32
ALU = mybir.AluOpType
ACT = mybir.ActivationFunctionType
AX = mybir.AxisListType.X

P = 128
D = 1024
C = D // P
SEQ = 256
QT = SEQ // P
NEG = -1e30

HEADS = 6
NOPE, ROPE, VDIM = 128, 64, 128
QLAT, KVLAT = 384, 256
FOUR = 256
IN_W = FOUR + QLAT + KVLAT + ROPE
EPS = 1e-6
EXPERTS, TOPK, FF = 32, 4, 1024
SLOTS = 64
SPARE = (SEQ * TOPK) // (SLOTS + 1)
PASSES = EXPERTS + SPARE + 1
LIMIT, ALPHA = 7.0, 1.702

HD = 64
EVEN_IN = 2840
MQ, MK, MV, NQ, KC, VC, KSL, VSL, KWN, VWN, GZ = 0, 512, 1024, 1536, 2048, 2176, 2304, 2432, 2560, 2688, 2816
ODD_IN = 3088
CMP_BLOCK, CMP_STRIDE, CMP_HID = 32, 16, 256
NCMP = (SEQ - CMP_BLOCK) // CMP_STRIDE + 1
BUCKETS = 32
DFF2 = 4096
EPS2 = 1e-5

ROWS = {}
_at = 0
for _name, _n in (("pre", 8), ("mix", 16), ("mlp", 16), ("qlat", 3), ("kvlat", 2), ("c", 8), ("cctx", 8), ("bmod", 16)):
    ROWS[_name] = (_at, _n)
    _at += _n
NROWS = _at

CONST = {}
_at = 0
for _name, _n in (("ident", P), ("ones", P), ("swap", P), ("ccos", P), ("csin", P), ("tri", QT * SEQ), ("stri", QT * SEQ),
                  ("cos", SEQ), ("sin", SEQ), ("ncos", QT * SEQ), ("nsin", QT * SEQ), ("iota", P),
                  ("causal", QT * SEQ),
                  ("cmpmask", QT * NCMP), ("cmpvalid", QT), ("etri", EXPERTS)):
    CONST[_name] = (_at, _n)
    _at += _n
NCONST = _at


def shape_constants():
    out = np.zeros((P, NCONST), np.float32)
    buckets = np.zeros((BUCKETS, 3, 512), np.float32)

    def put(name, a):
        a = np.asarray(a, np.float32)
        a = a.reshape(a.shape[0], -1)
        at, n = CONST[name]
        out[:a.shape[0], at:at + n] = a

    eye = np.eye(P)
    put("ident", eye)
    put("ones", np.ones((P, P)))
    swap = np.zeros((P, P))
    for i in range(P // 2):
        swap[2 * i + 1, 2 * i] = -1.0
        swap[2 * i, 2 * i + 1] = 1.0
    put("swap", swap)
    k = np.arange(HD)
    ang = 2 * np.pi * np.outer(k, k) / HD
    put("ccos", np.kron(np.eye(2), np.cos(ang)))
    put("csin", np.kron(np.eye(2), np.sin(ang)))
    n = np.arange(SEQ)
    incl = (n[:, None] <= n[None, :]).astype(np.float32).reshape(QT, P, SEQ).transpose(1, 0, 2)
    strict = (n[:, None] < n[None, :]).astype(np.float32).reshape(QT, P, SEQ).transpose(1, 0, 2)
    put("tri", incl)
    put("stri", strict)
    half = ROPE // 2
    inv = (1.0 / (np.float32(10000.0) ** (np.arange(0, half, 2, dtype=np.float32) / np.float32(half)))).astype(np.float32)
    row = (n // 64).astype(np.float32)
    col = (n % 64).astype(np.float32)
    a = np.concatenate([row[:, None] * inv, col[:, None] * inv], axis=-1)
    put("cos", np.tile(np.repeat(np.cos(a).T, 2, axis=0), (2, 1)))
    put("sin", np.tile(np.repeat(np.sin(a).T, 2, axis=0), (2, 1)))
    big = 2 * np.pi * (np.outer(n, n) % SEQ) / SEQ
    norm = 1.0 / math.sqrt(SEQ * HD)
    put("ncos", (np.cos(big) * norm).reshape(QT, P, SEQ).transpose(1, 0, 2))
    put("nsin", (-np.sin(big) * norm).reshape(QT, P, SEQ).transpose(1, 0, 2))
    put("iota", np.tile(np.arange(P), (P, 1)))
    nf = np.maximum(n, 1).astype(np.float32)
    large = 16 + (np.log(nf / np.float32(16)) / np.float32(math.log(64)) * np.float32(16)).astype(np.int32)
    bucket = np.where(n < 16, n, np.minimum(large, BUCKETS - 1))
    fwd = np.zeros((BUCKETS, 512))
    fwd[bucket, n + 256] = 1.0
    buckets[:, 0] = fwd
    buckets[:, 1] = fwd[:, ::-1]
    buckets[:, 2] = np.where(np.arange(512) <= 255, 0.0, NEG)
    q = n[:, None]
    put("causal", np.where(n[None, :] <= q, 0.0, NEG).reshape(QT, P, SEQ).transpose(1, 0, 2))
    end = np.arange(NCMP) * CMP_STRIDE + CMP_BLOCK - 1
    seen = end[None, :] <= q
    put("cmpmask", np.where(seen, 0.0, NEG).reshape(QT, P, NCMP).transpose(1, 0, 2))
    put("cmpvalid", seen.any(1).astype(np.float32).reshape(QT, P).T)
    e = np.arange(EXPERTS)
    put("etri", (e[:, None] < e[None, :]).astype(np.float32))
    return out, buckets


def bcast_row(ap, n):
    return bass.AP(ap.tensor, ap.offset, [[0, P], [1, n]])


def stack(ap, p=P):
    return ap.rearrange("(c p) n -> p c n", p=p)


class Memory:

    def __init__(self, nc):
        self.nc = nc
        self.stack = ExitStack()
        self.of_stage, self.of_last = [], []

    def sb(self, name, shape, dt=F32):
        return self.stack.enter_context(self.nc.sbuf_tensor(name, shape, dt))

    def lasting(self, name):
        return self.stack.enter_context(self.nc.semaphore(name))

    def sem(self, name):
        context = self.nc.semaphore(name)
        s = context.__enter__()
        self.of_stage.append((context, s))
        return s

    def clear_last(self, pool):
        for _, s in self.of_last:
            pool.sem_clear(s)

    def end_stage(self):
        for context, _ in self.of_last:
            context.__exit__(None, None, None)
        self.of_stage, self.of_last = [], self.of_stage


def cst(m, name, rows=P, lo=0, n=None):
    at, width = CONST[name]
    return m.consts[0:rows, at + lo:at + (width if n is None else lo + n)]


def col(m, name, i=0, n=1):
    at, _ = ROWS[name]
    return m.cols[:, at + i:at + i + n]


def spread(ap, n):
    return ap.rearrange("p (a b) -> p a b", b=1).to_broadcast([ap.shape[0], ap.shape[1], n])


def stage_input(nc, m, t):
    s = m.stage = Memory(nc)
    rows = s.sb("rows", [P, P])
    ctx_sb = s.sb("ctx_sb", [P, QT, D])
    xn = m.hT[:].rearrange("p c n -> p (c n)").rearrange("p (i n) -> p i n", i=QT)
    hcT = s.sb("hcT", [P, C, SEQ])
    junk = s.sb("junk", [P, D])
    sums = s.sb("sums", [P, 16])
    std = s.sb("std", [P, 16])
    rstd = s.sb("rstd", [P, 16])
    silu = m.silu
    modv = s.sb("modv", [P, 16, 2])
    gain = s.sb("gain", [P, C, 2])
    buckets = s.sb("buckets", [BUCKETS, 2, 512])
    line = s.sb("line", [16, 512])
    tab = s.sb("tab", [BUCKETS, 16])
    qlat = s.sb("qlat", [P, QT, QLAT])
    kvlat = s.sb("kvlat", [P, 2 * QT, KVLAT])

    consts_in, rows_in, x_in, ctx_in, tab_in = (m.sem(n) for n in ("consts_in", "rows_in", "x_in", "ctx_in", "tab_in"))
    moda_in = [m.sem(f"moda_in{c}") for c in range(C)]
    win_in = [m.sem("win_in0"), m.sem("win_in1")]
    m.up_in = m.lasting("up_in")
    squares, stds, rstds, normed = (m.sem(n) for n in ("squares", "stds", "rstds", "normed"))
    rows_t, cols_ready, silu_ready, xt_ps, ctx_ps, moda_ps = (
        m.sem(n) for n in ("rows_t", "cols_ready", "silu_ready", "xt_ps", "ctx_ps", "moda_ps"))
    modv_ready, gain_ready, hT_ready, hcT_ready = (m.sem(n) for n in ("modv_ready", "gain_ready", "hT_ready", "hcT_ready"))
    line_ps, line_ready = m.sem("line_ps"), m.sem("line_ready")
    proj_ps, lat_raw, rope_raw, lat_sq, lat_std, lat_rstd, lat_normed, lat_tps, lat_ready = (
        m.sem(n) for n in ("proj_ps", "lat_raw", "rope_raw", "lat_sq", "lat_std", "lat_rstd", "lat_normed", "lat_tps", "lat_ready"))
    m.toeplitz_out = m.lasting("toeplitz_out")
    ps = m.ps
    win = m.ring[:, 16:24, :]

    with nc.Block() as block:

        @block.gpsimd
        def _(pool):
            m.clear_last(pool)

        @block.sync
        def _(sp):
            sp.dma_start(m.consts[:], t["consts"]).then_inc(consts_in, 16)
            sp.dma_start(tab[:], t["rel_bias_2"]).then_inc(tab_in, 16)
            sp.dma_start(buckets[:], t["buckets"][:, 1:3, :]).then_inc(tab_in, 16)
            for name, src in (("pre", t["norm_attn_pre"]), ("mix", t["mix_norm_2"]), ("mlp", t["mlp_norm_2"]),
                              ("qlat", t["norm_q_lat"]), ("kvlat", t["norm_kv_lat"]), ("c", t["c"]),
                              ("cctx", t["c_ctx"]), ("bmod", t["b_mod"])):
                at, n = ROWS[name]
                flat = bass.AP(src.tensor, 0, [[P, n], [1, P]])
                sp.dma_start(rows[at:at + n, :], flat).then_inc(rows_in, 16)
            sp.dma_start(m.x[:], stack(t["x"][0])).then_inc(x_in, 16)
            sp.dma_start(ctx_sb[:], stack(t["ctx"][0])).then_inc(ctx_in, 16)
            for c in range(C):
                sp.dma_start(m.ring[:, 2 * c:2 * c + 2, :].rearrange("p a n -> p (a n)"),
                             t["w_mod"][0, c * P:(c + 1) * P, 0:2 * D]).then_inc(moda_in[c], 16)
            for i in range(2):
                src = stack(t["w_in"][0, 512 * i:512 * i + 512, :])
                sp.dma_start(win[:, 4 * i:4 * i + 4, 0:IN_W], src).then_inc(win_in[i], 16)
                sp.dma_start(win[:, 4 * i:4 * i + 4, IN_W:D], src[:, :, IN_W - ROPE:IN_W]).then_inc(win_in[i], 16)
            sp.wait_ge(line_ready, 1)
            src = line[:, 0:511].rearrange("h (a n) -> h a n", a=1).to_broadcast([16, P, 511])
            sp.dma_start(bass.AP(t["toeplitz"].tensor, 0, [[P * 512, 16], [511, P], [1, 511]]), src).then_inc(m.toeplitz_out, 16)
            for k in range(3):
                src = t["w_q_up"][0, k * P:(k + 1) * P, :].rearrange("p (h n) -> p h n", h=HEADS)
                sp.dma_start(m.wq[:, k, :].rearrange("p (h n) -> p h n", h=HEADS), src[:, :, 0:NOPE]).then_inc(m.up_in, 16)
                sp.dma_start(m.wqr[:, k, :].rearrange("p (h n) -> p h n", h=HEADS), src[:, :, NOPE:]).then_inc(m.up_in, 16)
            sp.dma_start(m.wkv[:], stack(t["w_kv_up"][0])).then_inc(m.up_in, 16)

        @block.scalar
        def _(act):
            def rms(src, i, sem_value):
                act.activation(junk[:, 0:src.shape[1]], src, ACT.Square, accum_out=sums[:, i:i + 1]).then_inc(squares, 1)

            act.wait_ge(x_in, 16)
            for i in range(QT):
                if i:
                    act.wait_ge(squares, i)
                rms(m.x[:, i, :], i, 0)
            act.wait_ge(ctx_in, 16)
            for i in range(QT):
                act.wait_ge(squares, QT + i)
                rms(ctx_sb[:, i, :], QT + i, 0)
            act.wait_ge(squares, 4)
            act.wait_ge(m.init, 1)
            act.activation(std[:, 0:4], sums[:, 0:4], ACT.Sqrt, scale=1.0 / D, bias=m.eps[:, 0:1]).then_inc(stds, 1)
            act.wait_ge(cols_ready, 1)
            at = ROWS["c"][0]
            act.activation(silu[:].rearrange("p c s -> p s c"),
                           m.cols[:, at:at + 16].rearrange("p (s c) -> p s c", s=2), ACT.Silu).then_inc(silu_ready, 1)
            act.wait_ge(gain_ready, 1)
            act.wait_ge(ctx_ps, 1)
            for c in range(C):
                act.activation(hcT[:, c, :], ps[:, 4 + c // 2, (c % 2) * SEQ:(c % 2 + 1) * SEQ], ACT.Identity,
                               bias=modv[:, c, 1:2], scale=gain[:, c, 1:2]).then_inc(hcT_ready, 1)
            act.wait_ge(proj_ps, 1)
            act.copy(qlat[:], ps[:, 0:2, 0:QLAT]).then_inc(lat_raw, 1)
            act.wait_ge(proj_ps, 2)
            act.copy(kvlat[:].rearrange("p a n -> p (a n)"), ps[:, 2:4, :].rearrange("p a n -> p (a n)")).then_inc(lat_raw, 1)
            act.wait_ge(lat_raw, 2)
            for i in range(QT):
                if i:
                    act.wait_ge(lat_sq, i)
                act.activation(junk[:, 0:QLAT], qlat[:, i, :], ACT.Square, accum_out=sums[:, 4 + i:5 + i]).then_inc(lat_sq, 1)
            for i in range(2 * QT):
                act.wait_ge(lat_sq, QT + i)
                act.activation(junk[:, 0:KVLAT], kvlat[:, i, :], ACT.Square, accum_out=sums[:, 6 + i:7 + i]).then_inc(lat_sq, 1)
            act.wait_ge(lat_sq, 6)
            act.activation(std[:, 4:6], sums[:, 4:6], ACT.Sqrt, scale=1.0 / QLAT, bias=m.eps[:, 0:1]).then_inc(lat_std, 1)
            act.activation(std[:, 6:10], sums[:, 6:10], ACT.Sqrt, scale=1.0 / KVLAT, bias=m.eps[:, 0:1]).then_inc(lat_std, 1)
            act.wait_ge(lat_tps, 1)
            for k in range(3):
                act.activation(m.qlatT[:, k, :], ps[:, k // 2, (k % 2) * SEQ:(k % 2 + 1) * SEQ], ACT.Copy,
                               scale=col(m, "qlat", k)).then_inc(lat_ready, 1)
            act.wait_ge(lat_tps, 2)
            for k in range(2):
                act.activation(m.kvlatT[:, k, :], ps[:, 2 + k, :], ACT.Copy, scale=col(m, "kvlat", k)).then_inc(lat_ready, 1)

        @block.vector
        def _(v):
            v.memset(m.eps[:, 0:1], EPS)
            v.memset(m.eps[:, 1:2], EPS2).then_inc(m.init, 1)
            v.wait_ge(rows_t, 1)
            v.tensor_copy(m.cols[:], ps[:, 7, 0:NROWS]).then_inc(cols_ready, 1)
            v.wait_ge(stds, 1)
            v.reciprocal(rstd[:, 0:4], std[:, 0:4]).then_inc(rstds, 1)
            v.wait_ge(rstds, 1)
            for i in range(QT):
                v.tensor_scalar(xn[:, i, :], m.x[:, i, :], rstd[:, i:i + 1], None, ALU.mult).then_inc(normed, 1)
            for i in range(QT):
                v.tensor_scalar(ctx_sb[:, i, :], ctx_sb[:, i, :], rstd[:, 2 + i:3 + i], None, ALU.mult).then_inc(normed, 1)
            v.wait_ge(line_ps, 1)
            v.wait_ge(tab_in, 32)
            v.tensor_tensor(line[:], ps[0:16, 6, :], buckets[0:16, 1, :], ALU.add).then_inc(line_ready, 1)
            v.wait_ge(moda_ps, 1)
            v.wait_ge(cols_ready, 1)
            v.tensor_tensor(modv[:], ps[:, 7, 0:32].rearrange("p (a s) -> p a s", s=2), spread(col(m, "bmod", 0, 16), 2),
                            ALU.add).then_inc(modv_ready, 1)
            v.wait_ge(modv_ready, 1)
            v.scalar_tensor_tensor(gain[:], modv[:, 8:16, :], 1.0, spread(col(m, "pre", 0, 8), 2), ALU.add, ALU.mult).then_inc(gain_ready, 1)
            v.wait_ge(gain_ready, 1)
            v.wait_ge(xt_ps, 1)
            for c in range(C):
                v.tensor_scalar(m.hT[:, c, :], ps[:, c // 2, (c % 2) * SEQ:(c % 2 + 1) * SEQ], gain[:, c, 0:1],
                                modv[:, c, 0:1], ALU.mult, ALU.add).then_inc(hT_ready, 1)
            v.wait_ge(proj_ps, 3)
            v.tensor_copy(m.kropeT[:], ps[:, 4, :]).then_inc(rope_raw, 1)
            v.wait_ge(proj_ps, 4)
            v.tensor_copy(m.uT[:].rearrange("p a n -> p (a n)"), ps[:, 5, :]).then_inc(rope_raw, 1)
            v.wait_ge(lat_std, 2)
            v.reciprocal(rstd[:, 4:10], std[:, 4:10]).then_inc(lat_rstd, 1)
            v.wait_ge(lat_rstd, 1)
            for i in range(QT):
                v.tensor_scalar(qlat[:, i, :], qlat[:, i, :], rstd[:, 4 + i:5 + i], None, ALU.mult).then_inc(lat_normed, 1)
            for i in range(2 * QT):
                v.tensor_scalar(kvlat[:, i, :], kvlat[:, i, :], rstd[:, 6 + i:7 + i], None, ALU.mult).then_inc(lat_normed, 1)

        @block.tensor
        def _(pe):
            ident = cst(m, "ident")
            pe.wait_ge(consts_in, 16)
            pe.wait_ge(rows_in, 16 * len(ROWS))
            pe.transpose(ps[:, 7, 0:NROWS], rows[0:NROWS, :], ident[0:NROWS, 0:NROWS]).then_inc(rows_t, 1)
            pe.wait_ge(tab_in, 32)
            pe.matmul(ps[0:16, 6, :], tab[:], buckets[:, 0, :], start=True, stop=True).then_inc(line_ps, 1)
            pe.wait_ge(normed, QT)
            for c in range(C):
                for i in range(QT):
                    mm = pe.transpose(ps[:, c // 2, (c % 2) * SEQ + i * P:(c % 2) * SEQ + (i + 1) * P],
                                      xn[:, i, c * P:(c + 1) * P], ident)
            mm.then_inc(xt_ps, 1)
            pe.wait_ge(silu_ready, 1)
            for c in range(C):
                pe.wait_ge(moda_in[c], 16)
                for j in range(16):
                    mm = pe.matmul(ps[:, 7, 2 * j:2 * j + 2], m.ring[:, 2 * c + j // 8, (j % 8) * P:(j % 8 + 1) * P],
                                   silu[:, c, :], start=(c == 0 and j == 0), stop=(c == C - 1), skip_group_check=True)
            mm.then_inc(moda_ps, 1)
            pe.wait_ge(modv_ready, 1)
            pe.wait_ge(line_ready, 1)
            pe.wait_ge(normed, 2 * QT)
            for c in range(C):
                for i in range(QT):
                    mm = pe.transpose(ps[:, 4 + c // 2, (c % 2) * SEQ + i * P:(c % 2) * SEQ + (i + 1) * P],
                                      ctx_sb[:, i, c * P:(c + 1) * P], ident)
            mm.then_inc(ctx_ps, 1)
            pe.wait_ge(hT_ready, C)
            for i in range(2):
                pe.wait_ge(win_in[i], 32)
            for i in range(QT):
                for c in range(C):
                    mm = pe.matmul(ps[:, i, 0:QLAT], m.hT[:, c, i * P:(i + 1) * P], win[:, c, FOUR:FOUR + QLAT],
                                   start=(c == 0), stop=(c == C - 1))
            mm.then_inc(proj_ps, 1)
            for i in range(2 * QT):
                if i == QT:
                    pe.wait_ge(hcT_ready, C)
                src = m.hT if i < QT else hcT
                for c in range(C):
                    mm = pe.matmul(ps[:, 2 + i // 2, (i % 2) * KVLAT:(i % 2 + 1) * KVLAT], src[:, c, (i % 2) * P:(i % 2 + 1) * P],
                                   win[:, c, FOUR + QLAT:FOUR + QLAT + KVLAT], start=(c == 0), stop=(c == C - 1))
            mm.then_inc(proj_ps, 1)
            for j, src in enumerate((m.hT, hcT)):
                for c in range(C):
                    mm = pe.matmul(ps[:, 4, j * SEQ:(j + 1) * SEQ], win[:, c, D - P:D], src[:, c, :], start=(c == 0), stop=(c == C - 1))
            mm.then_inc(proj_ps, 1)
            for j in range(2):
                for c in range(C):
                    mm = pe.matmul(ps[:, 5, j * SEQ:(j + 1) * SEQ], win[:, c, j * P:(j + 1) * P], m.hT[:, c, :],
                                   start=(c == 0), stop=(c == C - 1))
            mm.then_inc(proj_ps, 1)
            pe.wait_ge(lat_raw, 2)
            pe.wait_ge(lat_normed, QT)
            for k in range(3):
                for i in range(QT):
                    mm = pe.transpose(ps[:, k // 2, (k % 2) * SEQ + i * P:(k % 2) * SEQ + (i + 1) * P],
                                      qlat[:, i, k * P:(k + 1) * P], ident)
            mm.then_inc(lat_tps, 1)
            pe.wait_ge(lat_normed, 3 * QT)
            for k in range(2):
                for i in range(2 * QT):
                    mm = pe.transpose(ps[:, 2 + k, i * P:(i + 1) * P], kvlat[:, i, k * P:(k + 1) * P], ident)
            mm.then_inc(lat_tps, 1)
    s.stack.close()


def stage_latent(nc, m, t):
    s = Memory(nc)
    qropeT = s.sb("qropeT", [P, 3, SEQ])
    val = s.sb("val", [P, 4, HEADS * VDIM])
    qn = s.sb("qn", [P, 2, SEQ])
    kn = s.sb("kn", [P, 2, 2 * SEQ])
    prob = s.sb("prob", [P, QT, 512])
    probT = s.sb("probT", [P, 4, SEQ])
    bd = s.sb("bd", [P, 2, 2, P])
    wf = s.sb("wf", [P, 2, HD])
    top = s.sb("top", [P, 4 * HEADS])
    turn = prob[:].rearrange("p a n -> p (a n)")
    vs = probT[:].rearrange("p a n -> p (a n)").rearrange("p (a i n) -> p a i n", a=2, i=2)
    mixT = m.hT
    ps = m.ps
    acc = m.ring[:, 20:24, :].rearrange("p a n -> p (a n)")
    SCALE = (NOPE + ROPE) ** -0.5
    modb_slot = [0, 4, 8, 12, 16, 0, 4, 8]

    wf_in, acc_zero, acc_in, modb_done, bd_zero = (m.sem(n) for n in ("wf_in", "acc_zero", "acc_in", "modb_done", "bd_zero"))
    modb_in = [m.sem(f"modb_in{c}") for c in range(C)]
    m.wout_in = [m.lasting("wout_in0"), m.lasting("wout_in1")]
    m.rowvec_in = m.lasting("rowvec_in")
    rope_ps, rope_sb, rope_mul, rope_done = (m.sem(n) for n in ("rope_ps", "rope_sb", "rope_mul", "rope_done"))
    val_ps, val_sb = m.sem("val_ps"), m.sem("val_sb")
    four_ps, four_sb = m.sem("four_ps"), m.sem("four_sb")
    qk_ps, q_sb, k_sb, s_ps, s_max, s_neg, s_exp, s_inv, s_prob = (
        m.sem(n) for n in ("qk_ps", "q_sb", "k_sb", "s_ps", "s_max", "s_neg", "s_exp", "s_inv", "s_prob"))
    pt_ps, pt_sb0, pt_sb1, pv_ps, pv_sb = (m.sem(n) for n in ("pt_ps", "pt_sb0", "pt_sb1", "pv_ps", "pv_sb"))

    with nc.Block() as block:

        @block.sync
        def _(sp):
            sp.dma_start(wf[:], t["w_fourier"][0].rearrange("(a b) c d -> (b c) a d", b=2)).then_inc(wf_in, 16)
            sp.wait_ge(acc_zero, 1)
            sp.dma_start(acc[0:1, :], t["b_mod"][0:1, 2 * D:]).then_inc(acc_in, 16)
            for c in range(C):
                if c >= 5:
                    sp.wait_ge(modb_done, c - 4)
                a = modb_slot[c]
                sp.dma_start(m.ring[:, a:a + 4, :].rearrange("p a n -> p (a n)"),
                             t["w_mod"][0, c * P:(c + 1) * P, 2 * D:]).then_inc(modb_in[c], 16)
            sp.wait_ge(modb_done, 5)
            for i in range(2):
                sp.dma_start(m.ring[:, 12 + 4 * i:16 + 4 * i, :], stack(t["w_out"][0, 512 * i:512 * i + 512, :])).then_inc(m.wout_in[i], 16)
            sp.wait_ge(modb_done, 6)
            for j, name in enumerate(("norm_attn_post", "norm_ffn_pre", "norm_ffn_post")):
                sp.dma_start(m.ring[:, j, :], bcast_row(t[name], D)).then_inc(m.rowvec_in, 16)

        @block.gpsimd
        def _(pool):
            m.clear_last(pool)
            pool.memset(acc, 0.0).then_inc(acc_zero, 1)
            pool.memset(bd[:], 0.0).then_inc(bd_zero, 1)

        @block.tensor
        def _(pe):
            ident = cst(m, "ident")
            pe.wait_ge(m.up_in, 16 * 7)
            for j in range(3):
                for k in range(3):
                    mm = pe.matmul(ps[:, j // 2, (j % 2) * SEQ:(j % 2 + 1) * SEQ], m.wqr[:, k, j * P:(j + 1) * P],
                                   m.qlatT[:, k, :], start=(k == 0), stop=(k == 2))
            mm.then_inc(rope_ps, 1)
            pe.matmul(ps[:, 2, 0:SEQ], cst(m, "swap"), m.kropeT[:, 0:SEQ], start=True, stop=True).then_inc(rope_ps, 1)
            pe.wait_ge(rope_sb, 1)
            pe.matmul(ps[:, 3, :], cst(m, "swap"), qropeT[:, 0:2, :], start=True, stop=True)
            pe.matmul(ps[:, 4, 0:SEQ], cst(m, "swap"), qropeT[:, 2, :], start=True, stop=True).then_inc(rope_ps, 1)
            wv = [m.wkv[:, k, :].rearrange("p (h n) -> p h n", h=HEADS)[:, :, NOPE:] for k in range(2)]
            for n, i in enumerate((3, 0, 1, 2)):
                a = 2 * i
                if n == 1:
                    pe.wait_ge(rope_done, 2)
                for lo, hi in ((0, 4), (4, HEADS)):
                    for k in range(2):
                        mm = pe.matmul(ps[:, a, 0:(hi - lo) * VDIM], m.kvlatT[:, k, i * P:(i + 1) * P], wv[k][:, lo:hi, :],
                                       start=(k == 0), stop=(k == 1))
                    a += 1
                mm.then_inc(val_ps, 1)
            pe.wait_ge(wf_in, 16)
            pe.wait_ge(val_sb, 4)
            for a in range(2):
                for b, name in enumerate(("ccos", "csin")):
                    mm = pe.matmul(ps[:, 0, (2 * a + b) * HD:(2 * a + b + 1) * HD], cst(m, name), wf[:, a, :], start=True, stop=True)
            mm.then_inc(four_ps, 1)
            pe.wait_ge(four_sb, 2)
            for a in range(2):
                for i in range(QT):
                    mm = pe.matmul(ps[:, 1 + a, i * SEQ:(i + 1) * SEQ], m.uT[:, a, i * P:(i + 1) * P],
                                   bd[:, a, :, :].rearrange("p b n -> p (b n)"), start=True, stop=True)
            mm.then_inc(four_ps, 1)
            pe.wait_ge(four_sb, 3)
            for a in range(2):
                for i in range(QT):
                    pe.matmul(ps[:, 3, a * SEQ:(a + 1) * SEQ], vs[:, a, i, 0:P], cst(m, "ncos", P, i * SEQ, SEQ), start=(i == 0), stop=False)
                    mm = pe.matmul(ps[:, 3, a * SEQ:(a + 1) * SEQ], vs[:, a, i, P:2 * P], cst(m, "nsin", P, i * SEQ, SEQ), start=False, stop=(i == 1))
            mm.then_inc(four_ps, 1)

            def project(h):
                if h:
                    pe.wait_ge(q_sb, h)
                    pe.wait_ge(k_sb, h)
                for k in range(3):
                    pe.matmul(ps[:, 0, 0:SEQ], m.wq[:, k, h * NOPE:(h + 1) * NOPE], m.qlatT[:, k, :], start=(k == 0), stop=(k == 2))
                for k in range(2):
                    mm = pe.matmul(ps[:, 1, :], m.wkv[:, k, h * 256:h * 256 + NOPE], m.kvlatT[:, k, :], start=(k == 0), stop=(k == 1))
                mm.then_inc(qk_ps, 1)

            def scores(h):
                pe.wait_ge(q_sb, h + 1)
                pe.wait_ge(k_sb, h + 1)
                if h:
                    pe.wait_ge(s_exp, QT * h)
                r = (h % 2) * ROPE
                for i in range(QT):
                    pe.matmul(ps[:, 2 + i, :], qn[:, h % 2, i * P:(i + 1) * P], kn[:, h % 2, :], start=True, stop=False)
                    mm = pe.matmul(ps[:, 2 + i, :], qropeT[r:r + ROPE, h // 2, i * P:(i + 1) * P], m.kropeT[r:r + ROPE, :],
                                   start=False, stop=True)
                mm.then_inc(s_ps, 1)

            pe.wait_ge(four_sb, 4)
            pe.wait_ge(rope_done, 2)
            project(0)
            scores(0)
            for h in range(HEADS):
                if h + 1 < HEADS:
                    project(h + 1)
                pe.wait_ge(s_prob, h + 1)
                if h:
                    pe.wait_ge(pt_sb0, h)
                    pe.wait_ge(pt_sb1, h)
                for k in range(4):
                    for i in range(QT):
                        mm = pe.transpose(ps[:, 4 + k // 2, (k % 2) * SEQ + i * P:(k % 2) * SEQ + (i + 1) * P],
                                          prob[:, i, k * P:(k + 1) * P], ident)
                mm.then_inc(pt_ps, 1)
                if h + 1 < HEADS:
                    scores(h + 1)
                pe.wait_ge(pt_sb0, h + 1)
                pe.wait_ge(pt_sb1, h + 1)
                if h >= 2:
                    pe.wait_ge(pv_sb, h - 1)
                for k in range(4):
                    mm = pe.matmul(ps[:, 6 + h % 2, 0:SEQ], val[:, k, h * VDIM:(h + 1) * VDIM], probT[:, k, :], start=(k == 0), stop=(k == 3))
                mm.then_inc(pv_ps, 1)

        @block.scalar
        def _(act):
            act.wait_ge(rope_ps, 1)
            act.copy(qropeT[:].rearrange("p a n -> p (a n)"), ps[:, 0:2, :].rearrange("p a n -> p (a n)")[:, 0:3 * SEQ]).then_inc(rope_sb, 1)
            for n, i in enumerate((3, 0, 1, 2)):
                act.wait_ge(val_ps, n + 1)
                act.copy(val[:, i, :], ps[:, 2 * i:2 * i + 2, :].rearrange("p a n -> p (a n)")[:, 0:HEADS * VDIM]).then_inc(val_sb, 1)
            act.wait_ge(bd_zero, 1)
            act.wait_ge(four_ps, 1)
            blocks = ps[:, 0, 0:4 * HD].rearrange("p (a b n) -> p a b n", a=2, b=2)
            act.copy(bd[0:HD, :, :, 0:HD], blocks[0:HD]).then_inc(four_sb, 1)
            act.copy(bd[HD:P, :, :, HD:P], blocks[HD:P]).then_inc(four_sb, 1)
            act.wait_ge(four_ps, 2)
            act.copy(probT[:].rearrange("p a n -> p (a n)"), ps[:, 1:3, :].rearrange("p a n -> p (a n)")).then_inc(four_sb, 1)
            act.wait_ge(four_ps, 3)
            act.copy(mixT[:, HEADS:HEADS + 2, :].rearrange("p a n -> p (a n)"), ps[:, 3, :]).then_inc(four_sb, 1)

            def evacuate_q(h):
                act.wait_ge(qk_ps, h + 1)
                if h >= 2:
                    act.wait_ge(s_ps, h - 1)
                act.copy(qn[:, h % 2, :], ps[:, 0, 0:SEQ]).then_inc(q_sb, 1)

            evacuate_q(0)
            for h in range(HEADS):
                if h + 1 < HEADS:
                    evacuate_q(h + 1)
                act.wait_ge(s_neg, h + 1)
                if h:
                    act.wait_ge(pt_ps, h)
                for i in range(QT):
                    act.activation(prob[:, i, :], ps[:, 2 + i, :], ACT.Exp, bias=top[:, 4 * h + i:4 * h + i + 1], scale=SCALE,
                                   accum_out=top[:, 4 * h + 2 + i:4 * h + 3 + i]).then_inc(s_exp, 1)
                act.wait_ge(pt_ps, h + 1)
                if h:
                    act.wait_ge(pv_ps, h)
                act.copy(probT[:, 0:2, :].rearrange("p a n -> p (a n)"), ps[:, 4, :]).then_inc(pt_sb0, 1)
                act.wait_ge(pv_ps, h + 1)
                act.copy(mixT[:, h, :], ps[:, 6 + h % 2, 0:SEQ]).then_inc(pv_sb, 1)

        @block.vector
        def _(v):
            cos, sin = cst(m, "cos"), cst(m, "sin")
            three = lambda a: a.rearrange("p (b n) -> p b n", b=1).to_broadcast([P, 3, SEQ])
            v.wait_ge(rope_ps, 2)
            v.tensor_tensor(turn[:, 768:1024], ps[:, 2, 0:SEQ], sin, ALU.mult).then_inc(rope_mul, 1)
            v.tensor_tensor(m.kropeT[:, 0:SEQ], m.kropeT[:, 0:SEQ], cos, ALU.mult).then_inc(rope_mul, 1)
            v.wait_ge(rope_mul, 2)
            v.tensor_tensor(m.kropeT[:, 0:SEQ], m.kropeT[:, 0:SEQ], turn[:, 768:1024], ALU.add).then_inc(rope_done, 1)
            v.wait_ge(rope_ps, 3)
            raw = ps[:, 3:5, :].rearrange("p a n -> p (a n)")[:, 0:768].rearrange("p (b n) -> p b n", b=3)
            mul = turn[:, 0:768].rearrange("p (b n) -> p b n", b=3)
            v.tensor_tensor(mul, raw, three(sin), ALU.mult).then_inc(rope_mul, 1)
            v.tensor_tensor(qropeT[:], qropeT[:], three(cos), ALU.mult).then_inc(rope_mul, 1)
            v.wait_ge(rope_mul, 4)
            v.tensor_tensor(qropeT[:], qropeT[:], mul, ALU.add).then_inc(rope_done, 1)

            def modulate(c):
                v.wait_ge(modb_in[c], 16)
                if c:
                    v.wait_ge(modb_done, c)
                else:
                    v.wait_ge(acc_in, 16)
                a = modb_slot[c]
                v.scalar_tensor_tensor(acc, m.ring[:, a:a + 4, :].rearrange("p a n -> p (a n)"), m.silu[:, c, 0:1], acc,
                                       ALU.mult, ALU.add).then_inc(modb_done, 1)

            def evacuate_k(h):
                v.wait_ge(qk_ps, h + 1)
                if h >= 2:
                    v.wait_ge(s_ps, h - 1)
                v.tensor_copy(kn[:, h % 2, :], ps[:, 1, :]).then_inc(k_sb, 1)

            modulate(0)
            modulate(1)
            evacuate_k(0)
            for h in range(HEADS):
                v.wait_ge(s_ps, h + 1)
                v.tensor_reduce(top[:, 4 * h:4 * h + 2], ps[:, 2:4, :], AX, ALU.max).then_inc(s_max, 1)
                v.wait_ge(s_max, h + 1)
                v.tensor_scalar(top[:, 4 * h:4 * h + 2], top[:, 4 * h:4 * h + 2], -SCALE, None, ALU.mult).then_inc(s_neg, 1)
                if h + 1 < HEADS:
                    evacuate_k(h + 1)
                v.wait_ge(s_exp, QT * (h + 1))
                v.reciprocal(top[:, 4 * h + 2:4 * h + 4], top[:, 4 * h + 2:4 * h + 4]).then_inc(s_inv, 1)
                v.wait_ge(s_inv, h + 1)
                v.tensor_tensor(prob[:], prob[:], spread(top[:, 4 * h + 2:4 * h + 4], 512), ALU.mult).then_inc(s_prob, 1)
                v.wait_ge(pt_ps, h + 1)
                if h:
                    v.wait_ge(pv_ps, h)
                v.tensor_copy(probT[:, 2:4, :].rearrange("p a n -> p (a n)"), ps[:, 5, :]).then_inc(pt_sb1, 1)
                if h + 2 < C:
                    modulate(h + 2)
    s.stack.close()


def stage_residual(nc, m, t):
    m.mla.stack.close()
    s = m.moe = Memory(nc)
    h2 = m.h2 = s.sb("h2", [P, QT, D])
    stats = s.sb("stats", [P, 8])
    ps = m.ps
    rows = m.ring[:, 20:24, :].rearrange("p a n -> p (a n)")
    r_post, r_ffn, r_fpost = (m.ring[:, j, :] for j in range(3))
    junk = m.ring[:, 4, :]
    sum_ps, sum_sb, mix_ps, mix_sq, mix_std, mix_inv, row_mul, mixed, added = (
        m.sem(n) for n in ("sum_ps", "sum_sb", "mix_ps", "mix_sq", "mix_std", "mix_inv", "row_mul", "mixed", "added"))
    x_sq, x_std, x_inv, h2_mul, h2_ready, h2_ps, h2T_ready = (
        m.sem(n) for n in ("x_sq", "x_std", "x_inv", "h2_mul", "h2_ready", "h2_ps", "h2T_ready"))

    with nc.Block() as block:

        @block.gpsimd
        def _(pool):
            m.clear_last(pool)

        @block.tensor
        def _(pe):
            ident, ones = cst(m, "ident"), cst(m, "ones")
            for j in range(4):
                pe.matmul(ps[:, 4 + j, :], ones, rows[:, 512 * j:512 * (j + 1)], start=True, stop=True).then_inc(sum_ps, 1)
            for i in range(2):
                pe.wait_ge(m.wout_in[i], 16)
            for i in range(QT):
                for half in range(2):
                    for c in range(C):
                        mm = pe.matmul(ps[:, 2 * i + half, :], m.hT[:, c, i * P:(i + 1) * P], m.ring[:, 12 + c, half * 512:(half + 1) * 512],
                                       start=(c == 0), stop=(c == C - 1))
                mm.then_inc(mix_ps, 1)
            for j in range(4):
                pe.wait_ge(sum_sb, j + 1)
                pe.matmul(ps[:, 4 + j, :], ones, rows[:, 2048 + 512 * j:2048 + 512 * (j + 1)], start=True, stop=True).then_inc(sum_ps, 1)
            pe.wait_ge(added, 2)
            for i in range(QT):
                pe.wait_ge(h2_ready, i + 1)
                if i == 0:
                    pe.wait_ge(sum_sb, 8)
                for c in range(C):
                    mm = pe.transpose(ps[:, 4 * i + c // 4, (c % 4) * P:(c % 4 + 1) * P], h2[:, i, c * P:(c + 1) * P], ident)
                mm.then_inc(h2_ps, 1)

        @block.scalar
        def _(act):
            for j in range(8):
                act.wait_ge(sum_ps, j + 1)
                if j < 4:
                    act.wait_ge(sum_ps, j + 1)
                act.copy(rows[:, 512 * j:512 * (j + 1)], ps[:, 4 + j % 4, :]).then_inc(sum_sb, 1)
                if j in (3,):
                    for i in range(QT):
                        act.wait_ge(mix_ps, i + 1)
                        if i:
                            act.wait_ge(mix_sq, i)
                        act.activation(junk, ps[:, 2 * i:2 * i + 2, :].rearrange("p a n -> p (a n)"), ACT.Square,
                                       accum_out=stats[:, i:i + 1]).then_inc(mix_sq, 1)
                    act.wait_ge(mix_sq, 2)
                    act.activation(stats[:, 2:4], stats[:, 0:2], ACT.Sqrt, scale=1.0 / D, bias=m.eps[:, 0:1]).then_inc(mix_std, 1)
            for i in range(QT):
                act.wait_ge(added, i + 1)
                act.wait_ge(mix_sq, 2)
                if i:
                    act.wait_ge(x_sq, i)
                act.activation(junk, m.x[:, i, :], ACT.Square, accum_out=stats[:, 4 + i:5 + i]).then_inc(x_sq, 1)
            act.wait_ge(x_sq, 2)
            act.activation(stats[:, 6:8], stats[:, 4:6], ACT.Sqrt, scale=1.0 / D, bias=m.eps[:, 0:1]).then_inc(x_std, 1)
            for i in range(QT):
                act.wait_ge(h2_ps, i + 1)
                act.copy(m.hT[:, 4 * 0:4, i * P:(i + 1) * P], ps[:, 4 * i, :].rearrange("p (c n) -> p c n", c=4)).then_inc(h2T_ready, 1)
                act.copy(m.hT[:, 4:8, i * P:(i + 1) * P], ps[:, 4 * i + 1, :].rearrange("p (c n) -> p c n", c=4)).then_inc(h2T_ready, 1)

        @block.vector
        def _(v):
            v.wait_ge(m.rowvec_in, 48)
            v.wait_ge(sum_sb, 2)
            v.tensor_tensor(r_post, r_post, rows[:, 0:D], ALU.mult).then_inc(row_mul, 1)
            v.wait_ge(mix_std, 1)
            v.reciprocal(stats[:, 2:4], stats[:, 2:4]).then_inc(mix_inv, 1)
            v.wait_ge(mix_inv, 1)
            v.wait_ge(row_mul, 1)
            for i in range(QT):
                v.scalar_tensor_tensor(h2[:, i, :], ps[:, 2 * i:2 * i + 2, :].rearrange("p a n -> p (a n)"), stats[:, 2 + i:3 + i],
                                       r_post, ALU.mult, ALU.mult).then_inc(mixed, 1)
                v.wait_ge(mixed, i + 1)
                v.tensor_tensor(m.x[:, i, :], m.x[:, i, :], h2[:, i, :], ALU.add).then_inc(added, 1)
            v.wait_ge(sum_sb, 8)
            v.scalar_tensor_tensor(r_ffn, rows[:, 2 * D:3 * D], 1.0, r_ffn, ALU.add, ALU.mult).then_inc(row_mul, 1)
            v.tensor_tensor(m.r_g2[:], rows[:, 3 * D:4 * D], r_fpost, ALU.mult).then_inc(row_mul, 1)
            v.wait_ge(x_std, 1)
            v.reciprocal(stats[:, 6:8], stats[:, 6:8]).then_inc(x_inv, 1)
            v.wait_ge(x_inv, 1)
            v.wait_ge(row_mul, 3)
            v.wait_ge(added, 2)
            for i in range(QT):
                v.scalar_tensor_tensor(h2[:, i, :], m.x[:, i, :], stats[:, 6 + i:7 + i], r_ffn, ALU.mult, ALU.mult).then_inc(h2_mul, 1)
                v.wait_ge(h2_mul, i + 1)
                v.tensor_tensor(h2[:, i, :], h2[:, i, :], rows[:, D:2 * D], ALU.add).then_inc(h2_ready, 1)


def stage_route(nc, m, t):
    s = m.moe
    m.keys = s.sb("keys", [P, QT, PASSES])
    m.gates = s.sb("gates", [P, QT, PASSES])
    m.brows = s.sb("brows", [P, 2, D])
    m.pick = s.sb("pick", [P, PASSES])
    m.table = s.sb("table", [1, PASSES + 1 + EXPERTS], I32)
    m.ysum = s.sb("ysum", [P, QT, D])
    r = Memory(nc)
    wr = r.sb("wr", [P, C, EXPERTS])
    br = r.sb("br", [1, EXPERTS])
    bdown = r.sb("bdown", [EXPERTS, D])
    logit = r.sb("logit", [P, QT, EXPERTS])
    best = r.sb("best", [P, QT, 8])
    index = r.sb("index", [P, QT, 8], U32)
    indexf = r.sb("indexf", [P, QT, 8])
    mask = r.sb("mask", [P, QT, EXPERTS])
    gate = r.sb("gate", [P, QT, EXPERTS])
    gsum = r.sb("gsum", [P, 2 * QT])
    key = r.sb("key", [P, QT, EXPERTS])
    keyT = r.sb("keyT", [EXPERTS, QT, P])
    gateT = r.sb("gateT", [EXPERTS, QT, P])
    more = r.sb("more", [EXPERTS, 4])
    tmp = r.sb("tmp", [EXPERTS, 3, PASSES])
    pick = m.pick[0:EXPERTS, :]
    base = r.sb("base", [EXPERTS, PASSES])
    ps = m.ps
    w_in, logit_ps, logit_sb, top8, top_i, top_f, picked, peak, exped = (
        m.sem(n) for n in ("w_in", "logit_ps", "logit_sb", "top8", "top_i", "top_f", "picked", "peak", "exped"))
    g_chain, rank_ps, key_ok, more_chain, more_ps, table_ok, turned_ps, turned_sb, spread_ps, spread_sb = (
        m.sem(n) for n in ("g_chain", "rank_ps", "key_ok", "more_chain", "more_ps", "table_ok", "turned_ps", "turned_sb",
                           "spread_ps", "spread_sb"))
    zeroed, bdown_in = m.sem("zeroed"), m.sem("bdown_in")
    m.brows_in = m.lasting("brows_in")
    m.moe_in = [m.lasting(f"moe_in{k}") for k in range(12)]

    with nc.Block() as block:

        @block.gpsimd
        def _(pool):
            m.clear_last(pool)
            pool.memset(m.brows[:], 0.0).then_inc(zeroed, 1)
            pool.memset(m.pick[:], 0.0).then_inc(zeroed, 1)

        @block.sync
        def _(sp):
            sp.dma_start(wr[:], stack(t["w_router"][0])).then_inc(w_in, 16)
            sp.dma_start(br[:], t["b_router"]).then_inc(w_in, 16)
            sp.dma_start(bdown[:], t["b_down"][0]).then_inc(bdown_in, 16)
            sp.wait_ge(zeroed, 2)
            for j, name in enumerate(("b_gate", "b_up")):
                sp.dma_start(m.brows[0:EXPERTS, j, :], t[name][0]).then_inc(m.brows_in, 16)
            for k in range(12):
                sp.dma_start(m.ring[:, 2 * k:2 * k + 2, :], expert_rows(t, 0, k)).then_inc(m.moe_in[k], 16)

        @block.tensor
        def _(pe):
            ident, ones = cst(m, "ident"), cst(m, "ones")
            pe.wait_ge(w_in, 32)
            for i in range(QT):
                for c in range(C):
                    pe.matmul(ps[:, 0, i * EXPERTS:(i + 1) * EXPERTS], m.hT[:, c, i * P:(i + 1) * P], wr[:, c, :], start=(c == 0), stop=False)
                mm = pe.matmul(ps[:, 0, i * EXPERTS:(i + 1) * EXPERTS], ones[0:1, :], br[:], start=False, stop=True)
            mm.then_inc(logit_ps, 1)
            pe.wait_ge(picked, 8)
            for i in range(QT):
                for j in range(QT):
                    pe.matmul(ps[:, 1, i * EXPERTS:(i + 1) * EXPERTS], cst(m, "stri", P, j * SEQ + i * P, P), mask[:, j, :],
                              start=(j == 0), stop=(j == QT - 1))
            for j in range(QT):
                pe.matmul(ps[0:EXPERTS, 2, 0:1], mask[:, j, :], ones[:, 0:1], start=(j == 0), stop=(j == QT - 1))
            pe.matmul(ps[0:EXPERTS, 2, 1:2], cst(m, "etri", EXPERTS), ones[0:EXPERTS, 0:1], start=True, stop=True).then_inc(rank_ps, 1)
            pe.wait_ge(more_chain, 5)
            pe.matmul(ps[0:EXPERTS, 2, 2:3], cst(m, "etri", EXPERTS), more[:, 1:2], start=True, stop=True)
            pe.matmul(ps[0:1, 3, PASSES:PASSES + 1], more[:, 1:2], ones[0:EXPERTS, 0:1], start=True, stop=True)
            pe.matmul(ps[0:1, 3, PASSES + 1:PASSES + 1 + EXPERTS], more[:, 1:2], cst(m, "etri", EXPERTS), start=True, stop=True).then_inc(more_ps, 1)
            pe.wait_ge(key_ok, 1)
            pe.wait_ge(g_chain, 5)
            for i in range(QT):
                pe.transpose(ps[0:EXPERTS, 4, i * P:(i + 1) * P], key[:, i, :], ident)
                mm = pe.transpose(ps[0:EXPERTS, 4, (2 + i) * P:(3 + i) * P], gate[:, i, :], ident)
            mm.then_inc(turned_ps, 1)
            pe.wait_ge(more_chain, 9)
            pe.matmul(ps[0:1, 3, 0:PASSES], more[:, 3:4], pick, start=True, stop=True).then_inc(more_ps, 1)
            pe.wait_ge(turned_sb, 2)
            pe.wait_ge(more_chain, 10)
            for i in range(QT):
                pe.matmul(ps[:, 5, i * PASSES:(i + 1) * PASSES], keyT[:, i, :], pick, start=True, stop=False)
                pe.matmul(ps[:, 5, i * PASSES:(i + 1) * PASSES], ones[0:EXPERTS, :], base[:], start=False, stop=True)
                mm = pe.matmul(ps[:, 5, (2 + i) * PASSES:(3 + i) * PASSES], gateT[:, i, :], pick, start=True, stop=True)
            mm.then_inc(spread_ps, 1)
            pe.wait_ge(bdown_in, 16)
            pe.wait_ge(table_ok, 2)
            for i in range(QT):
                for half in range(2):
                    mm = pe.matmul(ps[:, 2 * i + half, :], gateT[:, i, :], bdown[:, half * 512:(half + 1) * 512], start=True, stop=True)
            mm.then_inc(spread_ps, 1)

        @block.scalar
        def _(act):
            act.wait_ge(peak, 2)
            act.wait_ge(logit_sb, 1)
            for i in range(QT):
                act.activation(gate[:, i, :], logit[:, i, :], ACT.Exp, bias=gsum[:, i:i + 1]).then_inc(exped, 1)
            act.wait_ge(turned_ps, 1)
            act.copy(keyT[:].rearrange("e i n -> e (i n)"), ps[0:EXPERTS, 4, 0:SEQ]).then_inc(turned_sb, 1)
            act.copy(gateT[:].rearrange("e i n -> e (i n)"), ps[0:EXPERTS, 4, SEQ:2 * SEQ]).then_inc(turned_sb, 1)
            act.wait_ge(spread_ps, 2)
            act.copy(m.ysum[:].rearrange("p i n -> p (i n)"), ps[:, 0:4, :].rearrange("p a n -> p (a n)")).then_inc(spread_sb, 1)

        @block.vector
        def _(v):
            iota = cst(m, "iota")
            v.wait_ge(logit_ps, 1)
            v.tensor_copy(logit[:].rearrange("p i n -> p (i n)"), ps[:, 0, 0:QT * EXPERTS]).then_inc(logit_sb, 1)
            v.wait_ge(logit_sb, 1)
            for i in range(QT):
                v.max(best[:, i, :], logit[:, i, :]).then_inc(top8, 1)
            v.wait_ge(top8, 2)
            for i in range(QT):
                v.max_index(index[:, i, :], best[:, i, :], logit[:, i, :]).then_inc(top_i, 1)
                v.tensor_scalar(gsum[:, i:i + 1], best[:, i, 0:1], -1.0, None, ALU.mult).then_inc(peak, 1)
            v.wait_ge(top_i, 2)
            v.tensor_copy(indexf[:], index[:]).then_inc(top_f, 1)
            v.wait_ge(top_f, 1)
            for k in range(TOPK):
                for i in range(QT):
                    if k == 0:
                        v.tensor_scalar(mask[:, i, :], iota[:, 0:EXPERTS], indexf[:, i, 0:1], None, ALU.is_equal).then_inc(picked, 1)
                    else:
                        v.wait_ge(picked, QT * k)
                        v.scalar_tensor_tensor(mask[:, i, :], iota[:, 0:EXPERTS], indexf[:, i, k:k + 1], mask[:, i, :],
                                               ALU.is_equal, ALU.add).then_inc(picked, 1)
            v.wait_ge(exped, 2)
            v.wait_ge(picked, 8)
            v.tensor_tensor(gate[:], gate[:], mask[:], ALU.mult).then_inc(g_chain, 1)
            v.wait_ge(g_chain, 1)
            v.tensor_reduce(gsum[:, QT:2 * QT], gate[:], AX, ALU.add).then_inc(g_chain, 1)
            v.wait_ge(g_chain, 2)
            v.reciprocal(gsum[:, QT:2 * QT], gsum[:, QT:2 * QT]).then_inc(g_chain, 1)
            v.wait_ge(g_chain, 3)
            for i in range(QT):
                v.tensor_scalar(gate[:, i, :], gate[:, i, :], gsum[:, QT + i:QT + i + 1], None, ALU.mult).then_inc(g_chain, 1)
            v.wait_ge(rank_ps, 1)
            v.tensor_copy(more[:, 0:1], ps[0:EXPERTS, 2, 0:1])
            v.tensor_copy(more[:, 3:4], ps[0:EXPERTS, 2, 1:2]).then_inc(more_chain, 1)
            v.wait_ge(more_chain, 1)
            v.tensor_scalar(more[:, 1:2], more[:, 0:1], float(SLOTS), 1.0, ALU.is_gt, ALU.add).then_inc(more_chain, 1)
            for n in range(2, SEQ // SLOTS):
                v.wait_ge(more_chain, n)
                v.scalar_tensor_tensor(more[:, 1:2], more[:, 0:1], float(n * SLOTS), more[:, 1:2], ALU.is_gt, ALU.add).then_inc(more_chain, 1)
            v.wait_ge(zeroed, 2)
            v.wait_ge(more_chain, SEQ // SLOTS)
            v.sem_inc(more_chain, 1)
            v.scalar_tensor_tensor(key[:].rearrange("p i n -> p (i n)"), ps[:, 1, 0:QT * EXPERTS], 1.0,
                                   mask[:].rearrange("p i n -> p (i n)"), ALU.add, ALU.mult).then_inc(table_ok, 1)
            v.wait_ge(table_ok, 1)
            v.tensor_scalar(key[:], key[:], -1.0, None, ALU.add).then_inc(key_ok, 1)
            v.wait_ge(more_ps, 1)
            v.tensor_copy(more[:, 2:3], ps[0:EXPERTS, 2, 2:3]).then_inc(more_chain, 1)
            v.wait_ge(more_chain, 6)
            v.tensor_scalar(tmp[:, 0, :], iota[0:EXPERTS, 0:PASSES], more[:, 2:3], None, ALU.subtract).then_inc(more_chain, 1)
            v.wait_ge(more_chain, 7)
            v.tensor_scalar(tmp[:, 1, :], tmp[:, 0, :], more[:, 1:2], None, ALU.is_lt).then_inc(more_chain, 1)
            v.wait_ge(more_chain, 8)
            v.scalar_tensor_tensor(pick, tmp[:, 0, :], 0.0, tmp[:, 1, :], ALU.is_ge, ALU.mult).then_inc(more_chain, 1)
            v.wait_ge(more_chain, 9)
            v.scalar_tensor_tensor(base[:], tmp[:, 0, :], float(-SLOTS), pick, ALU.mult, ALU.mult).then_inc(more_chain, 1)
            v.wait_ge(more_ps, 2)
            v.tensor_copy(m.table[:, 0:PASSES + 1], ps[0:1, 3, 0:PASSES + 1])
            v.tensor_scalar(m.table[:, PASSES + 1:], ps[0:1, 3, PASSES + 1:PASSES + 1 + EXPERTS], -1.0, None, ALU.add).then_inc(table_ok, 1)
            v.wait_ge(spread_ps, 1)
            v.tensor_copy(m.keys[:].rearrange("p i n -> p (i n)"), ps[:, 5, 0:2 * PASSES]).then_inc(spread_sb, 1)
            v.tensor_copy(m.gates[:].rearrange("p i n -> p (i n)"), ps[:, 5, 2 * PASSES:4 * PASSES]).then_inc(spread_sb, 1)
    r.stack.close()


def expert_rows(t, e, k):
    w = t[("w_gate", "w_up", "w_down")[k // 4]]
    k %= 4
    if isinstance(e, int):
        return w[0, e, k * 256:(k + 1) * 256, :].rearrange("(a p) n -> p a n", p=P)
    return w[0, bass.ds(e, 1), k * 256:(k + 1) * 256, :].rearrange("e (a p) n -> p (e a) n", p=P)


def stage_experts(nc, m, t):
    s = m.moe
    h2, ps, ysum = m.h2, m.ps, m.ysum
    sel = s.sb("sel", [P, QT, SLOTS])
    selg = s.sb("selg", [P, QT, 3 * SLOTS])
    selT = s.sb("selT", [P, QT, 2, P])
    now = s.sb("now", [P, SLOTS])
    xs = s.sb("xs", [P, C, SLOTS])
    g = s.sb("g", [P, 512])
    u = s.sb("u", [P, 512])
    sig = s.sb("sig", [P, 512])
    actT = s.sb("actT", [P, 4, P])
    y = s.sb("y", [P, 512])
    stats = s.sb("stats2", [P, 4])
    moe_in = m.moe_in
    X, G, U, TURN, COMB, Y = 0, 1, 2, 3, 4, 7
    w_free, gather_ps, gate_ps, up_ps, down_ps, comb_ps, actT_ps = (
        m.sem(n) for n in ("w_free", "gather_ps", "gate_ps", "up_ps", "down_ps", "comb_ps", "actT_ps"))
    zeroed, sel_ok, now_ok, g_ok, u_ok, act_mul, act_ok, y_added = (
        m.sem(n) for n in ("zeroed2", "sel_ok", "now_ok", "g_ok", "u_ok", "act_mul", "act_ok", "y_added"))
    sig_ok, xs_sb, selT_sb, actT_sb, y_sb = (m.sem(n) for n in ("sig_ok", "xs_sb", "selT_sb", "actT_sb", "y_sb"))
    ysq, ystd, yinv, ymul, x2_done = (m.sem(n) for n in ("ysq", "ystd", "yinv", "ymul", "x2_done"))

    def passes(eng):
        return eng.value_load(m.table[0:1, PASSES:PASSES + 1], min_val=EXPERTS, max_val=EXPERTS + SPARE)

    with nc.Block() as block:

        @block.gpsimd
        def _(pool):
            m.clear_last(pool)
            pool.memset(selg[:], 0.0).then_inc(zeroed, 1)

        @block.sync
        def _(sp):
            with sp.Fori(1, EXPERTS) as e:
                last = sp.value_load(m.table[0:1, bass.ds(e + (PASSES + 1), 1)], min_val=0, max_val=EXPERTS + SPARE)
                for k in range(12):
                    if k < 11:
                        sp.wait_ge(w_free, last * 11 + (k + 1))
                    else:
                        sp.wait_ge(down_ps, last + 1)
                    sp.dma_start(m.ring[:, 2 * k:2 * k + 2, :], expert_rows(t, e, k)).then_inc(moe_in[k], 16)

        @block.tensor
        def _(pe):
            ident = cst(m, "ident")
            n = passes(pe)

            def gather():
                for c in range(C):
                    for i in range(QT):
                        mm = pe.matmul(ps[:, X, c * SLOTS:(c + 1) * SLOTS], h2[:, i, c * P:(c + 1) * P], sel[:, i, :],
                                       start=(i == 0), stop=(i == QT - 1))
                mm.then_inc(gather_ps, 1)

            def expand(bank, part, landed, done):
                for c in range(C):
                    if c % 2 == 0:
                        pe.wait_ge(moe_in[4 * part + c // 2], landed)
                    for half in range(2):
                        mm = pe.matmul(ps[SLOTS * half:SLOTS * (half + 1), bank, :], xs[:, c, :],
                                       m.ring[:, 8 * part + c, half * 512:(half + 1) * 512], start=(c == 0), stop=False)
                    if c % 2 == 1:
                        mm.then_inc(w_free, 1)
                for half in range(2):
                    mm = pe.matmul(ps[SLOTS * half:SLOTS * (half + 1), bank, :], now[:], m.brows[:, part, half * 512:(half + 1) * 512],
                                   start=False, stop=True)
                mm.then_inc(done, 1)

            def combine():
                for i in range(QT):
                    for half in range(2):
                        mm = pe.matmul(ps[:, COMB + 2 * i + half, :], selT[:, i, half, :], y[:], start=True, stop=True)
                    mm.then_inc(comb_ps, 1)

            pe.wait_ge(m.brows_in, 32)
            pe.wait_ge(sel_ok, 1)
            gather()
            with pe.Fori(0, n) as i:
                landed = pe.value_load(m.table[0:1, bass.ds(i, 1)], min_val=0, max_val=EXPERTS - 1) * 16 + 16
                pe.wait_ge(xs_sb, i + 1)
                pe.wait_ge(now_ok, i + 1)
                expand(G, 0, landed, gate_ps)
                pe.wait_ge(y_sb, i + 1)
                pe.wait_ge(selT_sb, i + 1)
                combine()
                expand(U, 1, landed, up_ps)
                pe.wait_ge(sel_ok, i + 2)
                for j in range(QT):
                    for low in range(2):
                        a = SLOTS * (1 - low)
                        pe.transpose(ps[:, TURN, (2 * j + low) * P:(2 * j + low + 1) * P], selg[:, j, a:a + P], ident)
                gather()
                pe.wait_ge(selT_sb, i + 2)
                pe.wait_ge(act_ok, i + 1)
                for b in range(4):
                    mm = pe.transpose(ps[:, TURN, b * P:(b + 1) * P], g[:, b * P:(b + 1) * P], ident)
                mm.then_inc(actT_ps, 1)
                pe.wait_ge(y_added, i * 2 + 2)
                pe.wait_ge(actT_sb, i + 1)
                for f in range(C):
                    if f % 2 == 0:
                        pe.wait_ge(moe_in[8 + f // 2], landed)
                    for half in range(2):
                        mm = pe.matmul(ps[SLOTS * half:SLOTS * (half + 1), Y, :], actT[:, f % 4, f // 4 * SLOTS:(f // 4 + 1) * SLOTS],
                                       m.ring[:, 16 + f, half * 512:(half + 1) * 512], start=(f == 0), stop=(f == C - 1))
                    if f == C - 1:
                        mm.then_inc(down_ps, 1)
                    elif f % 2 == 1:
                        mm.then_inc(w_free, 1)
            pe.wait_ge(y_sb, n + 1)
            combine()

        @block.scalar
        def _(act):
            n = passes(act)
            zero = cst(m, "iota", P, 0, 1).to_broadcast([P, 512])
            act.activation(y[:], zero, ACT.Copy, scale=0.0).then_inc(y_sb, 1)
            act.activation(selT[:].rearrange("p i h n -> p (i h n)"), zero, ACT.Copy, scale=0.0).then_inc(selT_sb, 1)
            act.wait_ge(gather_ps, 1)
            act.copy(xs[:].rearrange("p c n -> p (c n)"), ps[:, X, :]).then_inc(xs_sb, 1)
            with act.Fori(0, n) as i:
                act.wait_ge(g_ok, i + 1)
                act.activation(sig[:], g[:], ACT.Sigmoid, scale=ALPHA).then_inc(sig_ok, 1)
                act.wait_ge(gather_ps, i + 2)
                act.copy(xs[:].rearrange("p c n -> p (c n)"), ps[:, X, :]).then_inc(xs_sb, 1)
                act.copy(selT[:].rearrange("p i h n -> p (i h n)"), ps[:, TURN, :]).then_inc(selT_sb, 1)
                act.wait_ge(actT_ps, i + 1)
                act.copy(actT[:].rearrange("p b n -> p (b n)"), ps[:, TURN, :]).then_inc(actT_sb, 1)
                act.wait_ge(down_ps, i + 1)
                act.copy(y[:], ps[:, Y, :]).then_inc(y_sb, 1)
            for i in range(QT):
                act.wait_ge(y_added, n * 2 + (i + 1))
                if i:
                    act.wait_ge(ysq, i)
                act.activation(h2[:, 0, :], ysum[:, i, :], ACT.Square, accum_out=stats[:, i:i + 1]).then_inc(ysq, 1)
            act.wait_ge(ysq, 2)
            act.activation(stats[:, 2:4], stats[:, 0:2], ACT.Sqrt, scale=1.0 / D, bias=m.eps[:, 0:1]).then_inc(ystd, 1)

        @block.vector
        def _(v):
            n = passes(v)
            iota = cst(m, "iota", P, 0, SLOTS)

            def add(i):
                v.tensor_tensor(ysum[:, i, :], ysum[:, i, :], ps[:, COMB + 2 * i:COMB + 2 * i + 2, :].rearrange("p a n -> p (a n)"),
                                ALU.add).then_inc(y_added, 1)

            for j in range(QT):
                ins = v.tensor_scalar(sel[:, j, :], iota, m.keys[:, j, 0:1], None, ALU.is_equal)
            ins.then_inc(sel_ok, 1)
            v.tensor_copy(now[:], m.pick[:, 0:1].to_broadcast([P, SLOTS])).then_inc(now_ok, 1)
            v.wait_ge(zeroed, 1)
            with v.Fori(0, n) as i:
                v.wait_ge(gather_ps, i + 1)
                for j in range(QT):
                    v.tensor_scalar(selg[:, j, SLOTS:2 * SLOTS], iota, m.keys[:, j, bass.ds(i, 1)], m.gates[:, j, bass.ds(i, 1)],
                                    ALU.is_equal, ALU.mult)
                    ins = v.tensor_scalar(sel[:, j, :], iota, m.keys[:, j, bass.ds(i + 1, 1)], None, ALU.is_equal)
                ins.then_inc(sel_ok, 1)
                v.wait_ge(gate_ps, i + 1)
                v.tensor_scalar(g[:], ps[:, G, :], LIMIT, None, ALU.min).then_inc(g_ok, 1)
                for j in range(QT):
                    v.wait_ge(comb_ps, i * 2 + (j + 1))
                    add(j)
                v.wait_ge(up_ps, i + 1)
                v.tensor_scalar(u[:], ps[:, U, :], -LIMIT, LIMIT, ALU.max, ALU.min).then_inc(u_ok, 1)
                v.tensor_copy(now[:], m.pick[:, bass.ds(i + 1, 1)].to_broadcast([P, SLOTS])).then_inc(now_ok, 1)
                v.wait_ge(u_ok, i + 1)
                v.scalar_tensor_tensor(u[:], u[:], 1.0, g[:], ALU.add, ALU.mult).then_inc(act_mul, 1)
                v.wait_ge(act_mul, i + 1)
                v.wait_ge(sig_ok, i + 1)
                v.tensor_tensor(g[:], u[:], sig[:], ALU.mult).then_inc(act_ok, 1)
            for j in range(QT):
                v.wait_ge(comb_ps, n * 2 + (j + 1))
                add(j)
            v.wait_ge(ystd, 1)
            v.reciprocal(stats[:, 2:4], stats[:, 2:4]).then_inc(yinv, 1)
            v.wait_ge(yinv, 1)
            for i in range(QT):
                v.scalar_tensor_tensor(ysum[:, i, :], ysum[:, i, :], stats[:, 2 + i:3 + i], m.r_g2[:], ALU.mult, ALU.mult).then_inc(ymul, 1)
                v.wait_ge(ymul, i + 1)
                v.tensor_tensor(m.x[:, i, :], m.x[:, i, :], ysum[:, i, :], ALU.add).then_inc(x2_done, 1)
    s.stack.close()


class Norm:

    def __init__(self, m, mem, name, eps, weight):
        self.m, self.eps, self.weight = m, eps, weight
        self.xn = mem.sb(f"{name}_xn", [P, QT, D])
        self.stats = mem.sb(f"{name}_st", [P, 2 * QT])
        self.sq, self.std, self.inv, self.ready, self.ps, self.hT_a, self.hT_v = (
            m.sem(f"{name}_{n}") for n in ("sq", "std", "inv", "ready", "ps", "hT_a", "hT_v"))

    def scalar_stats(self, act):
        for i in range(QT):
            act.activation(self.xn[:, i, :], self.m.x[:, i, :], ACT.Square, accum_out=self.stats[:, i:i + 1]).then_inc(self.sq, 1)
        act.wait_ge(self.sq, QT)
        act.activation(self.stats[:, QT:2 * QT], self.stats[:, 0:QT], ACT.Sqrt, scale=1.0 / D,
                       bias=self.m.eps[:, self.eps:self.eps + 1]).then_inc(self.std, 1)

    def vector_scale(self, v):
        v.wait_ge(self.std, 1)
        v.reciprocal(self.stats[:, QT:2 * QT], self.stats[:, QT:2 * QT]).then_inc(self.inv, 1)
        v.wait_ge(self.inv, 1)
        for i in range(QT):
            v.tensor_scalar(self.xn[:, i, :], self.m.x[:, i, :], self.stats[:, QT + i:QT + i + 1], None, ALU.mult).then_inc(self.ready, 1)

    def tensor_turn(self, pe):
        for i in range(QT):
            pe.wait_ge(self.ready, i + 1)
            for c in range(C):
                mm = pe.transpose(self.m.ps[:, c // 2, (c % 2) * SEQ + i * P:(c % 2) * SEQ + (i + 1) * P],
                                  self.xn[:, i, c * P:(c + 1) * P], cst(self.m, "ident"))
        mm.then_inc(self.ps, 1)

    def _tile(self, c):
        return self.m.hT[:, c, :], self.m.ps[:, c // 2, (c % 2) * SEQ:(c % 2 + 1) * SEQ], col(self.m, self.weight[0], self.weight[1] + c)

    def scalar_weigh(self, act):
        act.wait_ge(self.ps, 1)
        for c in range(0, C, 4):
            for d in (0, 1):
                out, src, w = self._tile(c + d)
                act.activation(out, src, ACT.Copy, scale=w).then_inc(self.hT_a, 1)

    def vector_weigh(self, v):
        v.wait_ge(self.ps, 1)
        for c in range(2, C, 4):
            for d in (0, 1):
                out, src, w = self._tile(c + d)
                v.tensor_scalar(out, src, w, None, ALU.mult).then_inc(self.hT_v, 1)

    def wait_turned(self, eng):
        eng.wait_ge(self.hT_a, 4)
        eng.wait_ge(self.hT_v, 4)


def stage_even_project(nc, m, t):
    s = m.even = Memory(nc)
    m.mqT, m.mkT, m.nqT = (s.sb(n, [P, 4, SEQ]) for n in ("mqT", "mkT", "nqT"))
    m.mv = s.sb("mv", [P, QT, 512])
    m.kcT, m.vcT, m.kslT, m.kwnT = (s.sb(n, [P, 2, SEQ]) for n in ("kcT", "vcT", "kslT", "kwnT"))
    m.nv = s.sb("nv", [P, QT, 280])
    r = Memory(nc)
    wv = r.sb("wv", [P, C, 280])
    norm = Norm(m, r, "n0", 1, ("mix", 0))
    W = m.ring[:].rearrange("p a n -> p (a n)").rearrange("p (c n) -> p c n", c=C)
    ps = m.ps
    w_in = [m.sem(f"even_in{k}") for k in range(6)]
    proj_ps, sb_a = m.sem("even_ps"), m.sem("even_sb")
    tiles = [(128 * j, m.mqT[:, j, :], HD ** -0.5) for j in range(4)]
    tiles += [(512 + 128 * j, m.mkT[:, j, :], 1.0) for j in range(4)]
    tiles += [(1536 + 128 * j, m.nqT[:, j, :], HD ** -0.5) for j in range(4)]
    shared = [(2048 + 128 * (2 * k + g), dst, g) for k, dst in enumerate((m.kcT, m.vcT, m.kslT, m.kwnT)) for g in range(2)]
    tiles += [(at, dst[:, g, :], None) for at, dst, g in shared]

    with nc.Block() as block:

        @block.gpsimd
        def _(pool):
            m.clear_last(pool)

        @block.sync
        def _(sp):
            src = stack(t["even_w_in_2"][0])
            for k, (a, lo, n) in enumerate(((0, MQ, 512), (512, MK, 512), (1536, NQ, 512), (1024, MV, 512))):
                sp.dma_start(W[:, :, a:a + n], src[:, :, lo:lo + n]).then_inc(w_in[k], 16)
            for k, lo in enumerate((KC, VC, KSL, KWN)):
                for g in range(2):
                    for twice in range(2):
                        a = 2048 + 128 * (2 * k + g) + HD * twice
                        sp.dma_start(W[:, :, a:a + HD], src[:, :, lo + HD * g:lo + HD * (g + 1)]).then_inc(w_in[4], 16)
            for a, lo, n in ((0, VSL, 128), (128, VWN, 128), (256, GZ, 24)):
                sp.dma_start(wv[:, :, a:a + n], src[:, :, lo:lo + n]).then_inc(w_in[5], 16)

        @block.tensor
        def _(pe):
            norm.tensor_turn(pe)
            norm.wait_turned(pe)
            landed = {0: (0, 16), 4: (1, 16), 8: (2, 16), 12: (4, 256)}
            for n, (at, _, _) in enumerate(tiles):
                if n in landed:
                    pe.wait_ge(w_in[landed[n][0]], landed[n][1])
                if n >= 8:
                    pe.wait_ge(sb_a, n - 7)
                for c in range(C):
                    mm = pe.matmul(ps[:, n % 8, 0:SEQ], W[:, c, at:at + P], m.hT[:, c, :], start=(c == 0), stop=(c == C - 1))
                mm.then_inc(proj_ps, 1)
            pe.wait_ge(w_in[3], 16)
            pe.wait_ge(w_in[5], 48)
            for k in range(4):
                i = k % 2
                pe.wait_ge(sb_a, len(tiles) - 8 + k + 1)
                b = (len(tiles) + k) % 8
                for c in range(C):
                    w = W[:, c, 1024:1536] if k < 2 else wv[:, c, :]
                    mm = pe.matmul(ps[:, b, 0:w.shape[1]], m.hT[:, c, i * P:(i + 1) * P], w, start=(c == 0), stop=(c == C - 1))
                mm.then_inc(proj_ps, 1)

        @block.scalar
        def _(act):
            norm.scalar_stats(act)
            norm.scalar_weigh(act)
            for n, (_, dst, scale) in enumerate(tiles):
                act.wait_ge(proj_ps, n + 1)
                b = n % 8
                if n in (12, 13, 14, 15):
                    act.copy(dst[0:HD], ps[0:HD, b, 0:SEQ])
                    act.copy(dst[HD:P, 0:SEQ - 1], ps[HD:P, b, 1:SEQ]).then_inc(sb_a, 1)
                elif scale is None or scale == 1.0:
                    act.copy(dst, ps[:, b, 0:SEQ]).then_inc(sb_a, 1)
                else:
                    act.mul(dst, ps[:, b, 0:SEQ], scale).then_inc(sb_a, 1)
            for k in range(4):
                act.wait_ge(proj_ps, len(tiles) + k + 1)
                b = (len(tiles) + k) % 8
                dst = m.mv[:, k, :] if k < 2 else m.nv[:, k - 2, :]
                act.copy(dst, ps[:, b, 0:dst.shape[1]]).then_inc(sb_a, 1)

        @block.vector
        def _(v):
            norm.vector_scale(v)
            norm.vector_weigh(v)
    r.stack.close()


class Unit:

    def __init__(self, scores, bias, values, keys, gate, first, last, out):
        self.scores, self.bias, self.values, self.keys = scores, bias, values, keys
        self.gate, self.first, self.last, self.out = gate, first, last, out


class Attention:

    def __init__(self, m, mem, name, units):
        self.m, self.units = m, units
        self.prob = mem.sb(f"{name}_prob", [P, 2, 4 * SEQ])
        self.probT = mem.sb(f"{name}_probT", [P, 4 * SEQ])
        self.top = mem.sb(f"{name}_top", [P, len(units), 8])
        (self.s_ps, self.biased, self.peak, self.neg, self.exped, self.inv, self.gated, self.ready, self.pt_ps, self.pt_sb,
         self.pv_ps, self.pv_sb) = (m.sem(f"{name}_{n}") for n in (
             "s_ps", "biased", "peak", "neg", "exped", "inv", "gated", "ready", "pt_ps", "pt_sb", "pv_ps", "pv_sb"))
        self.pair, n = [], 0
        for u in units:
            self.pair.append(n)
            n += u.last

    def scores_of(self, u):
        K, b = self.units[u].keys, 2 * (u % 2)
        return self.m.ps[:, b:b + 2, 0:QT * K].rearrange("p h (i n) -> p h i n", i=QT)

    def prob_of(self, u):
        return self.prob[:, u % 2, 0:4 * self.units[u].keys].rearrange("p (h i n) -> p h i n", h=2, i=QT)

    def tensor(self, pe):
        ps, ident = self.m.ps, cst(self.m, "ident")

        def scores(u):
            if u >= 2:
                pe.wait_ge(self.biased, u - 1)
            unit, S = self.units[u], self.scores_of(u)
            for hd in range(2):
                for i in range(QT):
                    mm = unit.scores(pe, S[:, hd, i, :], hd, i)
            mm.then_inc(self.s_ps, 1)

        for u in range(min(2, len(self.units))):
            scores(u)
        for u, unit in enumerate(self.units):
            K, prob = unit.keys, self.prob_of(u)
            pe.wait_ge(self.ready, u + 1)
            if u:
                pe.wait_ge(self.pt_sb, u)
            if K == SEQ:
                for k in range(2):
                    for j in range(4):
                        mm = pe.transpose(ps[:, 4 + k, j * P:(j + 1) * P], prob[:, j // 2, j % 2, k * P:(k + 1) * P], ident)
            else:
                for j in range(4):
                    mm = pe.transpose(ps[0:K, 4, j * P:(j + 1) * P], prob[:, j // 2, j % 2, :], ident)
            mm.then_inc(self.pt_ps, 1)
            if u + 2 < len(self.units):
                scores(u + 2)
            pe.wait_ge(self.pt_sb, u + 1)
            n = self.pair[u]
            if unit.first and n >= 2:
                pe.wait_ge(self.pv_sb, n - 1)
            for hd in range(2):
                for k in range(max(1, K // P)):
                    rows = min(K, P)
                    mm = pe.matmul(ps[HD * hd:HD * (hd + 1), 6 + n % 2, 0:SEQ], unit.values(hd, k),
                                   self.probT[0:rows, k * 512 + hd * SEQ:k * 512 + (hd + 1) * SEQ],
                                   start=(unit.first and k == 0), stop=(unit.last and k == max(1, K // P) - 1))
            mm.then_inc(self.pv_ps, 1)

    def scalar(self, act):
        ps = self.m.ps

        def exp(u):
            act.wait_ge(self.neg, u + 1)
            for j in range(4):
                ins = act.activation(self.prob_of(u)[:, j // 2, j % 2, :], self.prob_of(u)[:, j // 2, j % 2, :], ACT.Exp, bias=self.top[:, u, j:j + 1],
                                     accum_out=self.top[:, u, 4 + j:5 + j])
            ins.then_inc(self.exped, 1)

        exp(0)
        for u, unit in enumerate(self.units):
            if u + 1 < len(self.units):
                exp(u + 1)
            act.wait_ge(self.pt_ps, u + 1)
            if u:
                act.wait_ge(self.pv_ps, u)
            if unit.keys == SEQ:
                act.copy(self.probT[:], ps[:, 4:6, :].rearrange("p a n -> p (a n)")).then_inc(self.pt_sb, 1)
            else:
                act.copy(self.probT[0:unit.keys, 0:512], ps[0:unit.keys, 4, :]).then_inc(self.pt_sb, 1)
            if unit.last:
                act.wait_ge(self.pv_ps, u + 1)
                act.copy(unit.out, ps[:, 6 + self.pair[u] % 2, 0:SEQ]).then_inc(self.pv_sb, 1)

    def vector(self, v):
        def peak(u):
            v.wait_ge(self.s_ps, u + 1)
            if u >= 2:
                v.wait_ge(self.pt_ps, u - 1)
            self.units[u].bias(v, self.prob_of(u), self.scores_of(u)).then_inc(self.biased, 1)
            v.wait_ge(self.biased, u + 1)
            v.tensor_reduce(self.top[:, u, 0:4].rearrange("p (h i) -> p h i", h=2), self.prob_of(u), AX, ALU.max).then_inc(self.peak, 1)
            v.wait_ge(self.peak, u + 1)
            v.tensor_scalar(self.top[:, u, 0:4], self.top[:, u, 0:4], -1.0, None, ALU.mult).then_inc(self.neg, 1)

        gated = 0
        peak(0)
        for u, unit in enumerate(self.units):
            if u + 1 < len(self.units):
                peak(u + 1)
            v.wait_ge(self.exped, u + 1)
            v.reciprocal(self.top[:, u, 4:8], self.top[:, u, 4:8]).then_inc(self.inv, 1)
            v.wait_ge(self.inv, u + 1)
            if unit.gate is not None:
                r = self.top[:, u, 4:8].rearrange("p (h i) -> p h i", h=2)
                v.tensor_tensor(r, r, unit.gate, ALU.mult).then_inc(self.gated, 1)
                gated += 1
                v.wait_ge(self.gated, gated)
            p = self.prob[:, u % 2, 0:4 * unit.keys].rearrange("p (j n) -> p j n", j=4)
            v.tensor_tensor(p, p, spread(self.top[:, u, 4:8], unit.keys), ALU.mult).then_inc(self.ready, 1)


def stage_even_attend(nc, m, t):
    s = Memory(nc)
    cmp_w1 = m.ring[:, 8:16, :].rearrange("p a n -> p (a n)").rearrange("p (s j n) -> p s j n", s=2, j=16)
    toe = m.ring[:, 0:8, :].rearrange("p a n -> p (a n)").rearrange("p (h i n) -> p h i n", h=16, i=QT)
    pos = s.sb("pos", [P, 2, 16])
    w2k = s.sb("w2k", [P, 2, P])
    w2v = s.sb("w2v", [P, 2, HD])
    tab = s.sb("tab2", [BUCKETS, 16])
    fwd = s.sb("fwd", [BUCKETS, 512])
    blocks = s.sb("blocks", [P, 2, 16, 2 * NCMP])
    hid = s.sb("hid", [P, 2, 2, 2 * NCMP])
    kcmpT = s.sb("kcmpT", [P, 2 * NCMP])
    vcmp = s.sb("vcmp", [NCMP, 2, HD])
    cmpb = s.sb("cmpb", [P, 8, QT * NCMP])
    gates = s.sb("gates_sb", [P, QT, 24])
    ps = m.ps
    small_in, toe_in, w1_in = m.sem("small_in"), m.sem("toe_in"), m.sem("w1_in")
    m.eout_in = m.lasting("eout_in")
    blocks_ok, hid_ps, hid_ok, cmp_ps, cmp_sb, cb_ps, cb_ok, gz_ok, gz_valid = (
        m.sem(n) for n in ("blocks_ok", "hid_ps", "hid_ok", "cmp_ps", "cmp_sb", "cb_ps", "cb_ok", "gz_ok", "gz_valid"))

    def unit(q, k, group_keys, values, keys, bias, gate, first, last, out):
        def scores(pe, S, hd, i):
            r = slice(HD * hd, HD * (hd + 1))
            return pe.matmul(S, q[r, i * P:(i + 1) * P], k[r, :], start=True, stop=True)

        def add_bias(v, prob, S):
            return v.tensor_tensor(prob, S, bias, ALU.add)
        return Unit(scores=scores, values=values, keys=keys, bias=add_bias, gate=gate, first=first, last=last, out=out)

    units = []
    for p in range(4):
        units.append(unit(m.mqT[:, p, :], m.mkT[:, p, :], None, lambda hd, k, p=p: m.mv[:, k, (2 * p + hd) * HD:(2 * p + hd + 1) * HD],
                          SEQ, toe[:, 2 * p:2 * p + 2, :, :], None, True, True, m.hT[:, p, :]))
    for p in range(4):
        g = p // 2
        gz = [gates[:, :, 6 * p + b:6 * p + b + 4:3].rearrange("p i h -> p h i") for b in range(3)]
        bias = toe[:, 8 + 2 * p:10 + 2 * p, :, :]
        units.append(unit(m.nqT[:, p, :], m.kslT[:, g, :], g, lambda hd, k, g=g: m.nv[:, k, g * HD:(g + 1) * HD],
                          SEQ, bias, gz[1], True, False, None))
        units.append(unit(m.nqT[:, p, :], m.kwnT[:, g, :], g, lambda hd, k, g=g: m.nv[:, k, 128 + g * HD:128 + (g + 1) * HD],
                          SEQ, bias, gz[2], False, False, None))
        units.append(unit(m.nqT[:, p, :], kcmpT[:, g * NCMP:(g + 1) * NCMP], g, lambda hd, k, g=g: vcmp[:, g, :],
                          NCMP, cmpb[:, 2 * p:2 * p + 2, :].rearrange("p h (i n) -> p h i n", i=QT), gz[0], False, True, m.hT[:, 4 + p, :]))
    attn = Attention(m, s, "ev", units)

    with nc.Block() as block:

        @block.gpsimd
        def _(pool):
            m.clear_last(pool)

        @block.sync
        def _(sp):
            with nc.allow_non_contiguous_dma(reason="small columns"):
                for j, name in enumerate(("cmp_pos_k_2", "cmp_pos_v_2")):
                    flat = bass.AP(t[name].tensor, 0, [[1, P], [P, 16]])
                    sp.dma_start(pos[:, j, :], flat).then_inc(small_in, 16)
            for twice in range(2):
                sp.dma_start(w2k[:, :, HD * twice:HD * (twice + 1)], stack(t["cmp_k_w2_2"][0])).then_inc(small_in, 16)
            sp.dma_start(w2v[:], stack(t["cmp_v_w2_2"][0])).then_inc(small_in, 16)
            sp.dma_start(tab[:], t["rel_bias_2"]).then_inc(small_in, 16)
            sp.dma_start(fwd[:], t["buckets"][:, 0, :]).then_inc(small_in, 16)
            for j, name in enumerate(("cmp_k_w1_2", "cmp_v_w1_2")):
                sp.dma_start(cmp_w1[:, j, :, :], stack(t[name][0])).then_inc(w1_in, 16)
            sp.wait_ge(m.toeplitz_out, 16)
            for i in range(QT):
                src = bass.AP(t["toeplitz"].tensor, SEQ - 1 - P * i, [[510, P], [P * 512, 16], [1, SEQ]])
                sp.dma_start(toe[:, :, i, :], src).then_inc(toe_in, 16)
            sp.dma_start(m.ring[:, 16:24, :], stack(t["even_w_out_2"][0])).then_inc(m.eout_in, 16)

        @block.tensor
        def _(pe):
            pe.wait_ge(small_in, 112)
            for i in range(QT):
                for n in range(NCMP):
                    a = 256 - (CMP_BLOCK - 1) - CMP_STRIDE * n + P * i
                    mm = pe.matmul(ps[:, 0, (i * NCMP + n) * 8:(i * NCMP + n + 1) * 8], fwd[:, a:a + P], tab[:, 8:16], start=True, stop=True)
            mm.then_inc(cb_ps, 1)
            pe.wait_ge(w1_in, 32)
            for j in range(2):
                pe.wait_ge(blocks_ok, j + 1)
                for h in range(2):
                    for k in range(16):
                        mm = pe.matmul(ps[:, 1, (2 * j + h) * 32:(2 * j + h) * 32 + 30], cmp_w1[:, j, k, h * P:(h + 1) * P], blocks[:, j, k, :],
                                       start=(k == 0), stop=(k == 15))
            mm.then_inc(hid_ps, 1)
            pe.wait_ge(hid_ok, 1)
            for h in range(2):
                pe.matmul(ps[:, 2, 0:2 * NCMP], w2k[:, h, :], hid[:, 0, h, :], start=(h == 0), stop=(h == 1))
            for g in range(2):
                for h in range(2):
                    mm = pe.matmul(ps[0:NCMP, 3, g * HD:(g + 1) * HD], hid[:, 1, h, g * NCMP:(g + 1) * NCMP], w2v[:, h, :],
                                   start=(h == 0), stop=(h == 1))
            mm.then_inc(cmp_ps, 1)
            pe.wait_ge(cmp_sb, 2)
            pe.wait_ge(cb_ok, 1)
            attn.tensor(pe)

        @block.scalar
        def _(act):
            act.activation(gates[:], m.nv[:, :, 256:280], ACT.Sigmoid).then_inc(gz_ok, 1)
            act.wait_ge(hid_ps, 1)
            src = ps[:, 1, 0:128].rearrange("p (a b n) -> p a b n", a=2, b=2)[:, :, :, 0:2 * NCMP]
            act.activation(hid[:], src, ACT.Silu).then_inc(hid_ok, 1)
            act.wait_ge(cmp_ps, 1)
            act.copy(kcmpT[:], ps[:, 2, 0:2 * NCMP]).then_inc(cmp_sb, 1)
            act.copy(vcmp[:].rearrange("n g d -> n (g d)"), ps[0:NCMP, 3, 0:2 * HD]).then_inc(cmp_sb, 1)
            attn.scalar(act)

        @block.vector
        def _(v):
            v.wait_ge(small_in, 112)
            for j, src in enumerate((m.kcT, m.vcT)):
                for g in range(2):
                    for half in range(2):
                        tok = src[:, g, 16 * half:16 * half + 240].rearrange("p (n k) -> p k n", k=16)[:, 0:16:2, :]
                        ins = v.tensor_tensor(blocks[:, j, 8 * half:8 * half + 8, g * NCMP:(g + 1) * NCMP], tok,
                                              spread(pos[:, j, 8 * half:8 * half + 8], NCMP), ALU.add)
                ins.then_inc(blocks_ok, 1)
            v.wait_ge(cb_ps, 1)
            v.tensor_tensor(cmpb[:].rearrange("p h a -> p a h"), ps[:, 0, 0:240].rearrange("p (a h) -> p a h", h=8),
                            spread(cst(m, "cmpmask"), 8), ALU.add).then_inc(cb_ok, 1)
            v.wait_ge(gz_ok, 1)
            for i in range(QT):
                g3 = gates[:, i, 0:24:3]
                ins = v.tensor_scalar(g3, g3, cst(m, "cmpvalid", P, i, 1), None, ALU.mult)
            ins.then_inc(gz_valid, 1)
            v.wait_ge(gz_valid, 1)
            v.wait_ge(cb_ok, 1)
            v.wait_ge(toe_in, 32)
            attn.vector(v)
    s.stack.close()
    m.even.stack.close()


def stage_mlp(nc, m, t, layer, w_out_in, w_out_value):
    s = Memory(nc)
    name = f"p{layer}"
    norm = Norm(m, s, name, 1, ("mlp", 8 * layer))
    pos = s.sb(f"{name}_pos", [P, 2, 4, SEQ])
    sq = s.sb(f"{name}_sqr", [P, 2, 4, SEQ])
    GROUPS = DFF2 // 512
    ps = m.ps
    out_ps, added, x_ps, up_ps, down_ps, relu_ok, sq_ok, x_done = (
        m.sem(f"{name}_{n}") for n in ("out_ps", "added", "x_ps", "up_ps", "down_ps", "relu_ok", "sq_ok", "x_done"))
    w1_in = [m.sem(f"{name}_w1_in{b}") for b in range(2)]
    w2_in = [m.sem(f"{name}_w2_in{b}") for b in range(2)]
    w1 = [m.ring[:, 8 * b:8 * b + 4, :].rearrange("p a n -> p (a n)").rearrange("p (c n) -> p c n", c=C) for b in range(2)]
    w2 = [m.ring[:, 8 * b + 4:8 * b + 8, :] for b in range(2)]
    W1, W2 = stack(t["mlp_w1_2"][layer]), t["mlp_w2_2"][layer].rearrange("(g c p) n -> g p c n", p=P, c=4)

    with nc.Block() as block:

        @block.gpsimd
        def _(pool):
            m.clear_last(pool)

        @block.sync
        def _(sp):
            for b in range(2):
                sp.dma_start(w1[b], W1[:, :, b * 512:(b + 1) * 512]).then_inc(w1_in[b], 16)
                sp.dma_start(w2[b], W2[b]).then_inc(w2_in[b], 16)
            with sp.Fori(1, GROUPS // 2) as i:
                for b in range(2):
                    sp.wait_ge(up_ps, i * 2 + (b - 1))
                    sp.dma_start(w1[b], W1[:, :, bass.ds(i * 1024 + b * 512, 512)]).then_inc(w1_in[b], 16)
                    sp.wait_ge(down_ps, i * 2 + (b - 1))
                    sp.dma_start(w2[b], W2[bass.ds(i * 2 + b, 1)].rearrange("g p c n -> p (g c) n")).then_inc(w2_in[b], 16)

        @block.tensor
        def _(pe):
            pe.wait_ge(w_out_in, w_out_value)
            for i in range(QT):
                for half in range(2):
                    for c in range(C):
                        mm = pe.matmul(ps[:, 4 + 2 * i + half, :], m.hT[:, c, i * P:(i + 1) * P], m.ring[:, 16 + c, half * 512:(half + 1) * 512],
                                       start=(c == 0), stop=(c == C - 1))
                mm.then_inc(out_ps, 1)
            norm.tensor_turn(pe)
            norm.wait_turned(pe)

            def up(b, g):
                pe.wait_ge(w1_in[b], g * 8 + (16 - 8 * b))
                for f in range(4):
                    for c in range(C):
                        mm = pe.matmul(ps[:, 4 + 2 * b + f // 2, (f % 2) * SEQ:(f % 2 + 1) * SEQ], w1[b][:, c, f * P:(f + 1) * P], m.hT[:, c, :],
                                       start=(c == 0), stop=(c == C - 1))
                mm.then_inc(up_ps, 1)

            def down(b, g, last=False):
                pe.wait_ge(w2_in[b], g * 8 + (16 - 8 * b))
                pe.wait_ge(sq_ok, g + 1)
                for f in range(4):
                    for i in range(QT):
                        for half in range(2):
                            mm = pe.matmul(ps[:, 2 * i + half, :], sq[:, b, f, i * P:(i + 1) * P], w2[b][:, f, half * 512:(half + 1) * 512],
                                           start=False, stop=last, skip_group_check=True)
                mm.then_inc(down_ps, 1)

            up(0, 0)
            for i in range(QT):
                for half in range(2):
                    pe.matmul(ps[:, 2 * i + half, :], cst(m, "ident"), m.x[:, i, half * 512:(half + 1) * 512],
                              start=True, stop=False, skip_group_check=True)
            with pe.Fori(0, GROUPS // 2 - 1) as i:
                pe.wait_ge(relu_ok, i * 2 + 1)
                up(1, i * 2 + 1)
                down(0, i * 2)
                pe.wait_ge(relu_ok, i * 2 + 1)
                up(0, i * 2 + 2)
                down(1, i * 2 + 1)
            up(1, GROUPS - 1)
            down(0, GROUPS - 2)
            down(1, GROUPS - 1, last=True)

        @block.scalar
        def _(act):
            act.wait_ge(added, 2)
            norm.scalar_stats(act)
            norm.scalar_weigh(act)

            def relu(b, g, wait_sq):
                act.wait_ge(up_ps, g + 1)
                if wait_sq is not None:
                    act.wait_ge(sq_ok, wait_sq)
                act.activation(pos[:, b, :, :].rearrange("p f n -> p (f n)"), ps[:, 4 + 2 * b:6 + 2 * b, :].rearrange("p a n -> p (a n)"),
                               ACT.Relu).then_inc(relu_ok, 1)

            relu(0, 0, None)
            relu(1, 1, None)
            with act.Fori(1, GROUPS // 2) as i:
                for b in range(2):
                    relu(b, i * 2 + b, i * 2 + b - 1)

        @block.vector
        def _(v):
            for i in range(QT):
                v.wait_ge(out_ps, i + 1)
                v.tensor_tensor(m.x[:, i, :], m.x[:, i, :], ps[:, 4 + 2 * i:6 + 2 * i, :].rearrange("p a n -> p (a n)"), ALU.add).then_inc(added, 1)
            v.wait_ge(added, 2)
            norm.vector_scale(v)
            norm.vector_weigh(v)

            def square(b, g, wait_down):
                v.wait_ge(relu_ok, g + 1)
                if wait_down is not None:
                    v.wait_ge(down_ps, wait_down)
                v.tensor_tensor(sq[:, b, :, :], pos[:, b, :, :], pos[:, b, :, :], ALU.mult).then_inc(sq_ok, 1)

            square(0, 0, None)
            square(1, 1, None)
            with v.Fori(1, GROUPS // 2) as i:
                for b in range(2):
                    square(b, i * 2 + b, i * 2 + b - 1)
            v.wait_ge(down_ps, GROUPS)
            v.tensor_copy(m.x[:].rearrange("p i n -> p (i n)"), ps[:, 0:4, :].rearrange("p a n -> p (a n)")).then_inc(x_done, 1)
    s.stack.close()


def stage_mlp0(nc, m, t):
    stage_mlp(nc, m, t, 0, m.eout_in, 16)


def stage_odd_project(nc, m, t):
    s = m.odd = Memory(nc)
    m.fqT, m.fkT = (s.sb(n, [P, 8, SEQ]) for n in ("fqT", "fkT"))
    m.fv = s.sb("fv", [P, QT, D])
    m.cumq = s.sb("cumq", [P, QT, 16])
    m.ncumT = s.sb("ncumT", [P, SEQ])
    r = Memory(nc)
    wf = r.sb("wforget", [P, C, 16])
    bf = r.sb("bforget", [P, 16])
    z = r.sb("z", [P, QT, 16])
    e = r.sb("e", [P, QT, 16])
    lf = r.sb("lf", [P, QT, 16])
    norm = Norm(m, r, "n1", 1, ("mix", 8))
    W = m.ring[:].rearrange("p a n -> p (a n)").rearrange("p (c n) -> p c n", c=C)
    ps = m.ps
    w_in = [m.sem(f"odd_in{k}") for k in range(6)]
    f_in, proj_ps, proj_sb, fz_ps, chain, e_ok, cum_ps, cum_ok = (
        m.sem(n) for n in ("f_in", "odd_ps", "odd_sb", "fz_ps", "fz_chain", "e_ok", "cum_ps", "cum_ok"))
    tiles = [(P * j, m.fqT[:, j, :], HD ** -0.5) for j in range(8)] + [(D + P * j, m.fkT[:, j, :], 1.0) for j in range(8)]

    with nc.Block() as block:

        @block.gpsimd
        def _(pool):
            m.clear_last(pool)

        @block.sync
        def _(sp):
            src = stack(t["odd_w_in_2"][0])
            for k in range(6):
                sp.dma_start(W[:, :, 512 * k:512 * (k + 1)], src[:, :, 512 * k:512 * (k + 1)]).then_inc(w_in[k], 16)
                if k == 0:
                    sp.dma_start(wf[:], src[:, :, 3 * D:]).then_inc(f_in, 16)
                    sp.dma_start(bf[:], bcast_row(t["odd_b_forget_2"], 16)).then_inc(f_in, 16)

        @block.tensor
        def _(pe):
            norm.tensor_turn(pe)
            norm.wait_turned(pe)
            pe.wait_ge(f_in, 32)
            for i in range(QT):
                for c in range(C):
                    mm = pe.matmul(ps[:, 7, i * 16:(i + 1) * 16], m.hT[:, c, i * P:(i + 1) * P], wf[:, c, :], start=(c == 0), stop=(c == C - 1))
            mm.then_inc(fz_ps, 1)
            for n, (at, _, _) in enumerate(tiles):
                if n % 4 == 0:
                    pe.wait_ge(w_in[n // 4], 16)
                if n >= 6:
                    pe.wait_ge(proj_sb, n - 5)
                for c in range(C):
                    mm = pe.matmul(ps[:, n % 6, 0:SEQ], W[:, c, at:at + P], m.hT[:, c, :], start=(c == 0), stop=(c == C - 1))
                mm.then_inc(proj_ps, 1)
                if n == 2:
                    pe.wait_ge(chain, 3)
                    for i in range(QT):
                        for j in range(QT):
                            pe.matmul(ps[:, 6, i * 16:(i + 1) * 16], cst(m, "tri", P, j * SEQ + i * P, P), lf[:, j, :],
                                      start=(j == 0), stop=(j == QT - 1))
                    for a in (0, 64):
                        for j in range(QT):
                            mm = pe.matmul(ps[a:a + 16, 7, 0:SEQ], lf[:, j, :], cst(m, "tri", P, j * SEQ, SEQ),
                                           start=(j == 0), stop=(j == QT - 1))
                    mm.then_inc(cum_ps, 1)
            n = len(tiles)
            for half in range(2):
                pe.wait_ge(w_in[4 + half], 16)
                for i in range(QT):
                    pe.wait_ge(proj_sb, n - 5)
                    for c in range(C):
                        mm = pe.matmul(ps[:, n % 6, :], m.hT[:, c, i * P:(i + 1) * P], W[:, c, 2 * D + 512 * half:2 * D + 512 * (half + 1)],
                                       start=(c == 0), stop=(c == C - 1))
                    mm.then_inc(proj_ps, 1)
                    n += 1

        @block.scalar
        def _(act):
            norm.scalar_stats(act)
            norm.scalar_weigh(act)
            act.wait_ge(chain, 2)
            act.activation(e[:], e[:], ACT.Exp, scale=-1.0).then_inc(e_ok, 1)
            act.wait_ge(e_ok, 1)
            act.activation(e[:], e[:], ACT.Ln, bias=m.one[:, 0:1]).then_inc(e_ok, 1)
            for n, (_, dst, scale) in enumerate(tiles):
                act.wait_ge(proj_ps, n + 1)
                act.mul(dst, ps[:, n % 6, 0:SEQ], scale).then_inc(proj_sb, 1)
            n = len(tiles)
            for half in range(2):
                for i in range(QT):
                    act.wait_ge(proj_ps, n + 1)
                    act.copy(m.fv[:, i, 512 * half:512 * (half + 1)], ps[:, n % 6, :]).then_inc(proj_sb, 1)
                    n += 1

        @block.vector
        def _(v):
            norm.vector_scale(v)
            norm.vector_weigh(v)
            v.wait_ge(f_in, 32)
            v.wait_ge(fz_ps, 1)
            v.memset(m.one[:], 1.0)
            v.tensor_tensor(z[:], ps[:, 7, 0:32].rearrange("p (i h) -> p i h", i=QT),
                            bf[:].rearrange("p (a h) -> p a h", a=1).to_broadcast([P, QT, 16]), ALU.add).then_inc(chain, 1)
            v.wait_ge(chain, 1)
            v.scalar_tensor_tensor(e[:], z[:], -1.0, z[:], ALU.mult, ALU.max).then_inc(chain, 1)
            v.wait_ge(e_ok, 2)
            v.scalar_tensor_tensor(lf[:], z[:], 0.0, e[:], ALU.min, ALU.subtract).then_inc(chain, 1)
            v.wait_ge(cum_ps, 1)
            v.tensor_copy(m.cumq[:].rearrange("p i h -> p (i h)"), ps[:, 6, 0:32])
            for a in (0, 64):
                ins = v.tensor_scalar(m.ncumT[a:a + 16, :], ps[a:a + 16, 7, 0:SEQ], -1.0, None, ALU.mult)
            ins.then_inc(cum_ok, 1)
    r.stack.close()


def stage_odd_attend(nc, m, t):
    s = Memory(nc)
    m.oout_in = m.lasting("oout_in")

    def unit(p):
        def scores(pe, S, hd, i):
            r, a, h = slice(HD * hd, HD * (hd + 1)), 64 * hd, 2 * p + hd
            pe.matmul(S, m.fqT[r, p, i * P:(i + 1) * P], m.fkT[r, p, :], start=True, stop=False)
            one = cst(m, "ident", P, a + h, 1)[a:a + 16].to_broadcast([16, P])
            return pe.matmul(S, one, m.ncumT[a:a + 16, :], start=False, stop=True)

        def bias(v, prob, S):
            for hd in range(2):
                for i in range(QT):
                    h = 2 * p + hd
                    ins = v.scalar_tensor_tensor(prob[:, hd, i, :], S[:, hd, i, :], m.cumq[:, i, h:h + 1],
                                                 cst(m, "causal", P, i * SEQ, SEQ), ALU.add, ALU.add)
            return ins
        return Unit(scores=scores, bias=bias, values=lambda hd, k: m.fv[:, k, (2 * p + hd) * HD:(2 * p + hd + 1) * HD],
                               keys=SEQ, gate=None, first=True, last=True, out=m.hT[:, p, :])

    attn = Attention(m, s, "od", [unit(p) for p in range(8)])

    with nc.Block() as block:

        @block.gpsimd
        def _(pool):
            m.clear_last(pool)

        @block.sync
        def _(sp):
            sp.dma_start(m.ring[:, 16:24, :], stack(t["odd_w_out_2"][0])).then_inc(m.oout_in, 16)

        @block.tensor
        def _(pe):
            attn.tensor(pe)

        @block.scalar
        def _(act):
            attn.scalar(act)

        @block.vector
        def _(v):
            attn.vector(v)
    s.stack.close()
    m.odd.stack.close()


def stage_mlp1(nc, m, t):
    stage_mlp(nc, m, t, 1, m.oout_in, 16)


def stage_final(nc, m, t):
    s = Memory(nc)
    row = s.sb("final_row", [P, D])
    y = s.sb("final_y", [P, QT, D])
    stats = s.sb("final_st", [P, 2 * QT])
    row_in, sq, std, inv, done, out_done = (m.sem(f"final_{n}") for n in ("row_in", "sq", "std", "inv", "done", "out_done"))

    with nc.Block() as block:

        @block.gpsimd
        def _(pool):
            m.clear_last(pool)

        @block.sync
        def _(sp):
            sp.dma_start(row[:], bcast_row(t["final_norm_2"], D)).then_inc(row_in, 16)
            out = stack(t["out"][0])
            for i in range(QT):
                sp.wait_ge(done, i + 1)
                sp.dma_start(out[:, i, :], y[:, i, :]).then_inc(out_done, 16)
            sp.wait_ge(out_done, 16 * QT)

        @block.scalar
        def _(act):
            for i in range(QT):
                act.activation(y[:, i, :], m.x[:, i, :], ACT.Square, accum_out=stats[:, i:i + 1]).then_inc(sq, 1)
            act.wait_ge(sq, QT)
            act.activation(stats[:, QT:2 * QT], stats[:, 0:QT], ACT.Sqrt, scale=1.0 / D, bias=m.eps[:, 1:2]).then_inc(std, 1)

        @block.vector
        def _(v):
            v.wait_ge(std, 1)
            v.reciprocal(stats[:, QT:2 * QT], stats[:, QT:2 * QT]).then_inc(inv, 1)
            v.wait_ge(inv, 1)
            v.wait_ge(row_in, 16)
            for i in range(QT):
                v.scalar_tensor_tensor(y[:, i, :], m.x[:, i, :], stats[:, QT + i:QT + i + 1], row[:], ALU.mult, ALU.mult).then_inc(done, 1)


STAGES = (stage_input, stage_latent, stage_residual, stage_route, stage_experts, stage_even_project, stage_even_attend,
          stage_mlp0, stage_odd_project, stage_odd_attend, stage_mlp1, stage_final)


def program(nc, t):
    m = Memory(nc)
    m.consts = m.sb("consts_sb", [P, NCONST])
    m.ring = m.sb("ring", [P, 24, D])
    m.x = m.sb("x_sb", [P, QT, D])
    m.hT = m.sb("hT", [P, C, SEQ])
    m.cols = m.sb("cols", [P, NROWS])
    m.eps = m.sb("eps", [P, 2])
    m.one = m.sb("one", [P, 1])
    m.ps = m.stack.enter_context(nc.psum_tensor("ps", [P, 8, 512], F32))
    m.init = m.lasting("init")
    m.silu = m.sb("silu", [P, C, 2])
    m.r_g2 = m.sb("r_g2", [P, D])
    m.mla = Memory(nc)
    m.wq = m.mla.sb("wq", [P, 3, HEADS * NOPE])
    m.wqr = m.mla.sb("wqr", [P, 3, HEADS * ROPE])
    m.wkv = m.mla.sb("wkv", [P, 2, HEADS * (NOPE + VDIM)])
    m.qlatT = m.mla.sb("qlatT", [P, 3, SEQ])
    m.kvlatT = m.mla.sb("kvlatT", [P, 2, 2 * SEQ])
    m.kropeT = m.mla.sb("kropeT", [P, 2 * SEQ])
    m.uT = m.mla.sb("uT", [P, 2, SEQ])
    for stage in STAGES:
        stage(nc, m, t)
        m.end_stage()


_INS = ["x", "c", "ctx", "c_ctx", "w_mod", "b_mod", "norm_attn_pre", "norm_attn_post", "norm_ffn_pre", "norm_ffn_post",
        "w_in", "norm_q_lat", "norm_kv_lat", "w_q_up", "w_kv_up", "w_fourier", "w_out", "w_router", "b_router",
        "w_gate", "b_gate", "w_up", "b_up", "w_down", "b_down", "rel_bias_2", "mix_norm_2", "mlp_norm_2", "even_w_in_2",
        "even_w_out_2", "cmp_pos_k_2", "cmp_pos_v_2", "cmp_k_w1_2", "cmp_k_w2_2", "cmp_v_w1_2", "cmp_v_w2_2",
        "odd_w_in_2", "odd_b_forget_2", "odd_w_out_2", "mlp_w1_2", "mlp_w2_2", "final_norm_2"]


def kernel(**inputs):
    import concourse.bacc as bacc
    from concourse.bass_utils import run_bass_kernel_spmd

    nc = bacc.Bacc("TRN2", target_bir_lowering=False, num_devices=1)
    arrays, t = {}, {}
    for name in _INS:
        a = np.ascontiguousarray(inputs[name])
        arrays[f"in_{name}"] = a
        t[name] = nc.dram_tensor(f"in_{name}", a.shape, mybir.dt.from_np(a.dtype), kind="ExternalInput").ap()
    arrays["in_consts"], arrays["in_buckets"] = shape_constants()
    t["buckets"] = nc.dram_tensor("in_buckets", (BUCKETS, 3, 512), F32, kind="ExternalInput").ap()
    t["consts"] = nc.dram_tensor("in_consts", (P, NCONST), F32, kind="ExternalInput").ap()
    t["toeplitz"] = nc.dram_tensor("toeplitz", (16, P * 512), F32, kind="Internal").ap()
    t["out"] = nc.dram_tensor("out", (1, SEQ, D), F32, kind="ExternalOutput").ap()
    program(nc, t)
    r = run_bass_kernel_spmd(nc, [arrays], core_ids=[0])
    return r.results[0]["out"]
```

```python
import math
from contextlib import ExitStack

import numpy as np

import concourse.bass as bass
import concourse.mybir as mybir

F32 = mybir.dt.float32
I32 = mybir.dt.int32
U32 = mybir.dt.uint32
ALU = mybir.AluOpType
ACT = mybir.ActivationFunctionType
AX = mybir.AxisListType.X

P = 128
D = 1024
C = D // P
SEQ = 256
QT = SEQ // P
NEG = -1e30

HEADS = 6
NOPE, ROPE, VDIM = 128, 64, 128
QLAT, KVLAT = 384, 256
FOUR = 256
IN_W = FOUR + QLAT + KVLAT + ROPE
EPS = 1e-6
EXPERTS, TOPK, FF = 32, 4, 1024
SLOTS = 64
SPARE = (SEQ * TOPK) // (SLOTS + 1)
PASSES = EXPERTS + SPARE + 1
LIMIT, ALPHA = 7.0, 1.702

HD = 64
EVEN_IN = 2840
MQ, MK, MV, NQ, KC, VC, KSL, VSL, KWN, VWN, GZ = 0, 512, 1024, 1536, 2048, 2176, 2304, 2432, 2560, 2688, 2816
ODD_IN = 3088
CMP_BLOCK, CMP_STRIDE, CMP_HID = 32, 16, 256
NCMP = (SEQ - CMP_BLOCK) // CMP_STRIDE + 1
BUCKETS = 32
DFF2 = 4096
EPS2 = 1e-5

ROWS = {}
_at = 0
for _name, _n in (("pre", 8), ("mix", 16), ("mlp", 16), ("qlat", 3), ("kvlat", 2), ("c", 8), ("cctx", 8), ("bmod", 16)):
    ROWS[_name] = (_at, _n)
    _at += _n
NROWS = _at

CONST = {}
_at = 0
for _name, _n in (("ident", P), ("ones", P), ("swap", P), ("ccos", P), ("csin", P), ("tri", QT * SEQ), ("stri", QT * SEQ),
                  ("cos", SEQ), ("sin", SEQ), ("ncos", QT * SEQ), ("nsin", QT * SEQ), ("iota", P),
                  ("causal", QT * SEQ),
                  ("cmpvalid", QT), ("etri", EXPERTS)):
    CONST[_name] = (_at, _n)
    _at += _n
NCONST = _at


def shape_constants():
    out = np.zeros((P, NCONST), np.float32)
    buckets = np.zeros((BUCKETS, 2, 512), np.float32)

    def put(name, a):
        a = np.asarray(a, np.float32)
        a = a.reshape(a.shape[0], -1)
        at, n = CONST[name]
        out[:a.shape[0], at:at + n] = a

    eye = np.eye(P)
    put("ident", eye)
    put("ones", np.ones((P, P)))
    swap = np.zeros((P, P))
    for i in range(P // 2):
        swap[2 * i + 1, 2 * i] = -1.0
        swap[2 * i, 2 * i + 1] = 1.0
    put("swap", swap)
    k = np.arange(HD)
    ang = 2 * np.pi * np.outer(k, k) / HD
    put("ccos", np.kron(np.eye(2), np.cos(ang)))
    put("csin", np.kron(np.eye(2), np.sin(ang)))
    n = np.arange(SEQ)
    incl = (n[:, None] <= n[None, :]).astype(np.float32).reshape(QT, P, SEQ).transpose(1, 0, 2)
    strict = (n[:, None] < n[None, :]).astype(np.float32).reshape(QT, P, SEQ).transpose(1, 0, 2)
    put("tri", incl)
    put("stri", strict)
    half = ROPE // 2
    inv = (1.0 / (np.float32(10000.0) ** (np.arange(0, half, 2, dtype=np.float32) / np.float32(half)))).astype(np.float32)
    row = (n // 64).astype(np.float32)
    col = (n % 64).astype(np.float32)
    a = np.concatenate([row[:, None] * inv, col[:, None] * inv], axis=-1)
    put("cos", np.tile(np.repeat(np.cos(a).T, 2, axis=0), (2, 1)))
    put("sin", np.tile(np.repeat(np.sin(a).T, 2, axis=0), (2, 1)))
    big = 2 * np.pi * (np.outer(n, n) % SEQ) / SEQ
    norm = 1.0 / math.sqrt(SEQ * HD)
    put("ncos", (np.cos(big) * norm).reshape(QT, P, SEQ).transpose(1, 0, 2))
    put("nsin", (-np.sin(big) * norm).reshape(QT, P, SEQ).transpose(1, 0, 2))
    put("iota", np.tile(np.arange(P), (P, 1)))
    nf = np.maximum(n, 1).astype(np.float32)
    large = 16 + (np.log(nf / np.float32(16)) / np.float32(math.log(64)) * np.float32(16)).astype(np.int32)
    bucket = np.where(n < 16, n, np.minimum(large, BUCKETS - 1))
    fwd = np.zeros((BUCKETS, 512))
    fwd[bucket, n + 256] = 1.0
    buckets[:, 0] = fwd[:, ::-1]
    buckets[:, 1] = np.where(np.arange(512) <= 255, 0.0, NEG)
    q = n[:, None]
    put("causal", np.where(n[None, :] <= q, 0.0, NEG).reshape(QT, P, SEQ).transpose(1, 0, 2))
    end = np.arange(NCMP) * CMP_STRIDE + CMP_BLOCK - 1
    seen = end[None, :] <= q
    put("cmpvalid", seen.any(1).astype(np.float32).reshape(QT, P).T)
    e = np.arange(EXPERTS)
    put("etri", (e[:, None] < e[None, :]).astype(np.float32))
    return out, buckets


def bcast_row(ap, n):
    return bass.AP(ap.tensor, ap.offset, [[0, P], [1, n]])


def stack(ap, p=P):
    return ap.rearrange("(c p) n -> p c n", p=p)


class Memory:

    def __init__(self, nc):
        self.nc = nc
        self.stack = ExitStack()
        self.of_stage, self.of_last = [], []

    def sb(self, name, shape, dt=F32):
        return self.stack.enter_context(self.nc.sbuf_tensor(name, shape, dt))

    def lasting(self, name):
        return self.stack.enter_context(self.nc.semaphore(name))

    def sem(self, name):
        context = self.nc.semaphore(name)
        s = context.__enter__()
        self.of_stage.append((context, s))
        return s

    def clear_last(self, pool):
        for _, s in self.of_last:
            pool.sem_clear(s)

    def end_stage(self):
        for context, _ in self.of_last:
            context.__exit__(None, None, None)
        self.of_stage, self.of_last = [], self.of_stage


def cst(m, name, rows=P, lo=0, n=None):
    at, width = CONST[name]
    return m.consts[0:rows, at + lo:at + (width if n is None else lo + n)]


def col(m, name, i=0, n=1):
    at, _ = ROWS[name]
    return m.cols[:, at + i:at + i + n]


def spread(ap, n):
    return ap.rearrange("p (a b) -> p a b", b=1).to_broadcast([ap.shape[0], ap.shape[1], n])


def stage_input(nc, m, t):
    s = m.stage = Memory(nc)
    rows = s.sb("rows", [P, P])
    ctx_sb = s.sb("ctx_sb", [P, QT, D])
    xn = m.hT[:].rearrange("p c n -> p (c n)").rearrange("p (i n) -> p i n", i=QT)
    hcT = s.sb("hcT", [P, C, SEQ])
    junk = s.sb("junk", [P, D])
    sums = s.sb("sums", [P, 16])
    std = s.sb("std", [P, 16])
    rstd = s.sb("rstd", [P, 16])
    silu = s.sb("silu32", [P, C, 32])
    mods = s.sb("mods", [P, 512])
    modv = s.sb("modv", [P, 16, 2])
    gain = s.sb("gain", [P, C, 2])
    buckets = s.sb("buckets", [BUCKETS, 2, 512])
    line = s.sb("line", [16, 512])
    tab = s.sb("tab", [BUCKETS, 16])
    qlat = s.sb("qlat", [P, QT, QLAT])
    kvlat = s.sb("kvlat", [P, 2 * QT, KVLAT])

    late_in = m.sem("late_in")
    consts_in, rows_in, x_in, ctx_in, tab_in = (m.sem(n) for n in ("consts_in", "rows_in", "x_in", "ctx_in", "tab_in"))
    moda_in = [m.sem(f"moda_in{c}") for c in range(C)]
    win_in = [m.sem("win_in0"), m.sem("win_in1")]
    m.up_in = m.lasting("up_in")
    m.modb_in = [m.lasting(f"modb_in{c}") for c in range(4)]
    squares, stds, rstds, normed = (m.sem(n) for n in ("squares", "stds", "rstds", "normed"))
    rows_t, cols_ready, silu_ready, xt_ps, ctx_ps, moda_ps = (
        m.sem(n) for n in ("rows_t", "cols_ready", "silu_ready", "xt_ps", "ctx_ps", "moda_ps"))
    silu_zero, mods_ps, mods_sb = m.sem("silu_zero"), m.sem("mods_ps"), m.sem("mods_sb")
    modv_ready, gain_ready, hT_ready, hcT_ready = (m.sem(n) for n in ("modv_ready", "gain_ready", "hT_ready", "hcT_ready"))
    line_ps, line_ready = m.sem("line_ps"), m.sem("line_ready")
    proj_ps, lat_raw, rope_raw, lat_sq, lat_std, lat_rstd, lat_normed, lat_tps, lat_ready = (
        m.sem(n) for n in ("proj_ps", "lat_raw", "rope_raw", "lat_sq", "lat_std", "lat_rstd", "lat_normed", "lat_tps", "lat_ready"))
    m.toeplitz_out = m.lasting("toeplitz_out")
    ps = m.ps
    win = m.ring[:, 16:24, :]

    with nc.Block() as block:

        @block.gpsimd
        def _(pool):
            m.clear_last(pool)
            pool.memset(silu[:], 0.0).then_inc(silu_zero, 1)

        @block.sync
        def _(sp):
            early = 2 * P
            sp.dma_start(m.consts[:, 0:early], t["consts"][:, 0:early]).then_inc(consts_in, 16)
            sp.dma_start(tab[:], t["rel_bias_2"]).then_inc(tab_in, 16)
            sp.dma_start(buckets[:], t["buckets"]).then_inc(tab_in, 16)
            for name, src in (("pre", t["norm_attn_pre"]), ("mix", t["mix_norm_2"]), ("mlp", t["mlp_norm_2"]),
                              ("qlat", t["norm_q_lat"]), ("kvlat", t["norm_kv_lat"]), ("c", t["c"]),
                              ("cctx", t["c_ctx"]), ("bmod", t["b_mod"])):
                at, n = ROWS[name]
                flat = bass.AP(src.tensor, 0, [[P, n], [1, P]])
                sp.dma_start(rows[at:at + n, :], flat).then_inc(rows_in, 16)
            sp.dma_start(m.x[:], stack(t["x"][0])).then_inc(x_in, 16)
            sp.dma_start(ctx_sb[:], stack(t["ctx"][0])).then_inc(ctx_in, 16)
            for c in range(C):
                sp.dma_start(m.ring[:, 2 * c:2 * c + 2, :].rearrange("p a n -> p (a n)"),
                             t["w_mod"][0, c * P:(c + 1) * P, 0:2 * D]).then_inc(moda_in[c], 16)
            for i in range(2):
                src = stack(t["w_in"][0, 512 * i:512 * i + 512, :])
                sp.dma_start(win[:, 4 * i:4 * i + 4, 0:IN_W], src).then_inc(win_in[i], 16)
                sp.dma_start(win[:, 4 * i:4 * i + 4, IN_W:D], src[:, :, IN_W - ROPE:IN_W]).then_inc(win_in[i], 16)
            sp.dma_start(m.consts[:, early:], t["consts"][:, early:]).then_inc(late_in, 16)
            sp.wait_ge(line_ready, 1)
            src = line[:, 0:511].rearrange("h (a n) -> h a n", a=1).to_broadcast([16, P, 511])
            sp.dma_start(bass.AP(t["toeplitz"].tensor, 0, [[P * 512, 16], [511, P], [1, 511]]), src).then_inc(m.toeplitz_out, 16)
            for k in range(3):
                src = t["w_q_up"][0, k * P:(k + 1) * P, :].rearrange("p (h n) -> p h n", h=HEADS)
                sp.dma_start(m.wq[:, k, :].rearrange("p (h n) -> p h n", h=HEADS), src[:, :, 0:NOPE]).then_inc(m.up_in, 16)
                sp.dma_start(m.wqr[:, k, :].rearrange("p (h n) -> p h n", h=HEADS), src[:, :, NOPE:]).then_inc(m.up_in, 16)
            sp.dma_start(m.wkv[:], stack(t["w_kv_up"][0])).then_inc(m.up_in, 16)
            sp.wait_ge(mods_ps, 1)
            for c in range(4):
                sp.dma_start(m.ring[:, 4 * c:4 * c + 4, :].rearrange("p a n -> p (a n)"),
                             t["w_mod"][0, c * P:(c + 1) * P, 2 * D:]).then_inc(m.modb_in[c], 16)
            sp.wait_ge(late_in, 16)

        @block.scalar
        def _(act):
            def rms(src, i):
                act.activation(junk[:, 0:src.shape[1]], src, ACT.Square, accum_out=sums[:, i:i + 1]).then_inc(squares, 1)

            act.wait_ge(x_in, 16)
            for i in range(QT):
                if i:
                    act.wait_ge(squares, i)
                rms(m.x[:, i, :], i)
            act.wait_ge(ctx_in, 16)
            for i in range(QT):
                act.wait_ge(squares, QT + i)
                rms(ctx_sb[:, i, :], QT + i)
            act.wait_ge(squares, 4)
            act.wait_ge(m.init, 1)
            act.activation(std[:, 0:4], sums[:, 0:4], ACT.Sqrt, scale=1.0 / D, bias=m.eps[:, 0:1]).then_inc(stds, 1)
            act.wait_ge(cols_ready, 1)
            at = ROWS["c"][0]
            act.activation(m.silu[:].rearrange("p c s -> p s c"),
                           m.cols[:, at:at + 16].rearrange("p (s c) -> p s c", s=2), ACT.Silu).then_inc(silu_ready, 1)
            act.wait_ge(silu_ready, 1)
            act.wait_ge(silu_zero, 1)
            act.copy(silu[:, :, 0:2], m.silu[:]).then_inc(silu_ready, 1)
            act.wait_ge(mods_ps, 1)
            act.copy(mods[:], ps[:, 5, :]).then_inc(mods_sb, 1)
            act.wait_ge(gain_ready, 1)
            act.wait_ge(ctx_ps, 1)
            for c in range(C):
                act.activation(hcT[:, c, :], ps[:, 4 + c // 2, (c % 2) * SEQ:(c % 2 + 1) * SEQ], ACT.Identity,
                               bias=modv[:, c, 1:2], scale=gain[:, c, 1:2]).then_inc(hcT_ready, 1)
            act.wait_ge(proj_ps, 1)
            act.copy(qlat[:], ps[:, 0:2, 0:QLAT]).then_inc(lat_raw, 1)
            act.wait_ge(proj_ps, 2)
            act.copy(kvlat[:].rearrange("p a n -> p (a n)"), ps[:, 2:4, :].rearrange("p a n -> p (a n)")).then_inc(lat_raw, 1)
            act.wait_ge(lat_raw, 2)
            for i in range(QT):
                if i:
                    act.wait_ge(lat_sq, i)
                act.activation(junk[:, 0:QLAT], qlat[:, i, :], ACT.Square, accum_out=sums[:, 4 + i:5 + i]).then_inc(lat_sq, 1)
            for i in range(2 * QT):
                act.wait_ge(lat_sq, QT + i)
                act.activation(junk[:, 0:KVLAT], kvlat[:, i, :], ACT.Square, accum_out=sums[:, 6 + i:7 + i]).then_inc(lat_sq, 1)
            act.wait_ge(lat_sq, 6)
            act.activation(std[:, 4:6], sums[:, 4:6], ACT.Sqrt, scale=1.0 / QLAT, bias=m.eps[:, 0:1]).then_inc(lat_std, 1)
            act.activation(std[:, 6:10], sums[:, 6:10], ACT.Sqrt, scale=1.0 / KVLAT, bias=m.eps[:, 0:1]).then_inc(lat_std, 1)
            act.wait_ge(lat_tps, 1)
            for k in range(3):
                act.activation(m.qlatT[:, k, :], ps[:, k // 2, (k % 2) * SEQ:(k % 2 + 1) * SEQ], ACT.Copy,
                               scale=col(m, "qlat", k)).then_inc(lat_ready, 1)
            act.wait_ge(lat_tps, 2)
            for k in range(2):
                act.activation(m.kvlatT[:, k, :], ps[:, 2 + k, :], ACT.Copy, scale=col(m, "kvlat", k)).then_inc(lat_ready, 1)

        @block.vector
        def _(v):
            v.memset(m.eps[:, 0:1], EPS)
            v.memset(m.eps[:, 1:2], EPS2).then_inc(m.init, 1)
            v.wait_ge(rows_t, 1)
            v.tensor_copy(m.cols[:], ps[:, 7, 0:NROWS]).then_inc(cols_ready, 1)
            v.wait_ge(stds, 1)
            v.reciprocal(rstd[:, 0:4], std[:, 0:4]).then_inc(rstds, 1)
            v.wait_ge(rstds, 1)
            for i in range(QT):
                v.tensor_scalar(xn[:, i, :], m.x[:, i, :], rstd[:, i:i + 1], None, ALU.mult).then_inc(normed, 1)
            for i in range(QT):
                v.tensor_scalar(ctx_sb[:, i, :], ctx_sb[:, i, :], rstd[:, 2 + i:3 + i], None, ALU.mult).then_inc(normed, 1)
            v.wait_ge(line_ps, 1)
            v.wait_ge(tab_in, 32)
            v.tensor_tensor(line[:], ps[0:16, 6, :], buckets[0:16, 1, :], ALU.add).then_inc(line_ready, 1)
            v.wait_ge(moda_ps, 1)
            v.wait_ge(cols_ready, 1)
            for b in range(4):
                v.tensor_tensor(modv[:, b:16:4, :], ps[:, 7, b * P:(b + 1) * P].rearrange("p (j s) -> p j s", j=4)[:, :, 0:2],
                                spread(col(m, "bmod", 0, 16)[:, b:16:4], 2), ALU.add).then_inc(modv_ready, 1)
            v.wait_ge(modv_ready, 4)
            v.scalar_tensor_tensor(gain[:], modv[:, 8:16, :], 1.0, spread(col(m, "pre", 0, 8), 2), ALU.add, ALU.mult).then_inc(gain_ready, 1)
            v.wait_ge(gain_ready, 1)
            v.wait_ge(xt_ps, 1)
            for c in range(C):
                v.tensor_scalar(m.hT[:, c, :], ps[:, c // 2, (c % 2) * SEQ:(c % 2 + 1) * SEQ], gain[:, c, 0:1],
                                modv[:, c, 0:1], ALU.mult, ALU.add).then_inc(hT_ready, 1)
            v.wait_ge(proj_ps, 3)
            v.tensor_copy(m.kropeT[:], ps[:, 4, :]).then_inc(rope_raw, 1)
            v.wait_ge(proj_ps, 4)
            v.tensor_copy(m.uT[:].rearrange("p a n -> p (a n)"), ps[:, 5, :]).then_inc(rope_raw, 1)
            v.wait_ge(lat_std, 2)
            v.reciprocal(rstd[:, 4:10], std[:, 4:10]).then_inc(lat_rstd, 1)
            v.wait_ge(lat_rstd, 1)
            for i in range(QT):
                v.tensor_scalar(qlat[:, i, :], qlat[:, i, :], rstd[:, 4 + i:5 + i], None, ALU.mult).then_inc(lat_normed, 1)
            for i in range(2 * QT):
                v.tensor_scalar(kvlat[:, i, :], kvlat[:, i, :], rstd[:, 6 + i:7 + i], None, ALU.mult).then_inc(lat_normed, 1)

        @block.tensor
        def _(pe):
            ident = cst(m, "ident")
            pe.wait_ge(consts_in, 16)
            pe.wait_ge(rows_in, 16 * len(ROWS))
            pe.transpose(ps[:, 7, 0:NROWS], rows[0:NROWS, :], ident[0:NROWS, 0:NROWS]).then_inc(rows_t, 1)
            pe.wait_ge(tab_in, 32)
            pe.matmul(ps[0:16, 6, :], tab[:], buckets[:, 0, :], start=True, stop=True).then_inc(line_ps, 1)
            pe.wait_ge(normed, QT)
            for c in range(C):
                for i in range(QT):
                    mm = pe.transpose(ps[:, c // 2, (c % 2) * SEQ + i * P:(c % 2) * SEQ + (i + 1) * P],
                                      xn[:, i, c * P:(c + 1) * P], ident)
            mm.then_inc(xt_ps, 1)
            pe.wait_ge(silu_ready, 2)
            for c in range(C):
                pe.wait_ge(moda_in[c], 16)
                for j in range(4):
                    mm = pe.matmul(ps[32 * j:32 * (j + 1), 5, :], silu[:, c, :],
                                   m.ring[:, 2 * c + j // 2, (j % 2) * 512:(j % 2 + 1) * 512], start=(c == 0), stop=(c == C - 1))
            mm.then_inc(mods_ps, 1)
            pe.wait_ge(mods_sb, 1)
            pe.wait_ge(cols_ready, 1)
            for b in range(4):
                mm = pe.transpose(ps[:, 7, b * P:(b + 1) * P], mods[:, b * P:(b + 1) * P], ident)
            mm.then_inc(moda_ps, 1)
            pe.wait_ge(modv_ready, 4)
            pe.wait_ge(line_ready, 1)
            pe.wait_ge(normed, 2 * QT)
            for c in range(C):
                for i in range(QT):
                    mm = pe.transpose(ps[:, 4 + c // 2, (c % 2) * SEQ + i * P:(c % 2) * SEQ + (i + 1) * P],
                                      ctx_sb[:, i, c * P:(c + 1) * P], ident)
            mm.then_inc(ctx_ps, 1)
            pe.wait_ge(hT_ready, C)
            for i in range(2):
                pe.wait_ge(win_in[i], 32)
            for i in range(QT):
                for c in range(C):
                    mm = pe.matmul(ps[:, i, 0:QLAT], m.hT[:, c, i * P:(i + 1) * P], win[:, c, FOUR:FOUR + QLAT],
                                   start=(c == 0), stop=(c == C - 1))
            mm.then_inc(proj_ps, 1)
            for i in range(2 * QT):
                if i == QT:
                    pe.wait_ge(hcT_ready, C)
                src = m.hT if i < QT else hcT
                for c in range(C):
                    mm = pe.matmul(ps[:, 2 + i // 2, (i % 2) * KVLAT:(i % 2 + 1) * KVLAT], src[:, c, (i % 2) * P:(i % 2 + 1) * P],
                                   win[:, c, FOUR + QLAT:FOUR + QLAT + KVLAT], start=(c == 0), stop=(c == C - 1))
            mm.then_inc(proj_ps, 1)
            for j, src in enumerate((m.hT, hcT)):
                for c in range(C):
                    mm = pe.matmul(ps[:, 4, j * SEQ:(j + 1) * SEQ], win[:, c, D - P:D], src[:, c, :], start=(c == 0), stop=(c == C - 1))
            mm.then_inc(proj_ps, 1)
            for j in range(2):
                for c in range(C):
                    mm = pe.matmul(ps[:, 5, j * SEQ:(j + 1) * SEQ], win[:, c, j * P:(j + 1) * P], m.hT[:, c, :],
                                   start=(c == 0), stop=(c == C - 1))
            mm.then_inc(proj_ps, 1)
            pe.wait_ge(lat_raw, 2)
            pe.wait_ge(lat_normed, QT)
            for k in range(3):
                for i in range(QT):
                    mm = pe.transpose(ps[:, k // 2, (k % 2) * SEQ + i * P:(k % 2) * SEQ + (i + 1) * P],
                                      qlat[:, i, k * P:(k + 1) * P], ident)
            mm.then_inc(lat_tps, 1)
            pe.wait_ge(lat_normed, 3 * QT)
            for k in range(2):
                for i in range(2 * QT):
                    mm = pe.transpose(ps[:, 2 + k, i * P:(i + 1) * P], kvlat[:, i, k * P:(k + 1) * P], ident)
            mm.then_inc(lat_tps, 1)
    s.stack.close()


def load_expert0(sp, m, t, parts):
    for k in parts:
        sp.dma_start(m.ring[:, 2 * k:2 * k + 2, :], expert_rows(t, 0, k)).then_inc(m.moe_in[k], 16)


def stage_latent(nc, m, t):
    s = Memory(nc)
    qrope = s.sb("qrope", [P, HEADS, SEQ])
    val = s.sb("val", [P, 4, HEADS * VDIM])
    qn = s.sb("qn", [P, 2, SEQ])
    kn = s.sb("kn", [P, 2, 2 * SEQ])
    prob = s.sb("prob", [P, 2, QT, 512])
    probT = s.sb("probT", [P, 4, SEQ])
    bd = s.sb("bd", [P, 2, 2, P])
    wf = s.sb("wf", [P, 2, HD])
    top = s.sb("top", [P, 4 * HEADS])
    turn = prob[:, 0].rearrange("p a n -> p (a n)")
    qropeT = prob[:, 1].rearrange("p a n -> p (a n)")[:, 0:3 * SEQ].rearrange("p (a n) -> p a n", a=3)
    vs = probT[:].rearrange("p a n -> p (a n)").rearrange("p (a i n) -> p a i n", a=2, i=2)
    mixT = m.hT
    ps = m.ps
    acc = m.ring[:, 20:24, :].rearrange("p a n -> p (a n)")
    SCALE = (NOPE + ROPE) ** -0.5
    modb_slot = [0, 4, 8, 12, 16, 0, 4, 8]
    m.moe_in = [m.lasting(f"moe_in{k}") for k in range(12)]

    wf_in, acc_zero, acc_in, modb_done, bd_zero = (m.sem(n) for n in ("wf_in", "acc_zero", "acc_in", "modb_done", "bd_zero"))
    modb_in = m.modb_in + [m.sem(f"modb_in{c}") for c in range(4, C)]
    m.wout_in = [m.lasting("wout_in0"), m.lasting("wout_in1")]
    m.rowvec_in = m.lasting("rowvec_in")
    rope_ps, rope_sb, rope_mul, rope_done = (m.sem(n) for n in ("rope_ps", "rope_sb", "rope_mul", "rope_done"))
    val_ps, val_sb = m.sem("val_ps"), m.sem("val_sb")
    four_ps, four_sb = m.sem("four_ps"), m.sem("four_sb")
    qk_ps, q_sb, k_sb, s_ps, s_max, s_neg, s_exp, s_inv, s_prob = (
        m.sem(n) for n in ("qk_ps", "q_sb", "k_sb", "s_ps", "s_max", "s_neg", "s_exp", "s_inv", "s_prob"))
    pt_ps, pt_sb0, pt_sb1, pv_ps, pv_sb = (m.sem(n) for n in ("pt_ps", "pt_sb0", "pt_sb1", "pv_ps", "pv_sb"))

    with nc.Block() as block:

        @block.sync
        def _(sp):
            sp.dma_start(wf[:], t["w_fourier"][0].rearrange("(a b) c d -> (b c) a d", b=2)).then_inc(wf_in, 16)
            sp.wait_ge(acc_zero, 1)
            sp.dma_start(acc[0:1, :], t["b_mod"][0:1, 2 * D:]).then_inc(acc_in, 16)
            for c in range(4, C):
                if c >= 5:
                    sp.wait_ge(modb_done, c - 4)
                a = modb_slot[c]
                sp.dma_start(m.ring[:, a:a + 4, :].rearrange("p a n -> p (a n)"),
                             t["w_mod"][0, c * P:(c + 1) * P, 2 * D:]).then_inc(modb_in[c], 16)
            sp.wait_ge(modb_done, 5)
            for i in range(2):
                sp.dma_start(m.ring[:, 12 + 4 * i:16 + 4 * i, :], stack(t["w_out"][0, 512 * i:512 * i + 512, :])).then_inc(m.wout_in[i], 16)
            sp.wait_ge(modb_done, 7)
            for j, name in enumerate(("norm_attn_post", "norm_ffn_pre", "norm_ffn_post")):
                sp.dma_start(m.ring[:, j, :], bcast_row(t[name], D)).then_inc(m.rowvec_in, 16)
            sp.wait_ge(modb_done, C)
            load_expert0(sp, m, t, (3, 4, 5))

        @block.gpsimd
        def _(pool):
            m.clear_last(pool)
            pool.memset(acc, 0.0).then_inc(acc_zero, 1)
            pool.memset(bd[:], 0.0).then_inc(bd_zero, 1)
            pool.memset(qrope[:], 0.0).then_inc(bd_zero, 1)

        @block.tensor
        def _(pe):
            ident = cst(m, "ident")
            pe.wait_ge(m.up_in, 16 * 7)
            for j in range(3):
                for k in range(3):
                    mm = pe.matmul(ps[:, j // 2, (j % 2) * SEQ:(j % 2 + 1) * SEQ], m.wqr[:, k, j * P:(j + 1) * P],
                                   m.qlatT[:, k, :], start=(k == 0), stop=(k == 2))
            mm.then_inc(rope_ps, 1)
            pe.matmul(ps[:, 2, 0:SEQ], cst(m, "swap"), m.kropeT[:, 0:SEQ], start=True, stop=True).then_inc(rope_ps, 1)
            pe.wait_ge(rope_sb, 1)
            pe.matmul(ps[:, 3, :], cst(m, "swap"), qropeT[:, 0:2, :], start=True, stop=True)
            pe.matmul(ps[:, 4, 0:SEQ], cst(m, "swap"), qropeT[:, 2, :], start=True, stop=True).then_inc(rope_ps, 1)
            wv = [m.wkv[:, k, :].rearrange("p (h n) -> p h n", h=HEADS)[:, :, NOPE:] for k in range(2)]
            for n, i in enumerate((3, 0, 1, 2)):
                a = 2 * i
                if n == 1:
                    pe.wait_ge(rope_done, 2)
                for lo, hi in ((0, 4), (4, HEADS)):
                    for k in range(2):
                        mm = pe.matmul(ps[:, a, 0:(hi - lo) * VDIM], m.kvlatT[:, k, i * P:(i + 1) * P], wv[k][:, lo:hi, :],
                                       start=(k == 0), stop=(k == 1))
                    a += 1
                mm.then_inc(val_ps, 1)
            pe.wait_ge(wf_in, 16)
            pe.wait_ge(val_sb, 4)
            for a in range(2):
                for b, name in enumerate(("ccos", "csin")):
                    mm = pe.matmul(ps[:, 0, (2 * a + b) * HD:(2 * a + b + 1) * HD], cst(m, name), wf[:, a, :], start=True, stop=True)
            mm.then_inc(four_ps, 1)
            pe.wait_ge(four_sb, 2)
            for a in range(2):
                for i in range(QT):
                    mm = pe.matmul(ps[:, 1 + a, i * SEQ:(i + 1) * SEQ], m.uT[:, a, i * P:(i + 1) * P],
                                   bd[:, a, :, :].rearrange("p b n -> p (b n)"), start=True, stop=True)
            mm.then_inc(four_ps, 1)
            pe.wait_ge(four_sb, 3)
            for a in range(2):
                for i in range(QT):
                    pe.matmul(ps[:, 3, a * SEQ:(a + 1) * SEQ], vs[:, a, i, 0:P], cst(m, "ncos", P, i * SEQ, SEQ), start=(i == 0), stop=False)
                    mm = pe.matmul(ps[:, 3, a * SEQ:(a + 1) * SEQ], vs[:, a, i, P:2 * P], cst(m, "nsin", P, i * SEQ, SEQ), start=False, stop=(i == 1))
            mm.then_inc(four_ps, 1)

            def project(h):
                if h:
                    pe.wait_ge(q_sb, h)
                    pe.wait_ge(k_sb, h)
                for k in range(3):
                    pe.matmul(ps[:, 0, 0:SEQ], m.wq[:, k, h * NOPE:(h + 1) * NOPE], m.qlatT[:, k, :], start=(k == 0), stop=(k == 2))
                for k in range(2):
                    mm = pe.matmul(ps[:, 1, :], m.wkv[:, k, h * 256:h * 256 + NOPE], m.kvlatT[:, k, :], start=(k == 0), stop=(k == 1))
                mm.then_inc(qk_ps, 1)

            def scores(h):
                pe.wait_ge(q_sb, h + 1)
                pe.wait_ge(k_sb, h + 1)
                if h >= 2:
                    pe.wait_ge(s_exp, QT * (h - 1))
                b = 2 + 4 * (h % 2)
                for i in range(QT):
                    pe.matmul(ps[:, b + i, :], qn[:, h % 2, i * P:(i + 1) * P], kn[:, h % 2, :], start=True, stop=False)
                    mm = pe.matmul(ps[:, b + i, :], qrope[:, h, i * P:(i + 1) * P], m.kropeT[:], start=False, stop=True)
                mm.then_inc(s_ps, 1)

            pe.wait_ge(four_sb, 4)
            pe.wait_ge(rope_done, 2)
            for h in range(2):
                project(h)
                scores(h)
            for h in range(HEADS):
                pe.wait_ge(s_prob, h + 1)
                if h:
                    pe.wait_ge(pt_sb1, h)
                    pe.wait_ge(pv_sb, h)
                for k in range(4):
                    for i in range(QT):
                        mm = pe.transpose(ps[:, 4 + k // 2, (k % 2) * SEQ + i * P:(k % 2) * SEQ + (i + 1) * P],
                                          prob[:, h % 2, i, k * P:(k + 1) * P], ident)
                mm.then_inc(pt_ps, 1)
                if h + 2 < HEADS:
                    project(h + 2)
                pe.wait_ge(pt_sb0, h + 1)
                pe.wait_ge(pt_sb1, h + 1)
                for k in range(4):
                    mm = pe.matmul(ps[:, 4, 0:SEQ], val[:, k, h * VDIM:(h + 1) * VDIM], probT[:, k, :], start=(k == 0), stop=(k == 3))
                mm.then_inc(pv_ps, 1)
                if h + 2 < HEADS:
                    scores(h + 2)

        @block.scalar
        def _(act):
            act.wait_ge(rope_ps, 1)
            act.copy(qropeT.rearrange("p a n -> p (a n)"), ps[:, 0:2, :].rearrange("p a n -> p (a n)")[:, 0:3 * SEQ]).then_inc(rope_sb, 1)
            for n, i in enumerate((3, 0, 1, 2)):
                act.wait_ge(val_ps, n + 1)
                act.copy(val[:, i, :], ps[:, 2 * i:2 * i + 2, :].rearrange("p a n -> p (a n)")[:, 0:HEADS * VDIM]).then_inc(val_sb, 1)
            act.wait_ge(bd_zero, 1)
            act.wait_ge(four_ps, 1)
            blocks = ps[:, 0, 0:4 * HD].rearrange("p (a b n) -> p a b n", a=2, b=2)
            act.copy(bd[0:HD, :, :, 0:HD], blocks[0:HD]).then_inc(four_sb, 1)
            act.copy(bd[HD:P, :, :, HD:P], blocks[HD:P]).then_inc(four_sb, 1)
            act.wait_ge(four_ps, 2)
            act.copy(probT[:].rearrange("p a n -> p (a n)"), ps[:, 1:3, :].rearrange("p a n -> p (a n)")).then_inc(four_sb, 1)
            act.wait_ge(four_ps, 3)
            act.copy(mixT[:, HEADS:HEADS + 2, :].rearrange("p a n -> p (a n)"), ps[:, 3, :]).then_inc(four_sb, 1)

            def evacuate_q(h):
                act.wait_ge(qk_ps, h + 1)
                if h >= 2:
                    act.wait_ge(s_ps, h - 1)
                act.copy(qn[:, h % 2, :], ps[:, 0, 0:SEQ]).then_inc(q_sb, 1)

            def exp(h):
                act.wait_ge(s_neg, h + 1)
                if h >= 2:
                    act.wait_ge(pt_ps, h - 1)
                for i in range(QT):
                    act.activation(prob[:, h % 2, i, :], ps[:, 2 + 4 * (h % 2) + i, :], ACT.Exp, bias=top[:, 4 * h + i:4 * h + i + 1],
                                   scale=SCALE, accum_out=top[:, 4 * h + 2 + i:4 * h + 3 + i]).then_inc(s_exp, 1)

            evacuate_q(0)
            evacuate_q(1)
            exp(0)
            exp(1)
            for h in range(HEADS):
                act.wait_ge(pt_ps, h + 1)
                if h:
                    act.wait_ge(pv_ps, h)
                act.copy(probT[:, 0:2, :].rearrange("p a n -> p (a n)"), ps[:, 4, :]).then_inc(pt_sb0, 1)
                if h + 2 < HEADS:
                    evacuate_q(h + 2)
                act.wait_ge(pv_ps, h + 1)
                act.copy(mixT[:, h, :], ps[:, 4, 0:SEQ]).then_inc(pv_sb, 1)
                if h + 2 < HEADS:
                    exp(h + 2)

        @block.vector
        def _(v):
            cos, sin = cst(m, "cos"), cst(m, "sin")
            three = lambda a: a.rearrange("p (b n) -> p b n", b=1).to_broadcast([P, 3, SEQ])
            v.wait_ge(rope_ps, 2)
            v.tensor_tensor(turn[:, 768:1024], ps[:, 2, 0:SEQ], sin, ALU.mult).then_inc(rope_mul, 1)
            v.tensor_tensor(m.kropeT[:, 0:SEQ], m.kropeT[:, 0:SEQ], cos, ALU.mult).then_inc(rope_mul, 1)
            v.wait_ge(rope_mul, 2)
            v.tensor_tensor(m.kropeT[:, 0:SEQ], m.kropeT[:, 0:SEQ], turn[:, 768:1024], ALU.add).then_inc(rope_done, 1)
            v.wait_ge(rope_ps, 3)
            raw = ps[:, 3:5, :].rearrange("p a n -> p (a n)")[:, 0:768].rearrange("p (b n) -> p b n", b=3)
            mul = turn[:, 0:768].rearrange("p (b n) -> p b n", b=3)
            v.tensor_tensor(mul, raw, three(sin), ALU.mult).then_inc(rope_mul, 1)
            v.tensor_tensor(qropeT, qropeT, three(cos), ALU.mult).then_inc(rope_mul, 1)
            v.wait_ge(rope_mul, 4)
            v.wait_ge(bd_zero, 2)
            v.tensor_tensor(qrope[0:ROPE, 0:HEADS:2, :], qropeT[0:ROPE], mul[0:ROPE], ALU.add)
            v.tensor_tensor(qrope[ROPE:P, 1:HEADS:2, :], qropeT[ROPE:P], mul[ROPE:P], ALU.add).then_inc(rope_done, 1)

            def modulate(c):
                v.wait_ge(modb_in[c], 16)
                if c:
                    v.wait_ge(modb_done, c)
                else:
                    v.wait_ge(acc_in, 16)
                a = modb_slot[c]
                v.scalar_tensor_tensor(acc, m.ring[:, a:a + 4, :].rearrange("p a n -> p (a n)"), m.silu[:, c, 0:1], acc,
                                       ALU.mult, ALU.add).then_inc(modb_done, 1)

            def evacuate_k(h):
                v.wait_ge(qk_ps, h + 1)
                if h >= 2:
                    v.wait_ge(s_ps, h - 1)
                v.tensor_copy(kn[:, h % 2, :], ps[:, 1, :]).then_inc(k_sb, 1)

            def peak(h):
                v.wait_ge(s_ps, h + 1)
                b = 2 + 4 * (h % 2)
                v.tensor_reduce(top[:, 4 * h:4 * h + 2], ps[:, b:b + 2, :], AX, ALU.max).then_inc(s_max, 1)
                v.wait_ge(s_max, h + 1)
                v.tensor_scalar(top[:, 4 * h:4 * h + 2], top[:, 4 * h:4 * h + 2], -SCALE, None, ALU.mult).then_inc(s_neg, 1)

            def normalize(h):
                v.wait_ge(s_exp, QT * (h + 1))
                v.reciprocal(top[:, 4 * h + 2:4 * h + 4], top[:, 4 * h + 2:4 * h + 4]).then_inc(s_inv, 1)
                v.wait_ge(s_inv, h + 1)
                v.tensor_tensor(prob[:, h % 2], prob[:, h % 2], spread(top[:, 4 * h + 2:4 * h + 4], 512), ALU.mult).then_inc(s_prob, 1)

            modulate(0)
            modulate(1)
            evacuate_k(0)
            evacuate_k(1)
            peak(0)
            normalize(0)
            peak(1)
            normalize(1)
            for h in range(HEADS):
                v.wait_ge(pt_ps, h + 1)
                if h:
                    v.wait_ge(pv_ps, h)
                v.tensor_copy(probT[:, 2:4, :].rearrange("p a n -> p (a n)"), ps[:, 5, :]).then_inc(pt_sb1, 1)
                if h + 2 < HEADS:
                    evacuate_k(h + 2)
                modulate(h + 2)
                if h + 2 < HEADS:
                    peak(h + 2)
                    normalize(h + 2)
    s.stack.close()


def stage_residual(nc, m, t):
    m.mla.stack.close()
    s = m.moe = Memory(nc)
    h2 = m.h2 = s.sb("h2", [P, QT, D])
    m.wr = s.sb("wr", [P, C, EXPERTS])
    m.br = s.sb("br", [1, EXPERTS])
    m.router_in = m.lasting("router_in")
    stats = s.sb("stats", [P, 8])
    ps = m.ps
    rows = m.ring[:, 20:24, :].rearrange("p a n -> p (a n)")
    r_post, r_ffn, r_fpost = (m.ring[:, j, :] for j in range(3))
    junk = m.ring[:, 4, :]
    sum_ps, sum_sb, mix_ps, mix_sq, mix_std, mix_inv, row_mul, mixed, added = (
        m.sem(n) for n in ("sum_ps", "sum_sb", "mix_ps", "mix_sq", "mix_std", "mix_inv", "row_mul", "mixed", "added"))
    x_sq, x_std, x_inv, h2_mul, h2_ready, h2_ps, h2T_ready = (
        m.sem(n) for n in ("x_sq", "x_std", "x_inv", "h2_mul", "h2_ready", "h2_ps", "h2T_ready"))

    with nc.Block() as block:

        @block.gpsimd
        def _(pool):
            m.clear_last(pool)

        @block.sync
        def _(sp):
            sp.dma_start(m.wr[:], stack(t["w_router"][0])).then_inc(m.router_in, 16)
            sp.dma_start(m.br[:], t["b_router"]).then_inc(m.router_in, 16)
            sp.wait_ge(mix_ps, 2)
            load_expert0(sp, m, t, (6, 7, 8, 9))

        @block.tensor
        def _(pe):
            ident, ones = cst(m, "ident"), cst(m, "ones")
            for j in range(4):
                pe.matmul(ps[:, 4 + j, :], ones, rows[:, 512 * j:512 * (j + 1)], start=True, stop=True).then_inc(sum_ps, 1)
            for i in range(2):
                pe.wait_ge(m.wout_in[i], 16)
            for i in range(QT):
                for half in range(2):
                    for c in range(C):
                        mm = pe.matmul(ps[:, 2 * i + half, :], m.hT[:, c, i * P:(i + 1) * P], m.ring[:, 12 + c, half * 512:(half + 1) * 512],
                                       start=(c == 0), stop=(c == C - 1))
                mm.then_inc(mix_ps, 1)
            for j in range(4):
                pe.wait_ge(sum_sb, j + 1)
                pe.matmul(ps[:, 4 + j, :], ones, rows[:, 2048 + 512 * j:2048 + 512 * (j + 1)], start=True, stop=True).then_inc(sum_ps, 1)
            pe.wait_ge(added, 2)
            for i in range(QT):
                pe.wait_ge(h2_ready, i + 1)
                if i == 0:
                    pe.wait_ge(sum_sb, 8)
                for c in range(C):
                    mm = pe.transpose(ps[:, 4 * i + c // 4, (c % 4) * P:(c % 4 + 1) * P], h2[:, i, c * P:(c + 1) * P], ident)
                mm.then_inc(h2_ps, 1)

        @block.scalar
        def _(act):
            for j in range(8):
                act.wait_ge(sum_ps, j + 1)
                act.copy(rows[:, 512 * j:512 * (j + 1)], ps[:, 4 + j % 4, :]).then_inc(sum_sb, 1)
                if j == 3:
                    for i in range(QT):
                        act.wait_ge(mix_ps, i + 1)
                        if i:
                            act.wait_ge(mix_sq, i)
                        act.activation(junk, ps[:, 2 * i:2 * i + 2, :].rearrange("p a n -> p (a n)"), ACT.Square,
                                       accum_out=stats[:, i:i + 1]).then_inc(mix_sq, 1)
                    act.wait_ge(mix_sq, 2)
                    act.activation(stats[:, 2:4], stats[:, 0:2], ACT.Sqrt, scale=1.0 / D, bias=m.eps[:, 0:1]).then_inc(mix_std, 1)
            for i in range(QT):
                act.wait_ge(added, i + 1)
                act.wait_ge(mix_sq, 2)
                if i:
                    act.wait_ge(x_sq, i)
                act.activation(junk, m.x[:, i, :], ACT.Square, accum_out=stats[:, 4 + i:5 + i]).then_inc(x_sq, 1)
            act.wait_ge(x_sq, 2)
            act.activation(stats[:, 6:8], stats[:, 4:6], ACT.Sqrt, scale=1.0 / D, bias=m.eps[:, 0:1]).then_inc(x_std, 1)
            for i in range(QT):
                act.wait_ge(h2_ps, i + 1)
                act.copy(m.hT[:, 0:4, i * P:(i + 1) * P], ps[:, 4 * i, :].rearrange("p (c n) -> p c n", c=4)).then_inc(h2T_ready, 1)
                act.copy(m.hT[:, 4:8, i * P:(i + 1) * P], ps[:, 4 * i + 1, :].rearrange("p (c n) -> p c n", c=4)).then_inc(h2T_ready, 1)

        @block.vector
        def _(v):
            v.wait_ge(m.rowvec_in, 48)
            v.wait_ge(sum_sb, 2)
            v.tensor_tensor(r_post, r_post, rows[:, 0:D], ALU.mult).then_inc(row_mul, 1)
            v.wait_ge(mix_std, 1)
            v.reciprocal(stats[:, 2:4], stats[:, 2:4]).then_inc(mix_inv, 1)
            v.wait_ge(mix_inv, 1)
            v.wait_ge(row_mul, 1)
            for i in range(QT):
                v.scalar_tensor_tensor(h2[:, i, :], ps[:, 2 * i:2 * i + 2, :].rearrange("p a n -> p (a n)"), stats[:, 2 + i:3 + i],
                                       r_post, ALU.mult, ALU.mult).then_inc(mixed, 1)
                v.wait_ge(mixed, i + 1)
                v.tensor_tensor(m.x[:, i, :], m.x[:, i, :], h2[:, i, :], ALU.add).then_inc(added, 1)
            v.wait_ge(sum_sb, 8)
            v.scalar_tensor_tensor(r_ffn, rows[:, 2 * D:3 * D], 1.0, r_ffn, ALU.add, ALU.mult).then_inc(row_mul, 1)
            v.tensor_tensor(m.r_g2[:], rows[:, 3 * D:4 * D], r_fpost, ALU.mult).then_inc(row_mul, 1)
            v.wait_ge(x_std, 1)
            v.reciprocal(stats[:, 6:8], stats[:, 6:8]).then_inc(x_inv, 1)
            v.wait_ge(x_inv, 1)
            v.wait_ge(row_mul, 3)
            v.wait_ge(added, 2)
            for i in range(QT):
                v.scalar_tensor_tensor(h2[:, i, :], m.x[:, i, :], stats[:, 6 + i:7 + i], r_ffn, ALU.mult, ALU.mult).then_inc(h2_mul, 1)
                v.wait_ge(h2_mul, i + 1)
                v.tensor_tensor(h2[:, i, :], h2[:, i, :], rows[:, D:2 * D], ALU.add).then_inc(h2_ready, 1)


def stage_route(nc, m, t):
    s = m.moe
    m.keys = s.sb("keys", [P, QT, PASSES])
    m.gates = s.sb("gates", [P, QT, PASSES])
    m.brows = s.sb("brows", [P, 3, D])
    m.pick = s.sb("pick", [P, PASSES])
    m.table = s.sb("table", [1, PASSES + 1 + EXPERTS], I32)
    m.ysum = s.sb("ysum", [P, QT, D])
    r = Memory(nc)
    wr, br = m.wr, m.br
    logit = r.sb("logit", [P, QT, EXPERTS])
    best = r.sb("best", [P, QT, 8])
    index = r.sb("index", [P, QT, 8], U32)
    indexf = r.sb("indexf", [P, QT, 8])
    mask = r.sb("mask", [P, QT, EXPERTS])
    gate = r.sb("gate", [P, QT, EXPERTS])
    gsum = r.sb("gsum", [P, 2 * QT])
    key = r.sb("key", [P, QT, EXPERTS])
    keyT = r.sb("keyT", [EXPERTS, QT, P])
    gateT = r.sb("gateT", [EXPERTS, QT, P])
    more = r.sb("more", [EXPERTS, 4])
    tmp = r.sb("tmp", [EXPERTS, 3, PASSES])
    pick = m.pick[0:EXPERTS, :]
    base = r.sb("base", [EXPERTS, PASSES])
    ps = m.ps
    logit_ps, logit_sb, top8, top_i, top_f, picked, peak, exped = (
        m.sem(n) for n in ("logit_ps", "logit_sb", "top8", "top_i", "top_f", "picked", "peak", "exped"))
    g_chain, rank_ps, key_ok, more_chain, more_ps, table_ok, turned_ps, turned_sb, spread_ps, spread_sb = (
        m.sem(n) for n in ("g_chain", "rank_ps", "key_ok", "more_chain", "more_ps", "table_ok", "turned_ps", "turned_sb",
                           "spread_ps", "spread_sb"))
    zeroed = m.sem("zeroed")
    m.brows_in = m.lasting("brows_in")

    with nc.Block() as block:

        @block.gpsimd
        def _(pool):
            m.clear_last(pool)
            pool.memset(m.brows[:], 0.0).then_inc(zeroed, 1)
            pool.memset(m.pick[:], 0.0).then_inc(zeroed, 1)
            pool.memset(m.ysum[:], 0.0).then_inc(zeroed, 1)

        @block.sync
        def _(sp):
            load_expert0(sp, m, t, (0, 1, 2, 10, 11))
            sp.wait_ge(zeroed, 2)
            for j, name in enumerate(("b_gate", "b_up", "b_down")):
                sp.dma_start(m.brows[0:EXPERTS, j, :], t[name][0]).then_inc(m.brows_in, 16)

        @block.tensor
        def _(pe):
            ident, ones = cst(m, "ident"), cst(m, "ones")
            pe.wait_ge(m.router_in, 32)
            for i in range(QT):
                for c in range(C):
                    pe.matmul(ps[:, 0, i * EXPERTS:(i + 1) * EXPERTS], m.hT[:, c, i * P:(i + 1) * P], wr[:, c, :], start=(c == 0), stop=False)
                mm = pe.matmul(ps[:, 0, i * EXPERTS:(i + 1) * EXPERTS], ones[0:1, :], br[:], start=False, stop=True)
            mm.then_inc(logit_ps, 1)
            pe.wait_ge(picked, 8)
            for i in range(QT):
                for j in range(QT):
                    pe.matmul(ps[:, 1, i * EXPERTS:(i + 1) * EXPERTS], cst(m, "stri", P, j * SEQ + i * P, P), mask[:, j, :],
                              start=(j == 0), stop=(j == QT - 1))
            for j in range(QT):
                pe.matmul(ps[0:EXPERTS, 2, 0:1], mask[:, j, :], ones[:, 0:1], start=(j == 0), stop=(j == QT - 1))
            pe.matmul(ps[0:EXPERTS, 2, 1:2], cst(m, "etri", EXPERTS), ones[0:EXPERTS, 0:1], start=True, stop=True).then_inc(rank_ps, 1)
            pe.wait_ge(more_chain, 5)
            pe.matmul(ps[0:EXPERTS, 2, 2:3], cst(m, "etri", EXPERTS), more[:, 1:2], start=True, stop=True)
            pe.matmul(ps[0:1, 3, PASSES:PASSES + 1], more[:, 1:2], ones[0:EXPERTS, 0:1], start=True, stop=True)
            pe.matmul(ps[0:1, 3, PASSES + 1:PASSES + 1 + EXPERTS], more[:, 1:2], cst(m, "etri", EXPERTS), start=True, stop=True).then_inc(more_ps, 1)
            pe.wait_ge(key_ok, 1)
            pe.wait_ge(g_chain, 5)
            for i in range(QT):
                pe.transpose(ps[0:EXPERTS, 4, i * P:(i + 1) * P], key[:, i, :], ident)
                mm = pe.transpose(ps[0:EXPERTS, 4, (2 + i) * P:(3 + i) * P], gate[:, i, :], ident)
            mm.then_inc(turned_ps, 1)
            pe.wait_ge(more_chain, 9)
            pe.matmul(ps[0:1, 3, 0:PASSES], more[:, 3:4], pick, start=True, stop=True).then_inc(more_ps, 1)
            pe.wait_ge(turned_sb, 2)
            pe.wait_ge(more_chain, 10)
            for i in range(QT):
                pe.matmul(ps[:, 5, i * PASSES:(i + 1) * PASSES], keyT[:, i, :], pick, start=True, stop=False)
                pe.matmul(ps[:, 5, i * PASSES:(i + 1) * PASSES], ones[0:EXPERTS, :], base[:], start=False, stop=True)
                mm = pe.matmul(ps[:, 5, (2 + i) * PASSES:(3 + i) * PASSES], gateT[:, i, :], pick, start=True, stop=True)
            mm.then_inc(spread_ps, 1)

        @block.scalar
        def _(act):
            act.wait_ge(peak, 2)
            act.wait_ge(logit_sb, 1)
            for i in range(QT):
                act.activation(gate[:, i, :], logit[:, i, :], ACT.Exp, bias=gsum[:, i:i + 1]).then_inc(exped, 1)
            act.wait_ge(turned_ps, 1)
            act.copy(keyT[:].rearrange("e i n -> e (i n)"), ps[0:EXPERTS, 4, 0:SEQ]).then_inc(turned_sb, 1)
            act.copy(gateT[:].rearrange("e i n -> e (i n)"), ps[0:EXPERTS, 4, SEQ:2 * SEQ]).then_inc(turned_sb, 1)

        @block.vector
        def _(v):
            iota = cst(m, "iota")
            v.wait_ge(logit_ps, 1)
            v.tensor_copy(logit[:].rearrange("p i n -> p (i n)"), ps[:, 0, 0:QT * EXPERTS]).then_inc(logit_sb, 1)
            v.wait_ge(logit_sb, 1)
            for i in range(QT):
                v.max(best[:, i, :], logit[:, i, :]).then_inc(top8, 1)
            v.wait_ge(top8, 2)
            for i in range(QT):
                v.max_index(index[:, i, :], best[:, i, :], logit[:, i, :]).then_inc(top_i, 1)
                v.tensor_scalar(gsum[:, i:i + 1], best[:, i, 0:1], -1.0, None, ALU.mult).then_inc(peak, 1)
            v.wait_ge(top_i, 2)
            v.tensor_copy(indexf[:], index[:]).then_inc(top_f, 1)
            v.wait_ge(top_f, 1)
            for k in range(TOPK):
                for i in range(QT):
                    if k == 0:
                        v.tensor_scalar(mask[:, i, :], iota[:, 0:EXPERTS], indexf[:, i, 0:1], None, ALU.is_equal).then_inc(picked, 1)
                    else:
                        v.wait_ge(picked, QT * k)
                        v.scalar_tensor_tensor(mask[:, i, :], iota[:, 0:EXPERTS], indexf[:, i, k:k + 1], mask[:, i, :],
                                               ALU.is_equal, ALU.add).then_inc(picked, 1)
            v.wait_ge(exped, 2)
            v.wait_ge(picked, 8)
            v.tensor_tensor(gate[:], gate[:], mask[:], ALU.mult).then_inc(g_chain, 1)
            v.wait_ge(g_chain, 1)
            v.tensor_reduce(gsum[:, QT:2 * QT], gate[:], AX, ALU.add).then_inc(g_chain, 1)
            v.wait_ge(g_chain, 2)
            v.reciprocal(gsum[:, QT:2 * QT], gsum[:, QT:2 * QT]).then_inc(g_chain, 1)
            v.wait_ge(g_chain, 3)
            for i in range(QT):
                v.tensor_scalar(gate[:, i, :], gate[:, i, :], gsum[:, QT + i:QT + i + 1], None, ALU.mult).then_inc(g_chain, 1)
            v.wait_ge(rank_ps, 1)
            v.tensor_copy(more[:, 0:1], ps[0:EXPERTS, 2, 0:1])
            v.tensor_copy(more[:, 3:4], ps[0:EXPERTS, 2, 1:2]).then_inc(more_chain, 1)
            v.wait_ge(more_chain, 1)
            v.tensor_scalar(more[:, 1:2], more[:, 0:1], float(SLOTS), 1.0, ALU.is_gt, ALU.add).then_inc(more_chain, 1)
            for n in range(2, SEQ // SLOTS):
                v.wait_ge(more_chain, n)
                v.scalar_tensor_tensor(more[:, 1:2], more[:, 0:1], float(n * SLOTS), more[:, 1:2], ALU.is_gt, ALU.add).then_inc(more_chain, 1)
            v.wait_ge(zeroed, 2)
            v.wait_ge(more_chain, SEQ // SLOTS)
            v.sem_inc(more_chain, 1)
            v.scalar_tensor_tensor(key[:].rearrange("p i n -> p (i n)"), ps[:, 1, 0:QT * EXPERTS], 1.0,
                                   mask[:].rearrange("p i n -> p (i n)"), ALU.add, ALU.mult).then_inc(table_ok, 1)
            v.wait_ge(table_ok, 1)
            v.tensor_scalar(key[:], key[:], -1.0, None, ALU.add).then_inc(key_ok, 1)
            v.wait_ge(more_ps, 1)
            v.tensor_copy(more[:, 2:3], ps[0:EXPERTS, 2, 2:3]).then_inc(more_chain, 1)
            v.wait_ge(more_chain, 6)
            v.tensor_scalar(tmp[:, 0, :], iota[0:EXPERTS, 0:PASSES], more[:, 2:3], None, ALU.subtract).then_inc(more_chain, 1)
            v.wait_ge(more_chain, 7)
            v.tensor_scalar(tmp[:, 1, :], tmp[:, 0, :], more[:, 1:2], None, ALU.is_lt).then_inc(more_chain, 1)
            v.wait_ge(more_chain, 8)
            v.scalar_tensor_tensor(pick, tmp[:, 0, :], 0.0, tmp[:, 1, :], ALU.is_ge, ALU.mult).then_inc(more_chain, 1)
            v.wait_ge(more_chain, 9)
            v.scalar_tensor_tensor(base[:], tmp[:, 0, :], float(-SLOTS), pick, ALU.mult, ALU.mult).then_inc(more_chain, 1)
            v.wait_ge(more_ps, 2)
            v.tensor_copy(m.table[:, 0:PASSES + 1], ps[0:1, 3, 0:PASSES + 1])
            v.tensor_scalar(m.table[:, PASSES + 1:], ps[0:1, 3, PASSES + 1:PASSES + 1 + EXPERTS], -1.0, None, ALU.add).then_inc(table_ok, 1)
            v.wait_ge(spread_ps, 1)
            v.tensor_copy(m.keys[:].rearrange("p i n -> p (i n)"), ps[:, 5, 0:2 * PASSES]).then_inc(spread_sb, 1)
            v.tensor_copy(m.gates[:].rearrange("p i n -> p (i n)"), ps[:, 5, 2 * PASSES:4 * PASSES]).then_inc(spread_sb, 1)
    r.stack.close()


def expert_rows(t, e, k):
    w = t[("w_gate", "w_up", "w_down")[k // 4]]
    k %= 4
    if isinstance(e, int):
        return w[0, e, k * 256:(k + 1) * 256, :].rearrange("(a p) n -> p a n", p=P)
    return w[0, bass.ds(e, 1), k * 256:(k + 1) * 256, :].rearrange("e (a p) n -> p (e a) n", p=P)


def stage_experts(nc, m, t):
    s = m.moe
    h2, ps, ysum = m.h2, m.ps, m.ysum
    sel = s.sb("sel", [P, QT, SLOTS])
    selg = s.sb("selg", [P, QT, 3 * SLOTS])
    selT = s.sb("selT", [P, QT, 2, P])
    now = s.sb("now", [P, SLOTS])
    xs = s.sb("xs", [P, C, SLOTS])
    g = s.sb("g", [P, 512])
    u = s.sb("u", [P, 512])
    sig = s.sb("sig", [P, 512])
    actT = s.sb("actT", [P, 4, P])
    y = s.sb("y", [P, 512])
    stats = s.sb("stats2", [P, 4])
    moe_in = m.moe_in
    m.even_in = [m.lasting(f"even_in{k}") for k in range(5)]
    X, G, U, TURN, COMB = 0, 1, 2, 3, 4
    SELT, Y = G, U
    bias_ps = m.sem("bias_ps")
    w_free, gather_ps, gate_ps, up_ps, down_ps, comb_ps, actT_ps = (
        m.sem(n) for n in ("w_free", "gather_ps", "gate_ps", "up_ps", "down_ps", "comb_ps", "actT_ps"))
    zeroed, sel_ok, now_ok, g_ok, u_ok, act_mul, act_ok, y_added = (
        m.sem(n) for n in ("zeroed2", "sel_ok", "now_ok", "g_ok", "u_ok", "act_mul", "act_ok", "y_added"))
    sig_ok, xs_sb, selT_sb, actT_sb, y_sb = (m.sem(n) for n in ("sig_ok", "xs_sb", "selT_sb", "actT_sb", "y_sb"))
    ysq, ystd, yinv, ymul, x2_done = (m.sem(n) for n in ("ysq", "ystd", "yinv", "ymul", "x2_done"))

    def passes(eng):
        return eng.value_load(m.table[0:1, PASSES:PASSES + 1], min_val=EXPERTS, max_val=EXPERTS + SPARE)

    with nc.Block() as block:

        @block.gpsimd
        def _(pool):
            m.clear_last(pool)
            pool.memset(selg[:], 0.0).then_inc(zeroed, 1)

        @block.sync
        def _(sp):
            with sp.Fori(1, EXPERTS) as e:
                last = sp.value_load(m.table[0:1, bass.ds(e + (PASSES + 1), 1)], min_val=0, max_val=EXPERTS + SPARE)
                for k in range(12):
                    if k < 11:
                        sp.wait_ge(w_free, last * 11 + (k + 1))
                    else:
                        sp.wait_ge(down_ps, last + 1)
                    sp.dma_start(m.ring[:, 2 * k:2 * k + 2, :], expert_rows(t, e, k)).then_inc(moe_in[k], 16)

            n = passes(sp)
            src = stack(t["even_w_in_2"][0])
            for k, lo in enumerate((MQ, MK, NQ)):
                if k == 0:
                    sp.wait_ge(gate_ps, n)
                elif k == 2:
                    sp.wait_ge(up_ps, n)
                w = m.ring[:, 4 * k:4 * k + 4, :].rearrange("p a n -> p (a n)").rearrange("p (c n) -> p c n", c=C)
                sp.dma_start(w, src[:, :, lo:lo + 512]).then_inc(m.even_in[k], 16)

        @block.tensor
        def _(pe):
            ident = cst(m, "ident")
            n = passes(pe)

            def gather():
                for c in range(C):
                    for i in range(QT):
                        mm = pe.matmul(ps[:, X, c * SLOTS:(c + 1) * SLOTS], h2[:, i, c * P:(c + 1) * P], sel[:, i, :],
                                       start=(i == 0), stop=(i == QT - 1))
                return mm

            def expand(bank, part, landed, done):
                for c in range(C):
                    if c % 2 == 0:
                        pe.wait_ge(moe_in[4 * part + c // 2], landed)
                    for half in range(2):
                        mm = pe.matmul(ps[SLOTS * half:SLOTS * (half + 1), bank, :], xs[:, c, :],
                                       m.ring[:, 8 * part + c, half * 512:(half + 1) * 512], start=(c == 0), stop=False)
                    if c % 2 == 1:
                        mm.then_inc(w_free, 1)
                for half in range(2):
                    mm = pe.matmul(ps[SLOTS * half:SLOTS * (half + 1), bank, :], now[:], m.brows[:, part, half * 512:(half + 1) * 512],
                                   start=False, stop=True)
                mm.then_inc(done, 1)

            def combine():
                for i in range(QT):
                    for half in range(2):
                        mm = pe.matmul(ps[:, COMB + 2 * i + half, :], selT[:, i, half, :], y[:], start=True, stop=True)
                    mm.then_inc(comb_ps, 1)

            pe.wait_ge(m.brows_in, 48)
            pe.wait_ge(sel_ok, 1)
            gather().then_inc(gather_ps, 1)
            with pe.Fori(0, n) as i:
                landed = pe.value_load(m.table[0:1, bass.ds(i, 1)], min_val=0, max_val=EXPERTS - 1) * 16 + 16
                pe.wait_ge(xs_sb, i + 1)
                pe.wait_ge(now_ok, i + 1)
                pe.wait_ge(selT_sb, i + 1)
                expand(G, 0, landed, gate_ps)
                pe.wait_ge(y_sb, i + 1)
                expand(U, 1, landed, up_ps)
                pe.wait_ge(sel_ok, i + 2)
                gather()
                pe.wait_ge(g_ok, i + 1)
                for j in range(QT):
                    for low in range(2):
                        a = SLOTS * (1 - low)
                        mm = pe.transpose(ps[:, SELT, (2 * j + low) * P:(2 * j + low + 1) * P], selg[:, j, a:a + P], ident)
                mm.then_inc(gather_ps, 1)
                pe.wait_ge(act_ok, i + 1)
                for b in range(4):
                    mm = pe.transpose(ps[:, TURN, b * P:(b + 1) * P], g[:, b * P:(b + 1) * P], ident)
                mm.then_inc(actT_ps, 1)
                combine()
                for half in range(2):
                    mm = pe.matmul(ps[SLOTS * half:SLOTS * (half + 1), Y, :], now[:], m.brows[:, 2, half * 512:(half + 1) * 512],
                                   start=True, stop=False)
                mm.then_inc(bias_ps, 1)
                pe.wait_ge(actT_sb, i + 1)
                for f in range(C):
                    if f % 2 == 0:
                        pe.wait_ge(moe_in[8 + f // 2], landed)
                    for half in range(2):
                        mm = pe.matmul(ps[SLOTS * half:SLOTS * (half + 1), Y, :], actT[:, f % 4, f // 4 * SLOTS:(f // 4 + 1) * SLOTS],
                                       m.ring[:, 16 + f, half * 512:(half + 1) * 512], start=False, stop=(f == C - 1))
                    if f == C - 1:
                        mm.then_inc(down_ps, 1)
                    elif f % 2 == 1:
                        mm.then_inc(w_free, 1)
            pe.wait_ge(y_sb, n + 1)
            pe.wait_ge(selT_sb, n + 1)
            pe.wait_ge(y_added, n * 2)
            combine()

        @block.scalar
        def _(act):
            n = passes(act)
            zero = cst(m, "iota", P, 0, 1).to_broadcast([P, 512])
            act.activation(y[:], zero, ACT.Copy, scale=0.0).then_inc(y_sb, 1)
            act.activation(selT[:].rearrange("p i h n -> p (i h n)"), zero, ACT.Copy, scale=0.0).then_inc(selT_sb, 1)
            act.wait_ge(gather_ps, 1)
            act.copy(xs[:].rearrange("p c n -> p (c n)"), ps[:, X, :]).then_inc(xs_sb, 1)
            with act.Fori(0, n) as i:
                act.wait_ge(g_ok, i + 1)
                act.activation(sig[:], g[:], ACT.Sigmoid, scale=ALPHA).then_inc(sig_ok, 1)
                act.wait_ge(gather_ps, i + 2)
                act.copy(xs[:].rearrange("p c n -> p (c n)"), ps[:, X, :]).then_inc(xs_sb, 1)
                act.wait_ge(actT_ps, i + 1)
                act.copy(actT[:].rearrange("p b n -> p (b n)"), ps[:, TURN, :]).then_inc(actT_sb, 1)
                act.wait_ge(comb_ps, i * 2 + 2)
                act.copy(selT[:].rearrange("p i h n -> p (i h n)"), ps[:, SELT, :]).then_inc(selT_sb, 1)
                act.wait_ge(down_ps, i + 1)
                act.copy(y[:], ps[:, Y, :]).then_inc(y_sb, 1)
            for i in range(QT):
                act.wait_ge(y_added, n * 2 + (i + 1))
                if i:
                    act.wait_ge(ysq, i)
                act.activation(h2[:, 0, :], ysum[:, i, :], ACT.Square, accum_out=stats[:, i:i + 1]).then_inc(ysq, 1)
            act.wait_ge(ysq, 2)
            act.activation(stats[:, 2:4], stats[:, 0:2], ACT.Sqrt, scale=1.0 / D, bias=m.eps[:, 0:1]).then_inc(ystd, 1)

        @block.vector
        def _(v):
            n = passes(v)
            iota = cst(m, "iota", P, 0, SLOTS)

            def add(i):
                v.tensor_tensor(ysum[:, i, :], ysum[:, i, :], ps[:, COMB + 2 * i:COMB + 2 * i + 2, :].rearrange("p a n -> p (a n)"),
                                ALU.add).then_inc(y_added, 1)

            for j in range(QT):
                ins = v.tensor_scalar(sel[:, j, :], iota, m.keys[:, j, 0:1], None, ALU.is_equal)
            ins.then_inc(sel_ok, 1)
            v.tensor_copy(now[:], m.pick[:, 0:1].to_broadcast([P, SLOTS])).then_inc(now_ok, 1)
            v.wait_ge(zeroed, 1)
            with v.Fori(0, n) as i:
                v.wait_ge(gather_ps, i + 1)
                for j in range(QT):
                    v.tensor_scalar(selg[:, j, SLOTS:2 * SLOTS], iota, m.keys[:, j, bass.ds(i, 1)], m.gates[:, j, bass.ds(i, 1)],
                                    ALU.is_equal, ALU.mult)
                    ins = v.tensor_scalar(sel[:, j, :], iota, m.keys[:, j, bass.ds(i + 1, 1)], None, ALU.is_equal)
                ins.then_inc(sel_ok, 1)
                v.wait_ge(gate_ps, i + 1)
                v.tensor_scalar(g[:], ps[:, G, :], LIMIT, None, ALU.min).then_inc(g_ok, 1)
                v.wait_ge(up_ps, i + 1)
                v.tensor_scalar(u[:], ps[:, U, :], -LIMIT, LIMIT, ALU.max, ALU.min).then_inc(u_ok, 1)
                v.wait_ge(u_ok, i + 1)
                v.scalar_tensor_tensor(u[:], u[:], 1.0, g[:], ALU.add, ALU.mult).then_inc(act_mul, 1)
                v.wait_ge(act_mul, i + 1)
                v.wait_ge(sig_ok, i + 1)
                v.tensor_tensor(g[:], u[:], sig[:], ALU.mult).then_inc(act_ok, 1)
                for j in range(QT):
                    v.wait_ge(comb_ps, i * 2 + (j + 1))
                    add(j)
                v.wait_ge(bias_ps, i + 1)
                v.tensor_copy(now[:], m.pick[:, bass.ds(i + 1, 1)].to_broadcast([P, SLOTS])).then_inc(now_ok, 1)
            for j in range(QT):
                v.wait_ge(comb_ps, n * 2 + (j + 1))
                add(j)
            v.wait_ge(ystd, 1)
            v.reciprocal(stats[:, 2:4], stats[:, 2:4]).then_inc(yinv, 1)
            v.wait_ge(yinv, 1)
            for i in range(QT):
                v.scalar_tensor_tensor(ysum[:, i, :], ysum[:, i, :], stats[:, 2 + i:3 + i], m.r_g2[:], ALU.mult, ALU.mult).then_inc(ymul, 1)
                v.wait_ge(ymul, i + 1)
                v.tensor_tensor(m.x[:, i, :], m.x[:, i, :], ysum[:, i, :], ALU.add).then_inc(x2_done, 1)
    s.stack.close()


class Norm:

    def __init__(self, m, mem, name, eps, weight):
        self.m, self.eps, self.weight = m, eps, weight
        self.xn = mem.sb(f"{name}_xn", [P, QT, D])
        self.stats = mem.sb(f"{name}_st", [P, 2 * QT])
        self.sq, self.std, self.inv, self.ready, self.ps, self.hT_a, self.hT_v = (
            m.sem(f"{name}_{n}") for n in ("sq", "std", "inv", "ready", "ps", "hT_a", "hT_v"))

    def scalar_stats(self, act, x_ready=None):
        for i in range(QT):
            if x_ready is not None:
                act.wait_ge(x_ready, i + 1)
            act.activation(self.xn[:, i, :], self.m.x[:, i, :], ACT.Square, accum_out=self.stats[:, i:i + 1]).then_inc(self.sq, 1)
        act.wait_ge(self.sq, QT)
        act.activation(self.stats[:, QT:2 * QT], self.stats[:, 0:QT], ACT.Sqrt, scale=1.0 / D,
                       bias=self.m.eps[:, self.eps:self.eps + 1]).then_inc(self.std, 1)

    def vector_scale(self, v):
        v.wait_ge(self.std, 1)
        v.reciprocal(self.stats[:, QT:2 * QT], self.stats[:, QT:2 * QT]).then_inc(self.inv, 1)
        v.wait_ge(self.inv, 1)
        for i in range(QT):
            v.tensor_scalar(self.xn[:, i, :], self.m.x[:, i, :], self.stats[:, QT + i:QT + i + 1], None, ALU.mult).then_inc(self.ready, 1)

    def tensor_turn(self, pe):
        for i in range(QT):
            pe.wait_ge(self.ready, i + 1)
            for c in range(C):
                mm = pe.transpose(self.m.ps[:, c // 2, (c % 2) * SEQ + i * P:(c % 2) * SEQ + (i + 1) * P],
                                  self.xn[:, i, c * P:(c + 1) * P], cst(self.m, "ident"))
        mm.then_inc(self.ps, 1)

    def _tile(self, c):
        return self.m.hT[:, c, :], self.m.ps[:, c // 2, (c % 2) * SEQ:(c % 2 + 1) * SEQ], col(self.m, self.weight[0], self.weight[1] + c)

    def scalar_weigh(self, act):
        act.wait_ge(self.ps, 1)
        for c in range(0, C, 4):
            for d in (0, 1):
                out, src, w = self._tile(c + d)
                act.activation(out, src, ACT.Copy, scale=w).then_inc(self.hT_a, 1)

    def vector_weigh(self, v):
        v.wait_ge(self.ps, 1)
        for c in range(2, C, 4):
            for d in (0, 1):
                out, src, w = self._tile(c + d)
                v.tensor_scalar(out, src, w, None, ALU.mult).then_inc(self.hT_v, 1)

    def wait_turned(self, eng):
        eng.wait_ge(self.hT_a, 4)
        eng.wait_ge(self.hT_v, 4)


def stage_even_project(nc, m, t):
    s = m.even = Memory(nc)
    m.mqT, m.nqT = (s.sb(n, [P, 4, 2, SEQ]) for n in ("mqT", "nqT"))
    m.mkT = s.sb("mkT", [P, 4, SEQ])
    m.mv = s.sb("mv", [P, QT, 512])
    m.kcT, m.vcT = (s.sb(n, [P, 2, SEQ]) for n in ("kcT", "vcT"))
    m.kslT, m.kwnT = (s.sb(n, [P, SEQ]) for n in ("kslT", "kwnT"))
    m.nv = s.sb("nv", [P, QT, 280])
    W = [m.ring[:, 4 * k:4 * k + 4, :].rearrange("p a n -> p (a n)").rearrange("p (c n) -> p c n", c=C) for k in range(5)]
    ps = m.ps
    w_in = m.even_in
    m.toe = m.ring[:, 0:8, :].rearrange("p a n -> p (a n)").rearrange("p (h i n) -> p h i n", h=16, i=QT)
    m.cmp_w1 = m.ring[:, 8:16, :].rearrange("p a n -> p (a n)").rearrange("p (s j n) -> p s j n", s=2, j=16)
    m.pos = s.sb("pos", [P, 2, 16])
    m.w2k = s.sb("w2k", [P, 2, P])
    m.w2v = s.sb("w2v", [P, 2, HD])
    r = Memory(nc)
    wv = r.sb("wv", [P, C, 280])
    norm = Norm(m, r, "n0", 1, ("mix", 0))
    m.small_in, m.toe_in, m.w1_in, m.eout_in = (m.lasting(n) for n in ("small_in", "toe_in", "w1_in", "eout_in"))
    wv_in = m.sem("even_wv_in")
    proj_ps, sb_a, zeroed = m.sem("even_ps"), m.sem("even_sb"), m.sem("even_zeroed")
    tiles = [(128 * j, m.mqT[:, j, :, :], HD ** -0.5) for j in range(4)]
    tiles += [(512 + 128 * j, m.mkT[:, j, :], 1.0) for j in range(4)]
    tiles += [(1024 + 128 * j, m.nqT[:, j, :, :], HD ** -0.5) for j in range(4)]
    tiles += [(1536 + 128 * j, dst[:], None) for j, dst in enumerate((m.kcT, m.vcT, m.kslT, m.kwnT))]

    with nc.Block() as block:

        @block.gpsimd
        def _(pool):
            m.clear_last(pool)
            pool.memset(m.mqT[:], 0.0).then_inc(zeroed, 1)
            pool.memset(m.nqT[:], 0.0).then_inc(zeroed, 1)

        @block.sync
        def _(sp):
            src = stack(t["even_w_in_2"][0])
            for a, lo, n in ((0, VSL, 128), (128, VWN, 128), (256, GZ, 24)):
                sp.dma_start(wv[:, :, a:a + n], src[:, :, lo:lo + n]).then_inc(wv_in, 16)
            for k, lo in enumerate((KC, VC, KSL, KWN)):
                sp.dma_start(W[3][:, :, P * k:P * (k + 1)], src[:, :, lo:lo + P]).then_inc(w_in[3], 16)
            sp.dma_start(W[4], src[:, :, MV:MV + 512]).then_inc(w_in[4], 16)
            with nc.allow_non_contiguous_dma(reason="small columns"):
                for j, name in enumerate(("cmp_pos_k_2", "cmp_pos_v_2")):
                    flat = bass.AP(t[name].tensor, 0, [[1, P], [P, 16]])
                    sp.dma_start(m.pos[:, j, :], flat).then_inc(m.small_in, 16)
            for twice in range(2):
                sp.dma_start(m.w2k[:, :, HD * twice:HD * (twice + 1)], stack(t["cmp_k_w2_2"][0])).then_inc(m.small_in, 16)
            sp.dma_start(m.w2v[:], stack(t["cmp_v_w2_2"][0])).then_inc(m.small_in, 16)
            sp.wait_ge(m.toeplitz_out, 16)
            sp.wait_ge(proj_ps, 8)
            for i in range(QT):
                rows = bass.AP(t["toeplitz"].tensor, SEQ - 1 - P * i, [[510, P], [P * 512, 16], [1, SEQ]])
                sp.dma_start(m.toe[:, :, i, :], rows).then_inc(m.toe_in, 16)
            sp.wait_ge(proj_ps, 16)
            for j, name in enumerate(("cmp_k_w1_2", "cmp_v_w1_2")):
                sp.dma_start(m.cmp_w1[:, j, :, :], stack(t[name][0])).then_inc(m.w1_in, 16)
            sp.wait_ge(proj_ps, len(tiles) + 2)
            sp.dma_start(m.ring[:, 16:24, :], stack(t["even_w_out_2"][0])).then_inc(m.eout_in, 16)

        @block.tensor
        def _(pe):
            norm.tensor_turn(pe)
            norm.wait_turned(pe)
            for n, (at, _, _) in enumerate(tiles):
                if n % 4 == 0:
                    pe.wait_ge(w_in[n // 4], 16 if n < 12 else 64)
                if n >= 8:
                    pe.wait_ge(sb_a, n - 7)
                for c in range(C):
                    mm = pe.matmul(ps[:, n % 8, 0:SEQ], W[n // 4][:, c, at % 512:at % 512 + P], m.hT[:, c, :], start=(c == 0), stop=(c == C - 1))
                mm.then_inc(proj_ps, 1)
            pe.wait_ge(w_in[4], 16)
            pe.wait_ge(wv_in, 48)
            for k in range(4):
                i = k % 2
                pe.wait_ge(sb_a, len(tiles) - 8 + k + 1)
                b = (len(tiles) + k) % 8
                for c in range(C):
                    w = W[4][:, c, :] if k < 2 else wv[:, c, :]
                    mm = pe.matmul(ps[:, b, 0:w.shape[1]], m.hT[:, c, i * P:(i + 1) * P], w, start=(c == 0), stop=(c == C - 1))
                mm.then_inc(proj_ps, 1)

        @block.scalar
        def _(act):
            norm.scalar_stats(act)
            norm.scalar_weigh(act)
            for n, (_, dst, scale) in enumerate(tiles):
                act.wait_ge(proj_ps, n + 1)
                b = n % 8
                if n in (12, 13):
                    for g in range(2):
                        act.copy(dst[0:HD, g, :], ps[HD * g:HD * (g + 1), b, 0:SEQ])
                        ins = act.copy(dst[HD:P, g, 0:SEQ - 1], ps[HD * g:HD * (g + 1), b, 1:SEQ])
                    ins.then_inc(sb_a, 1)
                elif scale is None or scale == 1.0:
                    act.copy(dst, ps[:, b, 0:SEQ]).then_inc(sb_a, 1)
                else:
                    if n == 0:
                        act.wait_ge(zeroed, 2)
                    for hd in range(2):
                        half = hd if n < 8 else (n - 8) // 2
                        ins = act.mul(dst[HD * half:HD * (half + 1), hd, :], ps[HD * hd:HD * (hd + 1), b, 0:SEQ], scale)
                    ins.then_inc(sb_a, 1)
            for k in range(4):
                act.wait_ge(proj_ps, len(tiles) + k + 1)
                b = (len(tiles) + k) % 8
                dst = m.mv[:, k, :] if k < 2 else m.nv[:, k - 2, :]
                act.copy(dst, ps[:, b, 0:dst.shape[1]]).then_inc(sb_a, 1)

        @block.vector
        def _(v):
            norm.vector_scale(v)
            norm.vector_weigh(v)
    r.stack.close()


class Unit:

    def __init__(self, scores, bias, values, keys, gate, first, last, out):
        self.scores, self.bias, self.values, self.keys = scores, bias, values, keys
        self.gate, self.first, self.last, self.out = gate, first, last, out


class Attention:

    def __init__(self, m, mem, name, units):
        self.m, self.units = m, units
        self.prob = mem.sb(f"{name}_prob", [P, 3, 4 * SEQ])
        self.probT = mem.sb(f"{name}_probT", [P, 2, 4 * SEQ])
        self.top = mem.sb(f"{name}_top", [P, len(units), 8])
        (self.s_ps, self.biased, self.peak, self.neg, self.exped, self.inv, self.gated, self.ready, self.pt_ps, self.pt_sb,
         self.pv_ps, self.pv_sb) = (m.sem(f"{name}_{n}") for n in (
             "s_ps", "biased", "peak", "neg", "exped", "inv", "gated", "ready", "pt_ps", "pt_sb", "pv_ps", "pv_sb"))
        self.pair, n = [], 0
        for u in units:
            self.pair.append(n)
            n += u.last

    def scores_of(self, u):
        K, b = self.units[u].keys, 2 * (u % 2)
        return self.m.ps[:, b:b + 2, 0:QT * K].rearrange("p h (i n) -> p h i n", i=QT)

    def prob_of(self, u):
        return self.prob[:, u % 3, 0:4 * self.units[u].keys].rearrange("p (h i n) -> p h i n", h=2, i=QT)

    def tensor(self, pe, between=None):
        ps, ident = self.m.ps, cst(self.m, "ident")

        def scores(u):
            if u >= 2:
                pe.wait_ge(self.biased, u - 1)
            unit, S = self.units[u], self.scores_of(u)
            for hd in range(2):
                for i in range(QT):
                    mm = unit.scores(pe, S[:, hd, i, :], hd, i)
            mm.then_inc(self.s_ps, 1)

        for u in range(2):
            scores(u)
        if between is not None:
            between()
        def turn(u):
            K, prob = self.units[u].keys, self.prob_of(u)
            pe.wait_ge(self.ready, u + 1)
            if u:
                pe.wait_ge(self.pt_sb, u)
            if K == SEQ:
                for k in range(2):
                    for j in range(4):
                        mm = pe.transpose(ps[:, 4 + k, j * P:(j + 1) * P], prob[:, j // 2, j % 2, k * P:(k + 1) * P], ident)
            else:
                for j in range(4):
                    mm = pe.transpose(ps[0:K, 4, j * P:(j + 1) * P], prob[:, j // 2, j % 2, :], ident)
            mm.then_inc(self.pt_ps, 1)

        def weigh(u):
            unit, n = self.units[u], self.pair[u]
            pe.wait_ge(self.pt_sb, u + 1)
            if unit.first and n >= 2:
                pe.wait_ge(self.pv_sb, n - 1)
            rows, tiles = min(unit.keys, P), max(1, unit.keys // P)
            for k in range(tiles):
                for hd in range(2):
                    mm = pe.matmul(ps[HD * hd:HD * (hd + 1), 6 + n % 2, 0:SEQ], unit.values(hd, k),
                                   self.probT[0:rows, u % 2, k * 512 + hd * SEQ:k * 512 + (hd + 1) * SEQ],
                                   start=(unit.first and k == 0), stop=(unit.last and k == tiles - 1))
            mm.then_inc(self.pv_ps, 1)

        for u in range(len(self.units)):
            if u + 2 < len(self.units):
                scores(u + 2)
            turn(u)
            if u:
                weigh(u - 1)
        weigh(len(self.units) - 1)

    def scalar(self, act, between=None):
        ps = self.m.ps

        def exp(u):
            act.wait_ge(self.neg, u + 1)
            for j in range(4):
                ins = act.activation(self.prob_of(u)[:, j // 2, j % 2, :], self.prob_of(u)[:, j // 2, j % 2, :], ACT.Exp, bias=self.top[:, u, j:j + 1],
                                     accum_out=self.top[:, u, 4 + j:5 + j])
            ins.then_inc(self.exped, 1)

        exp(0)
        if between is not None:
            between()
        def store(u):
            if self.units[u].last:
                act.wait_ge(self.pv_ps, u + 1)
                act.copy(self.units[u].out, ps[:, 6 + self.pair[u] % 2, 0:SEQ]).then_inc(self.pv_sb, 1)

        for u, unit in enumerate(self.units):
            if u + 1 < len(self.units):
                exp(u + 1)
            act.wait_ge(self.pt_ps, u + 1)
            if u >= 2:
                act.wait_ge(self.pv_ps, u - 1)
            if unit.keys == SEQ:
                act.copy(self.probT[:, u % 2, :], ps[:, 4:6, :].rearrange("p a n -> p (a n)")).then_inc(self.pt_sb, 1)
            else:
                act.copy(self.probT[0:unit.keys, u % 2, 0:512], ps[0:unit.keys, 4, :]).then_inc(self.pt_sb, 1)
            if u:
                store(u - 1)
        store(len(self.units) - 1)

    def vector(self, v):
        def peak(u):
            v.wait_ge(self.s_ps, u + 1)
            if u >= 3:
                v.wait_ge(self.pt_ps, u - 2)
            self.units[u].bias(v, self.prob_of(u), self.scores_of(u)).then_inc(self.biased, 1)
            v.wait_ge(self.biased, u + 1)
            v.tensor_reduce(self.top[:, u, 0:4].rearrange("p (h i) -> p h i", h=2), self.prob_of(u), AX, ALU.max).then_inc(self.peak, 1)
            v.wait_ge(self.peak, u + 1)
            v.tensor_scalar(self.top[:, u, 0:4], self.top[:, u, 0:4], -1.0, None, ALU.mult).then_inc(self.neg, 1)

        gated = 0
        peak(0)
        for u, unit in enumerate(self.units):
            if u + 1 < len(self.units):
                peak(u + 1)
            v.wait_ge(self.exped, u + 1)
            v.reciprocal(self.top[:, u, 4:8], self.top[:, u, 4:8]).then_inc(self.inv, 1)
            v.wait_ge(self.inv, u + 1)
            if unit.gate is not None:
                r = self.top[:, u, 4:8].rearrange("p (h i) -> p h i", h=2)
                v.tensor_tensor(r, r, unit.gate, ALU.mult).then_inc(self.gated, 1)
                gated += 1
                v.wait_ge(self.gated, gated)
            p = self.prob[:, u % 3, 0:4 * unit.keys].rearrange("p (j n) -> p j n", j=4)
            v.tensor_tensor(p, p, spread(self.top[:, u, 4:8], unit.keys), ALU.mult).then_inc(self.ready, 1)


def stage_even_attend(nc, m, t):
    s = Memory(nc)
    toe, cmp_w1, pos, w2k, w2v = m.toe, m.cmp_w1, m.pos, m.w2k, m.w2v
    blocks = s.sb("blocks", [P, 2, 16, 32])
    hidn = s.sb("hidn", [64, CMP_HID])
    hid = s.sb("hid", [P, 2, 64])
    kcmpT = s.sb("kcmpT", [P, 2 * NCMP])
    vcmp = s.sb("vcmp", [NCMP, 2, HD])
    gates = s.sb("gates_sb", [P, QT, 24])
    ps = m.ps
    small_in, toe_in, w1_in = m.small_in, m.toe_in, m.w1_in
    zeroed, blocks_ok, hid_ps, hid_ok, cmp_ps, cmp_sb, gz_ok, gz_valid = (
        m.sem(n) for n in ("blocks_zeroed", "blocks_ok", "hid_ps", "hid_ok", "cmp_ps", "cmp_sb", "gz_ok", "gz_valid"))

    def unit(q, k, values, keys, bias, gate, first, last, out):
        def scores(pe, S, hd, i):
            return pe.matmul(S, q[:, hd, i * P:(i + 1) * P], k, start=True, stop=True)

        def add_bias(v, prob, S):
            return v.tensor_tensor(prob, S, bias, ALU.add)
        return Unit(scores=scores, values=values, keys=keys, bias=add_bias, gate=gate, first=first, last=last, out=out)

    units = []
    for p in range(4):
        units.append(unit(m.mqT[:, p, :, :], m.mkT[:, p, :], lambda hd, k, p=p: m.mv[:, k, (2 * p + hd) * HD:(2 * p + hd + 1) * HD],
                          SEQ, toe[:, 2 * p:2 * p + 2, :, :], None, True, True, m.hT[:, p, :]))
    for p in range(4):
        g = p // 2
        gz = [gates[:, :, 6 * p + b:6 * p + b + 4:3].rearrange("p i h -> p h i") for b in range(3)]
        bias = toe[:, 8 + 2 * p:10 + 2 * p, :, :]
        units.append(unit(m.nqT[:, p, :, :], m.kslT[:], lambda hd, k, g=g: m.nv[:, k, g * HD:(g + 1) * HD],
                          SEQ, bias, gz[1], True, False, None))
        units.append(unit(m.nqT[:, p, :, :], m.kwnT[:], lambda hd, k, g=g: m.nv[:, k, 128 + g * HD:128 + (g + 1) * HD],
                          SEQ, bias, gz[2], False, False, None))
        units.append(unit(m.nqT[:, p, :, :], kcmpT[:, g * NCMP:(g + 1) * NCMP], lambda hd, k, g=g: vcmp[:, g, :],
                          NCMP, bias[:, :, :, CMP_BLOCK - 1:SEQ:CMP_STRIDE], gz[0], False, True, m.hT[:, 4 + p, :]))
    attn = Attention(m, s, "ev", units)

    with nc.Block() as block:

        @block.gpsimd
        def _(pool):
            m.clear_last(pool)
            pool.memset(blocks[:, :, :, 2 * NCMP:], 0.0).then_inc(zeroed, 1)

        @block.tensor
        def _(pe):
            def compress():
                pe.wait_ge(w1_in, 32)
                pe.wait_ge(blocks_ok, 2)
                pe.wait_ge(zeroed, 1)
                for k in range(16):
                    for j in range(2):
                        mm = pe.matmul(ps[32 * j:32 * (j + 1), 4, 0:CMP_HID], blocks[:, j, k, :], cmp_w1[:, j, k, :],
                                       start=(k == 0), stop=(k == 15))
                mm.then_inc(hid_ps, 1)
                pe.wait_ge(hid_ok, 1)
                for h in range(2):
                    mm = pe.transpose(ps[:, 5, h * 64:(h + 1) * 64], hidn[:, h * P:(h + 1) * P], cst(m, "ident", 64, 0, 64))
                mm.then_inc(hid_ps, 1)
                pe.wait_ge(hid_ok, 2)
                for h in range(2):
                    pe.matmul(ps[:, 6, 0:2 * NCMP], w2k[:, h, :], hid[:, h, 0:2 * NCMP], start=(h == 0), stop=(h == 1))
                for g in range(2):
                    for h in range(2):
                        mm = pe.matmul(ps[0:NCMP, 7, g * HD:(g + 1) * HD], hid[:, h, 32 + g * NCMP:32 + (g + 1) * NCMP], w2v[:, h, :],
                                       start=(h == 0), stop=(h == 1))
                mm.then_inc(cmp_ps, 1)
                pe.wait_ge(cmp_sb, 2)

            attn.tensor(pe, compress)

        @block.scalar
        def _(act):
            act.activation(gates[:], m.nv[:, :, 256:280], ACT.Sigmoid).then_inc(gz_ok, 1)
            def compress():
                act.wait_ge(hid_ps, 1)
                act.activation(hidn[:], ps[0:64, 4, 0:CMP_HID], ACT.Silu).then_inc(hid_ok, 1)
                act.wait_ge(hid_ps, 2)
                act.copy(hid[:].rearrange("p h n -> p (h n)"), ps[:, 5, 0:P]).then_inc(hid_ok, 1)
                act.wait_ge(cmp_ps, 1)
                act.copy(kcmpT[:], ps[:, 6, 0:2 * NCMP]).then_inc(cmp_sb, 1)
                act.copy(vcmp[:].rearrange("n g d -> n (g d)"), ps[0:NCMP, 7, 0:2 * HD]).then_inc(cmp_sb, 1)

            attn.scalar(act, compress)

        @block.vector
        def _(v):
            v.wait_ge(small_in, 80)
            for j, src in enumerate((m.kcT, m.vcT)):
                for g in range(2):
                    for half in range(2):
                        tok = src[:, g, 16 * half:16 * half + 240].rearrange("p (n k) -> p k n", k=16)[:, 0:16:2, :]
                        ins = v.tensor_tensor(blocks[:, j, 8 * half:8 * half + 8, g * NCMP:(g + 1) * NCMP], tok,
                                              spread(pos[:, j, 8 * half:8 * half + 8], NCMP), ALU.add)
                ins.then_inc(blocks_ok, 1)
            v.wait_ge(gz_ok, 1)
            for i in range(QT):
                g3 = gates[:, i, 0:24:3]
                ins = v.tensor_scalar(g3, g3, cst(m, "cmpvalid", P, i, 1), None, ALU.mult)
            ins.then_inc(gz_valid, 1)
            v.wait_ge(gz_valid, 1)
            v.wait_ge(toe_in, 32)
            attn.vector(v)
    s.stack.close()
    m.even.stack.close()


def stage_mlp(nc, m, t, layer, w_out_in, w_out_value):
    s = Memory(nc)
    name = f"p{layer}"
    norm = Norm(m, s, name, 1, ("mlp", 8 * layer))
    pos = s.sb(f"{name}_pos", [P, 2, 4, SEQ])
    sq = s.sb(f"{name}_sqr", [P, 2, 4, SEQ])
    GROUPS = DFF2 // 512
    ps = m.ps
    out_ps, added, x_ps, up_ps, down_ps, relu_ok, sq_ok, x_done = (
        m.sem(f"{name}_{n}") for n in ("out_ps", "added", "x_ps", "up_ps", "down_ps", "relu_ok", "sq_ok", "x_done"))
    final_ps = m.sem(f"{name}_final_ps")
    w1_in = [m.sem(f"{name}_w1_in{b}") for b in range(2)]
    w2_in = [m.sem(f"{name}_w2_in{b}") for b in range(2)]
    w1 = [m.ring[:, 8 * b:8 * b + 4, :].rearrange("p a n -> p (a n)").rearrange("p (c n) -> p c n", c=C) for b in range(2)]
    w2 = [m.ring[:, 8 * b + 4:8 * b + 8, :] for b in range(2)]
    W1, W2 = stack(t["mlp_w1_2"][layer]), t["mlp_w2_2"][layer].rearrange("(g c p) n -> g p c n", p=P, c=4)

    with nc.Block() as block:

        @block.gpsimd
        def _(pool):
            m.clear_last(pool)

        @block.sync
        def _(sp):
            for b in range(2):
                sp.dma_start(w1[b], W1[:, :, b * 512:(b + 1) * 512]).then_inc(w1_in[b], 16)
                sp.dma_start(w2[b], W2[b]).then_inc(w2_in[b], 16)
            with sp.Fori(1, GROUPS // 2) as i:
                for b in range(2):
                    sp.wait_ge(up_ps, i * 2 + (b - 1))
                    sp.dma_start(w1[b], W1[:, :, bass.ds(i * 1024 + b * 512, 512)]).then_inc(w1_in[b], 16)
                    sp.wait_ge(down_ps, i * 2 + (b - 1))
                    sp.dma_start(w2[b], W2[bass.ds(i * 2 + b, 1)].rearrange("g p c n -> p (g c) n")).then_inc(w2_in[b], 16)

        @block.tensor
        def _(pe):
            pe.wait_ge(w_out_in, w_out_value)
            for i in range(QT):
                for half in range(2):
                    for c in range(C):
                        mm = pe.matmul(ps[:, 4 + 2 * i + half, :], m.hT[:, c, i * P:(i + 1) * P], m.ring[:, 16 + c, half * 512:(half + 1) * 512],
                                       start=(c == 0), stop=(c == C - 1))
                mm.then_inc(out_ps, 1)
            norm.tensor_turn(pe)
            norm.wait_turned(pe)

            def up(b, g):
                pe.wait_ge(w1_in[b], g * 8 + (16 - 8 * b))
                for f in range(4):
                    for c in range(C):
                        mm = pe.matmul(ps[:, 4 + 2 * b + f // 2, (f % 2) * SEQ:(f % 2 + 1) * SEQ], w1[b][:, c, f * P:(f + 1) * P], m.hT[:, c, :],
                                       start=(c == 0), stop=(c == C - 1))
                mm.then_inc(up_ps, 1)

            def down(b, g, last=False):
                pe.wait_ge(w2_in[b], g * 8 + (16 - 8 * b))
                pe.wait_ge(sq_ok, g + 1)
                steps = [(f, i) for f in range(4) for i in range(QT)]
                if last:
                    steps = [(f, i) for i in range(QT) for f in range(4)]
                for f, i in steps:
                    for half in range(2):
                        mm = pe.matmul(ps[:, 2 * i + half, :], sq[:, b, f, i * P:(i + 1) * P], w2[b][:, f, half * 512:(half + 1) * 512],
                                       start=False, stop=last, skip_group_check=True)
                    if last and f == 3:
                        mm.then_inc(final_ps, 1)
                if not last:
                    mm.then_inc(down_ps, 1)

            up(0, 0)
            for i in range(QT):
                for half in range(2):
                    pe.matmul(ps[:, 2 * i + half, :], cst(m, "ident"), m.x[:, i, half * 512:(half + 1) * 512],
                              start=True, stop=False, skip_group_check=True)
            with pe.Fori(0, GROUPS // 2 - 1) as i:
                pe.wait_ge(relu_ok, i * 2 + 1)
                up(1, i * 2 + 1)
                down(0, i * 2)
                pe.wait_ge(relu_ok, i * 2 + 1)
                up(0, i * 2 + 2)
                down(1, i * 2 + 1)
            up(1, GROUPS - 1)
            down(0, GROUPS - 2)
            down(1, GROUPS - 1, last=True)

        @block.scalar
        def _(act):
            norm.scalar_stats(act, added)
            norm.scalar_weigh(act)

            def relu(b, g, wait_sq):
                act.wait_ge(up_ps, g + 1)
                if wait_sq is not None:
                    act.wait_ge(sq_ok, wait_sq)
                act.activation(pos[:, b, :, :].rearrange("p f n -> p (f n)"), ps[:, 4 + 2 * b:6 + 2 * b, :].rearrange("p a n -> p (a n)"),
                               ACT.Relu).then_inc(relu_ok, 1)

            relu(0, 0, None)
            relu(1, 1, None)
            with act.Fori(1, GROUPS // 2) as i:
                for b in range(2):
                    relu(b, i * 2 + b, i * 2 + b - 1)
            act.wait_ge(final_ps, 2)
            act.copy(m.x[:, 1, 512:D], ps[:, 3, :]).then_inc(x_done, 1)

        @block.vector
        def _(v):
            for i in range(QT):
                v.wait_ge(out_ps, i + 1)
                v.tensor_tensor(m.x[:, i, :], m.x[:, i, :], ps[:, 4 + 2 * i:6 + 2 * i, :].rearrange("p a n -> p (a n)"), ALU.add).then_inc(added, 1)
            v.wait_ge(added, 2)
            norm.vector_scale(v)
            norm.vector_weigh(v)

            def square(b, g, wait_down):
                v.wait_ge(relu_ok, g + 1)
                if wait_down is not None:
                    v.wait_ge(down_ps, wait_down)
                v.tensor_tensor(sq[:, b, :, :], pos[:, b, :, :], pos[:, b, :, :], ALU.mult).then_inc(sq_ok, 1)

            square(0, 0, None)
            square(1, 1, None)
            with v.Fori(1, GROUPS // 2) as i:
                for b in range(2):
                    square(b, i * 2 + b, i * 2 + b - 1)
            v.wait_ge(final_ps, 1)
            v.tensor_copy(m.x[:, 0, :], ps[:, 0:2, :].rearrange("p a n -> p (a n)")).then_inc(x_done, 1)
            v.wait_ge(final_ps, 2)
            v.tensor_copy(m.x[:, 1, 0:512], ps[:, 2, :]).then_inc(x_done, 1)
    s.stack.close()


def stage_mlp0(nc, m, t):
    stage_mlp(nc, m, t, 0, m.eout_in, 16)


def stage_odd_project(nc, m, t):
    s = m.odd = Memory(nc)
    m.fqT = s.sb("fqT", [P, 8, 2, SEQ])
    m.fkT = s.sb("fkT", [P, 8, SEQ])
    m.fv = s.sb("fv", [P, QT, D])
    m.cumq = s.sb("cumq", [P, QT, 16])
    m.ncumT = s.sb("ncumT", [P, SEQ])
    r = Memory(nc)
    wf = r.sb("wforget", [P, C, 16])
    bf = r.sb("bforget", [P, 16])
    z = r.sb("z", [P, QT, 16])
    e = r.sb("e", [P, QT, 16])
    lf = r.sb("lf", [P, QT, 16])
    norm = Norm(m, r, "n1", 1, ("mix", 8))
    W = m.ring[:].rearrange("p a n -> p (a n)").rearrange("p (c n) -> p c n", c=C)
    ps = m.ps
    w_in = [m.sem(f"odd_in{k}") for k in range(6)]
    f_in, proj_ps, proj_sb, fz_ps, chain, e_ok, cum_ps, cum_ok = (
        m.sem(n) for n in ("f_in", "odd_ps", "odd_sb", "fz_ps", "fz_chain", "e_ok", "cum_ps", "cum_ok"))
    zeroed = m.sem("odd_zeroed")
    tiles = [(P * j, m.fqT[:, j, :, :], HD ** -0.5) for j in range(8)] + [(D + P * j, m.fkT[:, j, :], 1.0) for j in range(8)]

    with nc.Block() as block:

        @block.gpsimd
        def _(pool):
            m.clear_last(pool)
            pool.memset(m.fqT[:], 0.0).then_inc(zeroed, 1)
            pool.memset(m.ncumT[:], 0.0).then_inc(zeroed, 1)

        @block.sync
        def _(sp):
            src = stack(t["odd_w_in_2"][0])
            for k in range(6):
                sp.dma_start(W[:, :, 512 * k:512 * (k + 1)], src[:, :, 512 * k:512 * (k + 1)]).then_inc(w_in[k], 16)
                if k == 0:
                    sp.dma_start(wf[:], src[:, :, 3 * D:]).then_inc(f_in, 16)
                    sp.dma_start(bf[:], bcast_row(t["odd_b_forget_2"], 16)).then_inc(f_in, 16)

        @block.tensor
        def _(pe):
            norm.tensor_turn(pe)
            norm.wait_turned(pe)
            pe.wait_ge(f_in, 32)
            for i in range(QT):
                for c in range(C):
                    mm = pe.matmul(ps[:, 7, i * 16:(i + 1) * 16], m.hT[:, c, i * P:(i + 1) * P], wf[:, c, :], start=(c == 0), stop=(c == C - 1))
            mm.then_inc(fz_ps, 1)
            for n, (at, _, _) in enumerate(tiles):
                if n % 4 == 0:
                    pe.wait_ge(w_in[n // 4], 16)
                if n >= 6:
                    pe.wait_ge(proj_sb, n - 5)
                for c in range(C):
                    mm = pe.matmul(ps[:, n % 6, 0:SEQ], W[:, c, at:at + P], m.hT[:, c, :], start=(c == 0), stop=(c == C - 1))
                mm.then_inc(proj_ps, 1)
                if n == 2:
                    pe.wait_ge(chain, 3)
                    for i in range(QT):
                        for j in range(QT):
                            pe.matmul(ps[:, 6, i * 16:(i + 1) * 16], cst(m, "tri", P, j * SEQ + i * P, P), lf[:, j, :],
                                      start=(j == 0), stop=(j == QT - 1))
                    for j in range(QT):
                        mm = pe.matmul(ps[0:16, 7, 0:SEQ], lf[:, j, :], cst(m, "tri", P, j * SEQ, SEQ),
                                       start=(j == 0), stop=(j == QT - 1))
                    mm.then_inc(cum_ps, 1)
            n = len(tiles)
            for half in range(2):
                pe.wait_ge(w_in[4 + half], 16)
                for i in range(QT):
                    pe.wait_ge(proj_sb, n - 5)
                    for c in range(C):
                        mm = pe.matmul(ps[:, n % 6, :], m.hT[:, c, i * P:(i + 1) * P], W[:, c, 2 * D + 512 * half:2 * D + 512 * (half + 1)],
                                       start=(c == 0), stop=(c == C - 1))
                    mm.then_inc(proj_ps, 1)
                    n += 1

        @block.scalar
        def _(act):
            norm.scalar_stats(act)
            norm.scalar_weigh(act)
            act.wait_ge(chain, 2)
            act.activation(e[:], e[:], ACT.Exp, scale=-1.0).then_inc(e_ok, 1)
            act.wait_ge(e_ok, 1)
            act.activation(e[:], e[:], ACT.Ln, bias=m.one[:, 0:1]).then_inc(e_ok, 1)
            for n, (_, dst, scale) in enumerate(tiles):
                act.wait_ge(proj_ps, n + 1)
                if n == 0:
                    act.wait_ge(zeroed, 1)
                if n < 8:
                    act.mul(dst[0:HD, 0, :], ps[0:HD, n % 6, 0:SEQ], scale)
                    act.mul(dst[HD:P, 1, :], ps[HD:P, n % 6, 0:SEQ], scale).then_inc(proj_sb, 1)
                else:
                    act.copy(dst, ps[:, n % 6, 0:SEQ]).then_inc(proj_sb, 1)
            n = len(tiles)
            for half in range(2):
                for i in range(QT):
                    act.wait_ge(proj_ps, n + 1)
                    act.copy(m.fv[:, i, 512 * half:512 * (half + 1)], ps[:, n % 6, :]).then_inc(proj_sb, 1)
                    n += 1

        @block.vector
        def _(v):
            norm.vector_scale(v)
            norm.vector_weigh(v)
            v.wait_ge(f_in, 32)
            v.wait_ge(fz_ps, 1)
            v.memset(m.one[:], 1.0)
            v.tensor_tensor(z[:], ps[:, 7, 0:32].rearrange("p (i h) -> p i h", i=QT),
                            bf[:].rearrange("p (a h) -> p a h", a=1).to_broadcast([P, QT, 16]), ALU.add).then_inc(chain, 1)
            v.wait_ge(chain, 1)
            v.scalar_tensor_tensor(e[:], z[:], -1.0, z[:], ALU.mult, ALU.max).then_inc(chain, 1)
            v.wait_ge(e_ok, 2)
            v.scalar_tensor_tensor(lf[:], z[:], 0.0, e[:], ALU.min, ALU.subtract).then_inc(chain, 1)
            v.wait_ge(cum_ps, 1)
            v.tensor_copy(m.cumq[:].rearrange("p i h -> p (i h)"), ps[:, 6, 0:32])
            v.wait_ge(zeroed, 2)
            v.tensor_scalar(m.ncumT[0:16, :], ps[0:16, 7, 0:SEQ], -1.0, None, ALU.mult).then_inc(cum_ok, 1)
    r.stack.close()


def stage_odd_attend(nc, m, t):
    s = Memory(nc)
    m.oout_in = m.lasting("oout_in")

    def unit(p):
        def scores(pe, S, hd, i):
            pe.matmul(S, m.fqT[:, p, hd, i * P:(i + 1) * P], m.fkT[:, p, :], start=True, stop=False)
            one = cst(m, "ident", P, 2 * p + hd, 1).to_broadcast([P, P])
            return pe.matmul(S, one, m.ncumT[:], start=False, stop=True)

        def bias(v, prob, S):
            for hd in range(2):
                for i in range(QT):
                    h = 2 * p + hd
                    ins = v.scalar_tensor_tensor(prob[:, hd, i, :], S[:, hd, i, :], m.cumq[:, i, h:h + 1],
                                                 cst(m, "causal", P, i * SEQ, SEQ), ALU.add, ALU.add)
            return ins
        return Unit(scores=scores, bias=bias, values=lambda hd, k: m.fv[:, k, (2 * p + hd) * HD:(2 * p + hd + 1) * HD],
                               keys=SEQ, gate=None, first=True, last=True, out=m.hT[:, p, :])

    attn = Attention(m, s, "od", [unit(p) for p in range(8)])

    with nc.Block() as block:

        @block.gpsimd
        def _(pool):
            m.clear_last(pool)

        @block.sync
        def _(sp):
            sp.dma_start(m.ring[:, 16:24, :], stack(t["odd_w_out_2"][0])).then_inc(m.oout_in, 16)

        @block.tensor
        def _(pe):
            attn.tensor(pe)

        @block.scalar
        def _(act):
            attn.scalar(act)

        @block.vector
        def _(v):
            attn.vector(v)
    s.stack.close()
    m.odd.stack.close()


def stage_mlp1(nc, m, t):
    stage_mlp(nc, m, t, 1, m.oout_in, 16)


def stage_final(nc, m, t):
    s = Memory(nc)
    row = s.sb("final_row", [P, D])
    y = s.sb("final_y", [P, QT, D])
    stats = s.sb("final_st", [P, 2 * QT])
    row_in, sq, std, inv, done, out_done = (m.sem(f"final_{n}") for n in ("row_in", "sq", "std", "inv", "done", "out_done"))

    with nc.Block() as block:

        @block.gpsimd
        def _(pool):
            m.clear_last(pool)

        @block.sync
        def _(sp):
            sp.dma_start(row[:], bcast_row(t["final_norm_2"], D)).then_inc(row_in, 16)
            out = stack(t["out"][0])
            for i in range(QT):
                sp.wait_ge(done, i + 1)
                sp.dma_start(out[:, i, :], y[:, i, :]).then_inc(out_done, 16)
            sp.wait_ge(out_done, 16 * QT)

        @block.scalar
        def _(act):
            for i in range(QT):
                act.activation(y[:, i, :], m.x[:, i, :], ACT.Square, accum_out=stats[:, i:i + 1]).then_inc(sq, 1)
            act.wait_ge(sq, QT)
            act.activation(stats[:, QT:2 * QT], stats[:, 0:QT], ACT.Sqrt, scale=1.0 / D, bias=m.eps[:, 1:2]).then_inc(std, 1)

        @block.vector
        def _(v):
            v.wait_ge(std, 1)
            v.reciprocal(stats[:, QT:2 * QT], stats[:, QT:2 * QT]).then_inc(inv, 1)
            v.wait_ge(inv, 1)
            v.wait_ge(row_in, 16)
            for i in range(QT):
                v.scalar_tensor_tensor(y[:, i, :], m.x[:, i, :], stats[:, QT + i:QT + i + 1], row[:], ALU.mult, ALU.mult).then_inc(done, 1)


STAGES = (stage_input, stage_latent, stage_residual, stage_route, stage_experts, stage_even_project, stage_even_attend,
          stage_mlp0, stage_odd_project, stage_odd_attend, stage_mlp1, stage_final)


def program(nc, t):
    m = Memory(nc)
    m.consts = m.sb("consts_sb", [P, NCONST])
    m.ring = m.sb("ring", [P, 24, D])
    m.x = m.sb("x_sb", [P, QT, D])
    m.hT = m.sb("hT", [P, C, SEQ])
    m.cols = m.sb("cols", [P, NROWS])
    m.eps = m.sb("eps", [P, 2])
    m.one = m.sb("one", [P, 1])
    m.ps = m.stack.enter_context(nc.psum_tensor("ps", [P, 8, 512], F32))
    m.init = m.lasting("init")
    m.silu = m.sb("silu", [P, C, 2])
    m.r_g2 = m.sb("r_g2", [P, D])
    m.mla = Memory(nc)
    m.wq = m.mla.sb("wq", [P, 3, HEADS * NOPE])
    m.wqr = m.mla.sb("wqr", [P, 3, HEADS * ROPE])
    m.wkv = m.mla.sb("wkv", [P, 2, HEADS * (NOPE + VDIM)])
    m.qlatT = m.mla.sb("qlatT", [P, 3, SEQ])
    m.kvlatT = m.mla.sb("kvlatT", [P, 2, 2 * SEQ])
    m.kropeT = m.mla.sb("kropeT", [P, 2 * SEQ])
    m.uT = m.mla.sb("uT", [P, 2, SEQ])
    for stage in STAGES:
        stage(nc, m, t)
        m.end_stage()


_INS = ["x", "c", "ctx", "c_ctx", "w_mod", "b_mod", "norm_attn_pre", "norm_attn_post", "norm_ffn_pre", "norm_ffn_post",
        "w_in", "norm_q_lat", "norm_kv_lat", "w_q_up", "w_kv_up", "w_fourier", "w_out", "w_router", "b_router",
        "w_gate", "b_gate", "w_up", "b_up", "w_down", "b_down", "rel_bias_2", "mix_norm_2", "mlp_norm_2", "even_w_in_2",
        "even_w_out_2", "cmp_pos_k_2", "cmp_pos_v_2", "cmp_k_w1_2", "cmp_k_w2_2", "cmp_v_w1_2", "cmp_v_w2_2",
        "odd_w_in_2", "odd_b_forget_2", "odd_w_out_2", "mlp_w1_2", "mlp_w2_2", "final_norm_2"]


def kernel(**inputs):
    import concourse.bacc as bacc
    from concourse.bass_utils import run_bass_kernel_spmd

    nc = bacc.Bacc("TRN2", target_bir_lowering=False, num_devices=1)
    arrays, t = {}, {}
    for name in _INS:
        a = np.ascontiguousarray(inputs[name])
        arrays[f"in_{name}"] = a
        t[name] = nc.dram_tensor(f"in_{name}", a.shape, mybir.dt.from_np(a.dtype), kind="ExternalInput").ap()
    arrays["in_consts"], arrays["in_buckets"] = shape_constants()
    t["buckets"] = nc.dram_tensor("in_buckets", (BUCKETS, 2, 512), F32, kind="ExternalInput").ap()
    t["consts"] = nc.dram_tensor("in_consts", (P, NCONST), F32, kind="ExternalInput").ap()
    t["toeplitz"] = nc.dram_tensor("toeplitz", (16, P * 512), F32, kind="Internal").ap()
    t["out"] = nc.dram_tensor("out", (1, SEQ, D), F32, kind="ExternalOutput").ap()
    program(nc, t)
    r = run_bass_kernel_spmd(nc, [arrays], core_ids=[0])
    return r.results[0]["out"]
```
